# Optimizing a Trainium2 kernel written in Bass

```python
import math
import jax, jax.numpy as jnp
from jax import lax
import numpy as np

D_MODEL = 1024
BATCH = 1
SEQ = 512
DEPTH = 1

H_A = 8
DQK_A = D_MODEL // 16
DV_A = D_MODEL // 8
QK_A = H_A * DQK_A
V_A = H_A * DV_A
CHUNK = 64
CONV_K = 4
H_B = 8
HD_B = D_MODEL // 8
W_B = H_B * HD_B
QBLK = 128
D_FF = 4 * D_MODEL
EPS = 1e-6
IN_SIZES = (QK_A, QK_A, V_A, V_A, H_A, H_A, W_B, W_B, W_B, D_MODEL, D_MODEL)
IN_COLS = sum(IN_SIZES)


def rms_norm(x, g):
    xf = x.astype(jnp.float32)
    y = xf * lax.rsqrt(jnp.mean(xf * xf, axis=-1, keepdims=True) + EPS)
    return (y * g.astype(jnp.float32)).astype(x.dtype)

def head_rms_norm(x, g):
    xf = x.astype(jnp.float32)
    y = xf * lax.rsqrt(jnp.mean(xf * xf, axis=-1, keepdims=True) + EPS)
    return y * g.astype(jnp.float32)

def causal_conv(x, w):
    S = x.shape[1]
    xp = jnp.pad(x, ((0, 0), (CONV_K - 1, 0), (0, 0)))
    y = xp[:, 0:S] * w[0]
    for j in range(1, CONV_K):
        y = y + xp[:, j:j + S] * w[j]
    return y

def mlstm_chunkwise(q, k, v, i_pre, f_pre):
    B, S, H, _ = q.shape
    NC = S // CHUNK
    to_chunks = lambda a: jnp.moveaxis(a.astype(jnp.float32).reshape(B, NC, CHUNK, H, -1), 3, 1)
    q = to_chunks(q)
    k = to_chunks(k) * (DQK_A ** -0.5)
    v = to_chunks(v)
    gate = lambda a: jnp.moveaxis(a.astype(jnp.float32).reshape(B, NC, CHUNK, H), 3, 1)
    logf = jax.nn.log_sigmoid(gate(f_pre))
    ig = gate(i_pre)
    b = jnp.cumsum(logf, axis=-1)
    b_last = b[..., -1]

    a = b_last[..., None] - b + ig
    m_loc = jnp.max(a, axis=-1)
    w = jnp.exp(a - m_loc[..., None])
    S_loc = jnp.einsum('bhcs,bhcsk,bhcsv->bhckv', w, k, v)
    n_loc = jnp.einsum('bhcs,bhcsk->bhck', w, k)

    def step(carry, inp):
        S_prev, n_prev, m_prev = carry
        S_l, n_l, m_l, bl = inp
        m_new = jnp.maximum(bl + m_prev, m_l)
        sp = jnp.exp(bl + m_prev - m_new)
        sl = jnp.exp(m_l - m_new)
        S_new = sp[..., None, None] * S_prev + sl[..., None, None] * S_l
        n_new = sp[..., None] * n_prev + sl[..., None] * n_l
        return (S_new, n_new, m_new), (S_prev, n_prev, m_prev)

    init = (jnp.zeros_like(S_loc[:, :, 0]), jnp.zeros_like(n_loc[:, :, 0]), jnp.zeros_like(m_loc[:, :, 0]))
    xs = (jnp.moveaxis(S_loc, 2, 0), jnp.moveaxis(n_loc, 2, 0), jnp.moveaxis(m_loc, 2, 0), jnp.moveaxis(b_last, 2, 0))
    _, (S0, n0, m0) = lax.scan(step, init, xs)
    S0 = jnp.moveaxis(S0, 0, 2)
    n0 = jnp.moveaxis(n0, 0, 2)
    m0 = jnp.moveaxis(m0, 0, 2)

    causal = jnp.tril(jnp.ones((CHUNK, CHUNK), dtype=bool))
    D = jnp.where(causal, b[..., :, None] - b[..., None, :] + ig[..., None, :], -jnp.inf)
    b_inter = b + m0[..., None]
    m_t = jnp.maximum(b_inter, jnp.max(D, axis=-1))
    P = jnp.exp(D - m_t[..., None]) * jnp.einsum('bhctk,bhcsk->bhcts', q, k)
    inter = jnp.exp(b_inter - m_t)
    num = jnp.einsum('bhcts,bhcsv->bhctv', P, v) + inter[..., None] * jnp.einsum('bhctk,bhckv->bhctv', q, S0)
    den = jnp.sum(P, axis=-1) + inter * jnp.einsum('bhctk,bhck->bhct', q, n0)
    h = num / jnp.maximum(jnp.abs(den), jnp.exp(-m_t))[..., None]
    return jnp.moveaxis(h, 1, 3).reshape(B, S, H, DV_A)

def stick_breaking(q, k, v):
    S = q.shape[1]
    scale = HD_B ** -0.5
    outs = []
    for blk in range(S // QBLK):
        t0, t1 = blk * QBLK, (blk + 1) * QBLK
        z = jnp.einsum('bqhd,bshd->bhqs', q[:, t0:t1], k[:, :t1]) * scale
        t_idx = t0 + jnp.arange(QBLK)
        s_idx = jnp.arange(t1)
        strict = s_idx[None, :] < t_idx[:, None]
        log_keep = jnp.where(strict, jax.nn.log_sigmoid(-z), 0.0)
        suffix = lax.cumsum(log_keep, axis=3, reverse=True) - log_keep
        A = jnp.where(strict, jnp.exp(jax.nn.log_sigmoid(z) + suffix), 0.0)
        outs.append(jnp.einsum('bhqs,bshd->bqhd', A, v[:, :t1]))
    return jnp.concatenate(outs, axis=1)

def first_inputs(seed: int = 0) -> dict:
    key = jax.random.key(seed)
    ks = jax.random.split(key, 15)
    n = jax.random.normal
    f32 = jnp.float32
    x = n(ks[0], (BATCH, SEQ, D_MODEL), f32)
    norm_mix_g = 1.0 + 0.1 * n(ks[1], (DEPTH, D_MODEL), f32)
    w_in = n(ks[2], (DEPTH, D_MODEL, IN_COLS), f32) * D_MODEL ** -0.5
    b_if = jnp.concatenate([0.5 * n(ks[3], (DEPTH, H_A), f32),
                            3.0 + 0.5 * n(ks[4], (DEPTH, H_A), f32)], axis=-1)
    b_gate = 0.02 * n(ks[5], (DEPTH, 2 * D_MODEL), f32)
    conv_w = n(ks[6], (DEPTH, CONV_K, 2 * QK_A), f32) * CONV_K ** -0.5
    mlstm_norm_g = 1.0 + 0.1 * n(ks[7], (DEPTH, V_A), f32)
    sb_q_norm_g = 1.0 + 0.1 * n(ks[8], (DEPTH, HD_B), f32)
    sb_k_norm_g = 1.0 + 0.1 * n(ks[9], (DEPTH, HD_B), f32)
    w_out = n(ks[10], (DEPTH, D_MODEL, D_MODEL), f32) * D_MODEL ** -0.5
    norm_mlp_g = 1.0 + 0.1 * n(ks[11], (DEPTH, D_MODEL), f32)
    w_up = n(ks[12], (DEPTH, D_MODEL, D_FF), f32) * D_MODEL ** -0.5
    w_down = n(ks[13], (DEPTH, D_FF, D_MODEL), f32) * D_FF ** -0.5
    return {"x": x, "norm_mix_g": norm_mix_g, "w_in": w_in, "b_if": b_if, "b_gate": b_gate,
            "conv_w": conv_w, "mlstm_norm_g": mlstm_norm_g, "sb_q_norm_g": sb_q_norm_g,
            "sb_k_norm_g": sb_k_norm_g, "w_out": w_out, "norm_mlp_g": norm_mlp_g,
            "w_up": w_up, "w_down": w_down}

def first_block(x, norm_mix_g, w_in, b_if, b_gate, conv_w, mlstm_norm_g, sb_q_norm_g, sb_k_norm_g,
              w_out, norm_mlp_g, w_up, w_down):
    B, S, _ = x.shape
    split_idx = np.cumsum(IN_SIZES)[:-1].tolist()
    for l in range(DEPTH):
        h = rms_norm(x, norm_mix_g[l])
        p = h @ w_in[l]
        q_a, k_a, v_a, o_a, i_a, f_a, q_b, k_b, v_b, g_a, g_b = jnp.split(p, split_idx, axis=-1)
        qk_a = jax.nn.silu(causal_conv(jnp.concatenate([q_a, k_a], axis=-1), conv_w[l]))
        q_a, k_a = qk_a[..., :QK_A], qk_a[..., QK_A:]
        i_pre = i_a.astype(jnp.float32) + b_if[l, :H_A].astype(jnp.float32)
        f_pre = f_a.astype(jnp.float32) + b_if[l, H_A:].astype(jnp.float32)
        h_a = mlstm_chunkwise(q_a.reshape(B, S, H_A, DQK_A), k_a.reshape(B, S, H_A, DQK_A),
                              v_a.reshape(B, S, H_A, DV_A), i_pre, f_pre)
        h_a = head_rms_norm(h_a, mlstm_norm_g[l].reshape(H_A, DV_A)).reshape(B, S, V_A)
        y_a = jax.nn.sigmoid(o_a.astype(jnp.float32)) * h_a
        qn = head_rms_norm(q_b.reshape(B, S, H_B, HD_B), sb_q_norm_g[l])
        kn = head_rms_norm(k_b.reshape(B, S, H_B, HD_B), sb_k_norm_g[l])
        y_b = stick_breaking(qn, kn, v_b.reshape(B, S, H_B, HD_B).astype(jnp.float32)).reshape(B, S, W_B)
        gates = jax.nn.sigmoid(jnp.concatenate([g_a, g_b], axis=-1).astype(jnp.float32)
                               + b_gate[l].astype(jnp.float32))
        y = gates[..., :D_MODEL] * y_a + gates[..., D_MODEL:] * y_b
        x = x + y.astype(x.dtype) @ w_out[l]
        h2 = rms_norm(x, norm_mlp_g[l])
        x = x + jnp.square(jax.nn.relu(h2 @ w_up[l])) @ w_down[l]
    return x


MLA_HEADS = 8
MLA_Q_RANK = 256
MLA_KV_RANK = 128
MLA_NOPE_DIM = 64
MLA_ROPE_DIM = 32
MLA_QK_DIM = MLA_NOPE_DIM + MLA_ROPE_DIM
MLA_V_DIM = 64
MLA_WIDTH = MLA_HEADS * MLA_V_DIM
DSA_HEADS = 8
DSA_KV_HEADS = 2
DSA_HEAD_DIM = 64
DSA_WIDTH = DSA_HEADS * DSA_HEAD_DIM
DSA_ROT_DIM = DSA_HEAD_DIM // 4
IDX_HEADS = 8
IDX_DIM = 32
IDX_ROT_DIM = IDX_DIM // 4
INDEX_TOPK_MAX = 256
ROPE_THETA = 500000.0
Q_BLOCK = 128
NORM_EPS = 1e-6

IN_SPLITS = (
    MLA_Q_RANK, MLA_KV_RANK, MLA_ROPE_DIM, MLA_WIDTH,
    DSA_HEADS * DSA_HEAD_DIM, DSA_KV_HEADS * DSA_HEAD_DIM,
    DSA_KV_HEADS * DSA_HEAD_DIM, DSA_WIDTH,
    IDX_HEADS * IDX_DIM, IDX_DIM, IDX_HEADS,
    D_MODEL, D_MODEL,
)
D_IN = sum(IN_SPLITS)


def rms_norm_2(x, gain):
    xf = x.astype(jnp.float32)
    y = xf * lax.rsqrt(jnp.mean(xf * xf, axis=-1, keepdims=True) + NORM_EPS)
    return (y * gain.astype(jnp.float32)).astype(x.dtype)

def rope_angles(positions, rot_dim):
    inv_freq = ROPE_THETA ** (-jnp.arange(0, rot_dim, 2, dtype=jnp.float32) / rot_dim)
    ang = positions.astype(jnp.float32)[..., None] * inv_freq
    return jnp.cos(ang), jnp.sin(ang)

def apply_rope(x, cos, sin):
    xf = x.astype(jnp.float32)
    half = xf.shape[-1] // 2
    x1, x2 = xf[..., :half], xf[..., half:]
    c, s = cos[:, :, None, :], sin[:, :, None, :]
    return jnp.concatenate([x1 * c - x2 * s, x2 * c + x1 * s], axis=-1).astype(x.dtype)

def partial_rope(x, cos, sin, rot_dim):
    return jnp.concatenate([apply_rope(x[..., :rot_dim], cos, sin), x[..., rot_dim:]], axis=-1)

def to_blocks(a):
    b, s = a.shape[0], a.shape[1]
    a = a.reshape((b, s // Q_BLOCK, Q_BLOCK) + a.shape[2:])
    return jnp.moveaxis(a, 1, 0)

def from_blocks(a):
    a = jnp.moveaxis(a, 0, 1)
    return a.reshape((a.shape[0], a.shape[1] * a.shape[2]) + a.shape[3:])

def mla_attention(q, k, v):
    s_len = q.shape[1]
    scale = MLA_QK_DIM ** -0.5
    key_pos = jnp.arange(s_len, dtype=jnp.int32)
    starts = jnp.arange(s_len // Q_BLOCK, dtype=jnp.int32) * Q_BLOCK

    def one_block(args):
        qb, start = args
        qpos = start + jnp.arange(Q_BLOCK, dtype=jnp.int32)
        sc = jnp.einsum('bqhd,bkhd->bhqk', qb, k).astype(jnp.float32) * scale
        causal = key_pos[None, :] <= qpos[:, None]
        sc = jnp.where(causal[None, None], sc, -jnp.inf)
        p = jax.nn.softmax(sc, axis=-1).astype(v.dtype)
        return jnp.einsum('bhqk,bkhd->bqhd', p, v)

    return from_blocks(lax.map(one_block, (to_blocks(q), starts)))

def dsa_attention(q, k, v, q_idx, k_idx, w_idx, k_top):
    bsz, s_len, n_heads, hd = q.shape
    n_kv = k.shape[2]
    grp = n_heads // n_kv
    scale = hd ** -0.5
    key_pos = jnp.arange(s_len, dtype=jnp.int32)
    starts = jnp.arange(s_len // Q_BLOCK, dtype=jnp.int32) * Q_BLOCK
    gather = jax.vmap(lambda kb, ib: kb[ib])

    def one_block(args):
        qb, qib, wb, start = args
        qpos = start + jnp.arange(Q_BLOCK, dtype=jnp.int32)
        rel = jax.nn.relu(jnp.einsum('bqhd,bsd->bqhs', qib, k_idx).astype(jnp.float32))
        score = jnp.einsum('bqhs,bqh->bqs', rel, wb.astype(jnp.float32))
        causal = key_pos[None, None, :] <= qpos[None, :, None]
        score = jnp.where(causal, score, -jnp.inf)
        _, sel = lax.top_k(score, k_top)
        valid = sel <= qpos[None, :, None]
        kg = gather(k, sel)
        vg = gather(v, sel)
        qg = qb.reshape(bsz, Q_BLOCK, n_kv, grp, hd)
        sc = jnp.einsum('bqkgd,bqjkd->bqkgj', qg, kg).astype(jnp.float32) * scale
        sc = jnp.where(valid[:, :, None, None, :], sc, -jnp.inf)
        p = jax.nn.softmax(sc, axis=-1).astype(v.dtype)
        o = jnp.einsum('bqkgj,bqjkd->bqkgd', p, vg)
        return o.reshape(bsz, Q_BLOCK, n_heads, hd)

    out = lax.map(one_block, (to_blocks(q), to_blocks(q_idx), to_blocks(w_idx), starts))
    return from_blocks(out)

def second_inputs(seed: int = 0) -> dict:
    key = jax.random.key(seed)
    ks = jax.random.split(key, 20)
    f32 = jnp.float32

    def w(k, shape, fan_in):
        return jax.random.normal(k, shape, f32) * fan_in ** -0.5

    def g(k, n):
        return 1.0 + 0.01 * jax.random.normal(k, (DEPTH, n), f32)

    x = jax.random.normal(ks[0], (BATCH, SEQ, D_MODEL), f32)
    positions = jnp.broadcast_to(jnp.arange(SEQ, dtype=jnp.int32)[None, :], (BATCH, SEQ))
    return {
        'x': x,
        'positions': positions,
        'norm_gain': g(ks[1], D_MODEL),
        'w_in': w(ks[2], (DEPTH, D_MODEL, D_IN), D_MODEL),
        'b_merge': 0.01 * jax.random.normal(ks[3], (DEPTH, 2, D_MODEL), f32),
        'mla_q_norm': g(ks[4], MLA_Q_RANK),
        'mla_w_uq': w(ks[5], (DEPTH, MLA_Q_RANK, MLA_HEADS * MLA_QK_DIM), MLA_Q_RANK),
        'mla_kv_norm': g(ks[6], MLA_KV_RANK),
        'mla_w_ukv': w(ks[7], (DEPTH, MLA_KV_RANK, MLA_HEADS * (MLA_NOPE_DIM + MLA_V_DIM)), MLA_KV_RANK),
        'mla_q_gain': g(ks[8], MLA_QK_DIM),
        'mla_k_gain': g(ks[9], MLA_QK_DIM),
        'dsa_q_gain': g(ks[10], DSA_HEAD_DIM),
        'dsa_k_gain': g(ks[11], DSA_HEAD_DIM),
        'w_branch_mla': w(ks[12], (DEPTH, MLA_WIDTH, D_MODEL), MLA_WIDTH),
        'w_branch_dsa': w(ks[13], (DEPTH, DSA_WIDTH, D_MODEL), DSA_WIDTH),
        'w_out': w(ks[14], (DEPTH, D_MODEL, D_MODEL), D_MODEL),
    }

def second_block(x, positions, norm_gain, w_in, b_merge, mla_q_norm, mla_w_uq, mla_kv_norm, mla_w_ukv,
              mla_q_gain, mla_k_gain, dsa_q_gain, dsa_k_gain, w_branch_mla, w_branch_dsa, w_out):
    bsz, s_len, _ = x.shape
    k_top = min(INDEX_TOPK_MAX, s_len // 4)
    offsets = [int(o) for o in np.cumsum(IN_SPLITS)[:-1]]
    cos_m, sin_m = rope_angles(positions, MLA_ROPE_DIM)
    cos_d, sin_d = rope_angles(positions, DSA_ROT_DIM)
    cos_i, sin_i = rope_angles(positions, IDX_ROT_DIM)

    for l in range(DEPTH):
        h = rms_norm_2(x, norm_gain[l])
        proj = h @ w_in[l]
        (c_q, c_kv, k_pe, gate_a, q_b, k_b, v_b, gate_b,
         q_i, k_i, w_i, m_a, m_b) = jnp.split(proj, offsets, axis=-1)

        q_a = (rms_norm_2(c_q, mla_q_norm[l]) @ mla_w_uq[l]).reshape(bsz, s_len, MLA_HEADS, MLA_QK_DIM)
        kv_a = (rms_norm_2(c_kv, mla_kv_norm[l]) @ mla_w_ukv[l]).reshape(
            bsz, s_len, MLA_HEADS, MLA_NOPE_DIM + MLA_V_DIM)
        k_nope, v_a = kv_a[..., :MLA_NOPE_DIM], kv_a[..., MLA_NOPE_DIM:]
        k_rope = jnp.broadcast_to(k_pe[:, :, None, :], (bsz, s_len, MLA_HEADS, MLA_ROPE_DIM))
        k_a = jnp.concatenate([k_nope, k_rope], axis=-1)
        q_a = rms_norm_2(q_a, mla_q_gain[l])
        k_a = rms_norm_2(k_a, mla_k_gain[l])
        q_a = jnp.concatenate([q_a[..., :MLA_NOPE_DIM], apply_rope(q_a[..., MLA_NOPE_DIM:], cos_m, sin_m)], axis=-1)
        k_a = jnp.concatenate([k_a[..., :MLA_NOPE_DIM], apply_rope(k_a[..., MLA_NOPE_DIM:], cos_m, sin_m)], axis=-1)
        o_a = mla_attention(q_a, k_a, v_a).reshape(bsz, s_len, MLA_WIDTH) * jax.nn.silu(gate_a)

        q_b = rms_norm_2(q_b.reshape(bsz, s_len, DSA_HEADS, DSA_HEAD_DIM), dsa_q_gain[l])
        k_b = rms_norm_2(k_b.reshape(bsz, s_len, DSA_KV_HEADS, DSA_HEAD_DIM), dsa_k_gain[l])
        v_b = v_b.reshape(bsz, s_len, DSA_KV_HEADS, DSA_HEAD_DIM)
        q_b = partial_rope(q_b, cos_d, sin_d, DSA_ROT_DIM)
        k_b = partial_rope(k_b, cos_d, sin_d, DSA_ROT_DIM)
        q_i = partial_rope(q_i.reshape(bsz, s_len, IDX_HEADS, IDX_DIM), cos_i, sin_i, IDX_ROT_DIM)
        k_i = partial_rope(k_i[:, :, None, :], cos_i, sin_i, IDX_ROT_DIM)[:, :, 0, :]
        w_i = w_i * (IDX_HEADS ** -0.5 * IDX_DIM ** -0.5)
        o_b = dsa_attention(q_b, k_b, v_b, q_i, k_i, w_i, k_top).reshape(bsz, s_len, DSA_WIDTH)
        o_b = o_b * jax.nn.silu(gate_b)

        merged = (jax.nn.sigmoid(m_a + b_merge[l, 0]) * (o_a @ w_branch_mla[l])
                  + jax.nn.sigmoid(m_b + b_merge[l, 1]) * (o_b @ w_branch_dsa[l]))
        x = x + merged @ w_out[l]
    return x


def setup_inputs(seed=0):
    out = dict(first_inputs(seed))
    for name, value in second_inputs(seed + 1).items():
        if name != "x":
            out[name + "_2"] = value
    return out


def reference(
    x, norm_mix_g, w_in, b_if, b_gate, conv_w, mlstm_norm_g, sb_q_norm_g, sb_k_norm_g, w_out,
    norm_mlp_g, w_up, w_down, positions_2, norm_gain_2, w_in_2, b_merge_2, mla_q_norm_2,
    mla_w_uq_2, mla_kv_norm_2, mla_w_ukv_2, mla_q_gain_2, mla_k_gain_2, dsa_q_gain_2,
    dsa_k_gain_2, w_branch_mla_2, w_branch_dsa_2, w_out_2,
):
    x = first_block(
        x, norm_mix_g, w_in, b_if, b_gate, conv_w, mlstm_norm_g, sb_q_norm_g, sb_k_norm_g,
        w_out, norm_mlp_g, w_up, w_down,
    )
    return second_block(
        x, positions_2, norm_gain_2, w_in_2, b_merge_2, mla_q_norm_2, mla_w_uq_2, mla_kv_norm_2,
        mla_w_ukv_2, mla_q_gain_2, mla_k_gain_2, dsa_q_gain_2, dsa_k_gain_2, w_branch_mla_2,
        w_branch_dsa_2, w_out_2,
    )


_drawn_inputs = setup_inputs


def setup_inputs(seed=0):
    import zlib

    import numpy as np

    out = dict(_drawn_inputs(seed))
    spreads = {}
    factors = {'b_gate': 8.0,
     'sb_q_norm_g': 3.314,
     'sb_k_norm_g': 3.095,
     'norm_gain_2': 8.0,
     'b_merge_2': 41.744,
     'mla_q_norm_2': 8.0,
     'mla_kv_norm_2': 8.0,
     'mla_q_gain_2': 8.0,
     'mla_k_gain_2': 8.0,
     'dsa_q_gain_2': 8.0,
     'dsa_k_gain_2': 8.0}
    for name, (base, spread) in spreads.items():
        noise = np.random.default_rng([zlib.crc32(name.encode()), seed]).standard_normal(out[name].shape)
        drawn = base * np.exp(spread * noise) if base else spread * noise
        out[name] = __import__('jax').numpy.asarray(drawn.astype(out[name].dtype))
    for name, factor in factors.items():
        out[name] = (out[name] * factor).astype(out[name].dtype)
    return out
```

```python
from contextlib import ExitStack

import numpy as np

import concourse.bass as bass
from concourse import mybir

F32 = mybir.dt.float32
F32R = mybir.dt.float32r
ALU = mybir.AluOpType
ACT = mybir.ActivationFunctionType
AX = mybir.AxisListType

P = 128
SEQ = 512
TB = SEQ // P
DM = 1024
KT = DM // P
HEADS = 8
FF = 4096
CHUNKS = FF // DM
EPS = 1e-6
DQK_A = 64
HD_B = 128
NEG = -1.0e30

G_GATES = 0
G_HEADS = 1
G_OUT = G_HEADS + 2 * HEADS
G_MLP = G_OUT + 2
G_END1 = G_MLP + 4 * CHUNKS
T_HEADS = 2
T_OUT = T_HEADS + 8 * HEADS
T_MLP = T_OUT + 8
T_END1 = T_MLP + 16 * CHUNKS

TRI = {0: 0, 1: 512, 3: 896, 2: 1024}
TRI_COLS = 1280

QK_M = 96
NOPE = 64
D_D = 64
KV_D = 2
IDX_D = 32
N_FREQ = 28
TAKEN = -3.0e38
PI = float(np.pi)
TWO_PI_HI = 6.28125
TWO_PI_LO = 2 * PI - TWO_PI_HI
ROUND = 1.5 * 2.0 ** 23
G_C = G_END1
G_U = G_C + 3
G_L = G_U + 1
G_BR = G_L + 8
G_FIN = G_BR + 2
N_GROUPS = G_FIN + 2
T_C = T_END1
T_Q = T_C + 4
T_K = T_Q + 4
T_U = T_K + 4
T_L = T_U + 16
T_BR = T_L + 24
T_FIN = T_BR + 16
T_END = T_FIN + 8
SIN_MAX = 3.1415925


def program(nc, x_in, wall, gains, head_par, sb_gains, b_if, *rest):
    *block2_in, out = rest
    with ExitStack() as ctx:
        def sb(name, shape, dt=F32):
            return ctx.enter_context(nc.sbuf_tensor(name, shape, dt))

        class Signals(dict):
            def __missing__(self, name):
                self[name] = ctx.enter_context(nc.semaphore(name))
                return self[name]

        S = Signals()

        w_raw = sb("w_raw", [P, 2, 4, 512])
        w_hi = sb("w_hi", [P, 2, KT, 512], F32R)
        w_lo = sb("w_lo", [P, 2, KT, 512], F32R)
        h_hi = sb("h_hi", [P, KT, SEQ], F32R)
        h_lo = sb("h_lo", [P, KT, SEQ], F32R)
        ident = sb("ident", [P, P])
        mean = sb("mean", [P, P])
        ones = sb("ones", [P, P])
        ones_r = sb("ones_r", [P, P], F32R)
        eps = sb("eps", [P, 1])
        gain = sb("gain", [P, 3 * KT])
        ss = sb("ss", [P, 3, TB])
        lnv = sb("lnv", [P, 3, TB])
        rstd = sb("rstd", [P, 3, TB])
        K = 1024
        base = (nc.sbuf_base + 31) // 32 * 32
        slab = sb("slab", [P, 90 * 256])

        def at(name, offset, shape, dt=F32):
            return nc.alloc_sbuf_tensor_at(name, shape, dt, offset=base + int(offset))

        y_hi = at("y_hi", 0, [P, KT, SEQ], F32R)
        y_lo = at("y_lo", 16 * K, [P, KT, SEQ], F32R)
        sp_hi = at("sp_hi", 32 * K, [P, TRI_COLS], F32R)
        sp_lo = at("sp_lo", 37 * K, [P, TRI_COLS], F32R)
        z = at("z", 42 * K, [P, TRI_COLS])
        sp = at("sp", 47 * K, [P, TRI_COLS])
        decay = at("decay", 52 * K, [P, TRI_COLS])
        bc = at("bc", 57 * K, [P, 2, SEQ])
        names = "q_b k_b sq_q sq_k conv silu k_a v_bT v_aT v_b v_a gate_a gate_b".split()
        (q_b, k_b, sq_q, sq_k, conv, silu, k_a, v_bT, v_aT, v_b, v_a, gate_a, gate_b) = [
            at(n, (61 + 2 * i) * K, [P, SEQ]) for i, n in enumerate(names)]
        gate_o = at("gate_o", 87 * K + 128, [P, SEQ])
        den, num2, scl = sq_q, sq_k, silu
        qk_pad = at("qk_pad", 47 * K, [P, 3 + SEQ])
        tri_r = sb("tri_r", [P, P], F32R)
        tri = at("tri", 89.25 * K, [P, P])
        par = sb("par", [P, 7])
        hp = sb("hp", [P, HEADS, 7])
        col = sb("col", [P, TB])
        a_col = sb("a_col", [P, TB, HEADS])
        sbg = sb("sbg", [P, 2])
        x_res = at("x_res", 61 * K, [P, TB, DM])
        xs = at("xs", 44 * K, [P, TB, DM])
        act_hi = at("act_hi", 0, [P, KT, SEQ], F32R)
        act_lo = at("act_lo", 16 * K, [P, KT, SEQ], F32R)
        relu = at("relu", 32 * K, [P, 2, SEQ])
        relu_sq = at("relu_sq", 36 * K, [P, 2, SEQ])
        (g_i, g_f, g_abs, g_ls, g_F, g_a, g_G, g_m, one_row) = [
            at(f"gate_row{i}", (16 + 2 * i) * K, [HEADS, SEQ]) for i in range(9)]
        g_out = at("g_out", 40 * K, [HEADS, 2, SEQ])
        bif = sb("bif", [HEADS, 2])

        (positions, inv_freq, wide_gains, c_gains, b_merge) = block2_in
        cosine = sb("cosine", [P, TB, N_FREQ])
        sine = sb("sine", [P, TB, N_FREQ])
        c_gain = sb("c_gain", [P, 3])
        merge_bias = sb("merge_bias", [P, 2 * KT])
        c_ss = sb("c_ss", [P, 6, TB * HEADS])
        c_rstd = c_ss
        w_idx = sb("w_idx", [P, TB, HEADS])
        top8 = sb("top8", [P, 3, 8])
        tick = sb("tick", [P, 33])
        mx = sb("mx", [P, 2, TB])
        row_sum = sb("row_sum", [P, 2, TB])
        (ang, turns, angles_c) = [at(f"angles{i}", (34 + i) * K, [P, TB, N_FREQ]) for i in range(3)]
        pos_i = at("pos_i", 43 * K, [P, TB], mybir.dt.int32)
        pos_f = at("pos_f", 43 * K + 32, [P, TB])
        freqs = at("freqs", 43 * K + 64, [P, N_FREQ])
        q_a2 = at("q_a2", 0, [P, TB, HEADS * QK_M])
        k_a2 = at("k_a2", 12 * K, [P, TB, HEADS * QK_M])
        v_a2 = at("v_a2", 24 * K, [P, TB, HEADS * D_D])
        q_b2 = at("q_b2", 32 * K, [P, TB, HEADS * D_D])
        k_b2 = at("k_b2", 40 * K, [P, TB, KV_D * D_D])
        v_b2 = at("v_b2", 42 * K, [P, TB, KV_D * D_D])
        idx = at("idx", 44 * K, [P, TRI_COLS])
        causal = at("causal", 49 * K, [P, SEQ])
        p_sb = [at(f"p_sb{u}", (51 + 16 * u) * K, [P, TRI_COLS]) for u in range(2)]
        q_st = [at(f"q_st{u}", (51 + 16 * u) * K, [P, TB, QK_M]) for u in range(2)]
        k_st = [at(f"k_st{u}", (52.5 + 16 * u) * K, [P, TB, QK_M]) for u in range(2)]
        pT = [at(f"pT{u}", (56 + 16 * u) * K, [P, TRI_COLS]) for u in range(2)]
        qT = [at(f"qT{u}", (61 + 16 * u) * K, [P, SEQ]) for u in range(2)]
        kT = [at(f"kT{u}", (63 + 16 * u) * K, [P, SEQ]) for u in range(2)]
        v_st = [at(f"v_st{u}", (65 + 16 * u) * K, [P, TB, P]) for u in range(2)]
        gate_st = at("gate_st", 83 * K, [P, 2, SEQ])
        o_st = at("o_st", 87 * K, [P, SEQ])
        t_c = at("t_c", 51 * K, [P, TB, 512])
        t_k = at("t_k", 59 * K, [P, TB, 512])
        squares = at("squares", 67 * K, [P, TB * HEADS * QK_M])
        ra, rb, rc, rd = [at(f"rope{i}", (67 + 2 * i) * K, [P, TB * HEADS * 16]) for i in range(4)]
        cq_hi = at("cq_hi", 79 * K, [P, 2, SEQ], F32R)
        cq_lo = at("cq_lo", 83 * K, [P, 2, SEQ], F32R)
        ckv_hi = at("ckv_hi", 44 * K, [P, 1, SEQ], F32R)
        ckv_lo = at("ckv_lo", 46 * K, [P, 1, SEQ], F32R)
        qiT = [at(f"qiT{u}", (79 + 2 * u) * K, [IDX_D, SEQ]) for u in range(2)]
        kiT = at("kiT", 83 * K, [IDX_D, SEQ])
        rel = [at(f"rel{u}", (67 + 5 * u) * K, [P, TRI_COLS]) for u in range(2)]
        gain_qa, gain_ka, gain_qb, gain_kb = [at(f"gain_w{i}", (88 * 1024 + 384 * i), [P, d])
                                              for i, d in enumerate((96, 96, 64, 64))]
        o_all = at("o_all", 0, [P, KT, SEQ])
        g_all = at("g_all", 16 * K, [P, KT, SEQ])
        m_all = at("m_all", 32 * K, [P, 2 * KT, SEQ])
        x_fin = at("x_fin", 74 * K, [P, TB, DM])
        mg_hi = at("mg_hi", 0, [P, KT, SEQ], F32R)
        mg_lo = at("mg_lo", 16 * K, [P, KT, SEQ], F32R)
        x2_d = nc.dram_tensor("x2", [SEQ, DM], F32, kind="Internal").ap()
        gates_d = nc.dram_tensor("gates", [3 * KT, P, SEQ], F32, kind="Internal").ap()
        o_d = nc.dram_tensor("heads_out", [KT, P, SEQ], F32, kind="Internal").ap()

        def bcast(ap, shape):
            return ap.broadcast_to(shape)

        q_a3, k_a3 = [b[:, :, :].rearrange("p t (h d) -> p t h d", h=HEADS) for b in (q_a2, k_a2)]
        q_b3 = q_b2[:, :, :].rearrange("p t (h d) -> p t h d", h=HEADS)
        k_b3 = k_b2[:, :, :].rearrange("p t (h d) -> p t h d", h=KV_D)
        NORMS = [(t_c[:, :, 0:256].rearrange("p t (h d) -> p t h d", h=1), 1, 256),
                 (t_c[:, :, 256:384].rearrange("p t (h d) -> p t h d", h=1), 1, 128),
                 (q_b3, HEADS, D_D), (k_b3, KV_D, D_D), (q_a3, HEADS, QK_M), (k_a3, HEADS, QK_M)]
        LOW = {3: 0, 2: 512, 0: 896, 1: 1024}
        TOPB = {1: 1024, 2: 512, 3: 0}

        proj = ctx.enter_context(nc.psum_tensor("proj", [P, 2, 512], F32))
        pa = ctx.enter_context(nc.psum_tensor("pa", [P, 3 * 512], F32))
        pm = ctx.enter_context(nc.psum_tensor("pm", [P, 3 * 512], F32))
        rows_d = nc.dram_tensor("gate_rows", [HEADS, 2, SEQ], F32, kind="Internal").ap()

        block = ctx.enter_context(nc.Block())

        def tiles_by(g):
            return 2 + 4 * g

        def load_half(g, half, first=False):
            if not first:
                nc.sync.wait_ge(S["w_lo_done"], 2 * g + half - 1)
            nc.sync.dma_start(w_raw[:, half], wall[bass.ds(g, 1), :, 4 * half:4 * half + 4, :]
                              .rearrange("a p k n -> p (a k) n")).then_inc(S[f"w_landed{half}"], 16)

        def split_hi(g, slot, half, first=False, used=None):
            nc.scalar.wait_ge(S[f"w_landed{half}"], 16 * g + 16)
            if not first:
                nc.scalar.wait_ge(S["tile_made"], tiles_by(g - 2) if used is None else used)
            nc.scalar.activation(w_hi[:, slot, 4 * half:4 * half + 4, :], w_raw[:, half], ACT.Copy)\
                .then_inc(S["w_hi_done"], 1)

        def split_lo(g, slot, half):
            nc.vector.wait_ge(S[f"w_landed{half}"], 16 * g + 16)
            nc.vector.wait_ge(S["w_hi_done"], 2 * g + half + 1)
            nc.vector.tensor_tensor(w_lo[:, slot, 4 * half:4 * half + 4, :], w_raw[:, half],
                                    w_hi[:, slot, 4 * half:4 * half + 4, :], ALU.subtract)\
                .then_inc(S["w_lo_done"], 1)

        def project(g, slot, n, bank, j, tokens=False, act=None, kts=KT, k0=0, first=False, norm=None,
                    last=None):
            a_hi, a_lo = act or (h_hi, h_lo)
            if not first:
                nc.tensor.wait_ge(S["tile_free"], n - 1)
            c = slice(j * P, (j + 1) * P)
            for k in range(kts):
                if k == 0:
                    nc.tensor.wait_ge(S["w_lo_done"], 2 * g + 1 + k0 // 4)
                elif k + k0 == 4:
                    nc.tensor.wait_ge(S["w_lo_done"], 2 * g + 2)
                if norm is not None:
                    nc.tensor.wait_ge(S["norm_lo"], KT * norm + k + 1)
                if last and k == kts - 1:
                    nc.tensor.wait_ge(S[last[0]], last[1])
                for q, (w, a) in enumerate(((w_hi, a_hi), (w_hi, a_lo), (w_lo, a_hi))):
                    if tokens:
                        lhsT, rhs = a[:, k, c], w[:, slot, k0 + k, :]
                    else:
                        lhsT, rhs = w[:, slot, k0 + k, c], a[:, k, :]
                    mm = nc.tensor.matmul(proj[:, bank, :], lhsT, rhs, start=(k == 0 and q == 0),
                                          stop=(k == kts - 1 and q == 2))
            return mm

        def made(mm):
            mm.then_inc(S["tile_made"], 1)

        def norm_bank(k):
            if k < 2:
                return proj[:, k]
            return (pa, pm)[(k - 2) // 3][:, 512 * ((k - 2) % 3):512 * ((k - 2) % 3 + 1)]

        def norm_rstd(r, t):
            nc.scalar.activation(xs[:, t], x_res[:, t], ACT.Square, accum_out=ss[:, r, t:t + 1])\
                .then_inc(S["norm_ss"], 1)
            nc.scalar.wait_ge(S["norm_ss"], TB * r + t + 1)
            nc.scalar.activation(lnv[:, r, t:t + 1], ss[:, r, t:t + 1], ACT.Ln, bias=eps[:, 0:1], scale=1.0 / DM)\
                .then_inc(S["norm_ln"], 1)
            nc.scalar.wait_ge(S["norm_ln"], TB * r + t + 1)
            nc.scalar.activation(rstd[:, r, t:t + 1], lnv[:, r, t:t + 1], ACT.Exp, scale=-0.5).then_inc(S["norm_rstd"], 1)

        def norm_hi(r, k):
            nc.scalar.wait_ge(S["norm_turned"], KT * r + k + 1)
            nc.scalar.activation(h_hi[:, k], norm_bank(k), ACT.Copy, scale=gain[:, KT * r + k:KT * r + k + 1])\
                .then_inc(S["norm_hi"], 1)

        def norm_scale(r, t):
            nc.vector.wait_ge(S["norm_rstd"], TB * r + t + 1)
            nc.vector.tensor_scalar(xs[:, t], x_res[:, t], rstd[:, r, t:t + 1], None, ALU.mult)\
                .then_inc(S["norm_scaled"], 1)

        def norm_lo(r, k):
            nc.vector.wait_ge(S["norm_hi"], KT * r + k + 1)
            nc.vector.scalar_tensor_tensor(h_lo[:, k], norm_bank(k), gain[:, KT * r + k:KT * r + k + 1],
                                           h_hi[:, k], ALU.mult, ALU.subtract).then_inc(S["norm_lo"], 1)

        def norm_pe(r, tiles_before):
            if tiles_before:
                nc.tensor.wait_ge(S["tile_free"], tiles_before)
            for t in range(TB):
                nc.tensor.wait_ge(S["norm_scaled"], TB * r + t + 1)
                for k in range(KT):
                    mm = nc.tensor.transpose(norm_bank(k)[:, t * P:(t + 1) * P], xs[:, t, k * P:(k + 1) * P], ident[:, :])
                    if t == TB - 1:
                        mm.then_inc(S["norm_turned"], 1)

        pos_b = pos_f[:, :, None].broadcast_to([P, TB, N_FREQ])
        freq_b = freqs[:, None, :].broadcast_to([P, TB, N_FREQ])
        A3, T3, C3 = ang[:, :, :], turns[:, :, :], angles_c[:, :, :]
        ANGLES = [
            (pos_f, lambda v: v.tensor_copy(pos_f[:, :], pos_i[:, :])),
            (ang, lambda v: v.tensor_tensor(A3, pos_b, freq_b, ALU.mult)),
            (turns, lambda v: v.tensor_scalar(T3, A3, 1 / (2 * PI), ROUND, ALU.mult, ALU.add)),
            (turns, lambda v: v.tensor_scalar(T3, T3, ROUND, None, ALU.subtract)),
            (ang, lambda v: v.scalar_tensor_tensor(A3, T3, -TWO_PI_HI, A3, ALU.mult, ALU.add)),
            (ang, lambda v: v.scalar_tensor_tensor(A3, T3, -TWO_PI_LO, A3, ALU.mult, ALU.add)),
            (angles_c, lambda v: v.tensor_scalar(C3, A3, PI / 2, None, ALU.add)),
            (turns, lambda v: v.tensor_scalar(T3, C3, PI, 2 * PI, ALU.is_gt, ALU.mult)),
            (angles_c, lambda v: v.tensor_tensor(C3, C3, T3, ALU.subtract)),
            (ang, lambda v: v.tensor_scalar(A3, A3, SIN_MAX, -SIN_MAX, ALU.min, ALU.max)),
            (angles_c, lambda v: v.tensor_scalar(C3, C3, SIN_MAX, -SIN_MAX, ALU.min, ALU.max)),
        ]

        @block.sync
        def _(sp_):
            load_half(0, 0, first=True)
            load_half(0, 1, first=True)
            with nc.sync.Fori(1, N_GROUPS) as g:
                for half in (0, 1):
                    load_half(g, half)
            o_v, x_v = out.rearrange("(t p) d -> p t d", p=P), x_fin[:, :, :]
            for half in range(2):
                nc.sync.wait_ge(S["tile_free"], T_FIN + 4 * (half + 1))
                nc.sync.dma_start(o_v[:, :, 512 * half:512 * (half + 1)], x_v[:, :, 512 * half:512 * (half + 1)])\
                    .then_inc(S["out_stored"], 16)
            nc.sync.wait_ge(S["out_stored"], 32)

        @block.gpsimd
        def _(pool):
            gp = nc.gpsimd
            for dst, src in ((gain, gains), (hp, head_par), (sbg, sb_gains), (bif, b_if), (c_gain, c_gains), (merge_bias, b_merge),
                             (pos_i, positions), (freqs, inv_freq.broadcast_to([P, N_FREQ]))):
                gp.dma_start(dst[:], src).then_inc(S["par_landed"], 16)
            gp.memset(ident[:, :], 0.0).then_inc(S["c0"], 1)
            gp.memset(ones[:, :], 1.0).then_inc(S["c0"], 1)
            gp.memset(mean[:, :], 1.0 / P).then_inc(S["consts"], 1)
            gp.memset(eps[:, :], EPS).then_inc(S["consts"], 1)
            gp.memset(one_row[:, :], 1.0).then_inc(S["consts"], 1)
            gp.wait_ge(S["c0"], 2)
            gp.affine_select(out=ident[:, :], in_=ident[:, :], compare_op=ALU.not_equal, fill=1.0, base=0,
                             pattern=[[-1, P]], channel_multiplier=1).then_inc(S["consts"], 1)
            gp.tensor_copy(ones_r[:, :], ones[:, :]).then_inc(S["consts"], 1)
            gp.affine_select(out=tri[:, :], in_=ones[:, :], compare_op=ALU.is_ge, fill=0.0, base=0,
                             pattern=[[-1, P]], channel_multiplier=1).then_inc(S["consts"], 1)
            gp.affine_select(out=tri_r[:, :], in_=ones[:, :], compare_op=ALU.is_ge, fill=0.0, base=0,
                             pattern=[[-1, P]], channel_multiplier=1).then_inc(S["consts"], 1)
            gp.wait_ge(S["rows_ready"], 1)
            gp.dma_start(rows_d, g_out[:, :, :]).then_inc(S["rows_stored"], 16)
            gp.wait_ge(S["rows_stored"], 16)
            for h in range(HEADS):
                if h:
                    gp.wait_ge(S["head_done"], h + 1)
                gp.dma_start(bc[:, :, :], rows_d[bass.ds(h, 1)].broadcast_to([P, 2, SEQ])).then_inc(S["bc_landed"], 16)
                gp.wait_ge(S["silu_done"], h + 1)
                gp.dma_start(k_a[0:DQK_A, :], silu[DQK_A:P, :]).then_inc(S["ka_landed"], 16)
                gp.wait_ge(S["sp_done"], h + 1)
                for i in range(TB):
                    d = sp[:, TRI[i]:TRI[i] + P]
                    gp.affine_select(out=d, in_=d, compare_op=ALU.is_gt, fill=0.0, base=0,
                                     pattern=[[1, P]], channel_multiplier=-1).then_inc(S["sp_masked"], 1)
                gp.wait_ge(S["p_done"], h + 1)
                for i in range(TB):
                    d = decay[:, TRI[i]:TRI[i] + P]
                    gp.affine_select(out=d, in_=d, compare_op=ALU.is_ge, fill=0.0, base=0,
                                     pattern=[[1, P]], channel_multiplier=-1).then_inc(S["p_masked"], 1)
                gp.wait_ge(S["arg_b_done"], h + 1)
                for i in range(TB):
                    d = z[:, TRI[i]:TRI[i] + P]
                    gp.affine_select(out=d, in_=d, compare_op=ALU.is_gt, fill=NEG, base=0,
                                     pattern=[[1, P]], channel_multiplier=-1).then_inc(S["arg_b_masked"], 1)
            gp.wait_ge(S["head_done"], HEADS + 1)
            gp.wait_ge(S["x_area_free"], 1)
            gp.dma_start(x_res[:, :, :], x_in.rearrange("(t p) d -> p t d", p=P)).then_inc(S["x_landed"], 16)

            gp.wait_ge(S["tile_free"], T_END1)
            gp.dma_start(x2_d.rearrange("(t p) d -> p t d", p=P), x_res[:, :, :]).then_inc(S["x2_stored"], 16)
            gp.wait_ge(S["norm_turned"], KT * 3)
            for i, dst in enumerate((gain_qa, gain_ka, gain_qb, gain_kb)):
                d = dst.shape[1]
                gp.dma_start(dst[:, :], wide_gains[i:i + 1, 0:d].broadcast_to([P, d])).then_inc(S["wide_landed"], 16)
            gp.memset(causal[:, :], 0.0).then_inc(S["causal0"], 1)
            gp.wait_ge(S["causal0"], 1)
            gp.affine_select(out=causal[:, 384:512], in_=causal[:, 384:512], compare_op=ALU.is_ge, fill=NEG, base=0,
                             pattern=[[-1, P]], channel_multiplier=1).then_inc(S["causal_made"], 1)
            gp.wait_ge(S["tile_free"], T_K + 4)
            gp.tensor_copy(k_b2[:, :, :], t_k[:, :, 0:128]).then_inc(S["kv_b"], 1)
            gp.tensor_copy(v_b2[:, :, :], t_k[:, :, 128:256]).then_inc(S["kv_b"], 1)
            gp.wait_ge(S["idx_done"], 1)
            for i in range(TB):
                d = idx[:, LOW[i] + P * i:LOW[i] + P * (i + 1)]
                gp.affine_select(out=d, in_=d, compare_op=ALU.is_ge, fill=NEG, base=0,
                                 pattern=[[-1, P]], channel_multiplier=1).then_inc(S["idx_causal"], 1)
            for kind, (q, k, v, d) in enumerate(((q_a2, k_a2, v_a2, QK_M), (q_b2, k_b2, v_b2, D_D))):
                for hd in range(HEADS):
                    u, B = hd % 2, 4 * kind + hd // 2
                    if hd == 0 and kind == 0:
                        gp.wait_ge(S["q_a_ready"], 1)
                        gp.wait_ge(S["k_a_ready"], 1)
                        gp.wait_ge(S["idx_sum"], 4 * HEADS)
                        gp.wait_ge(S["kv_b"], 2)
                    if B:
                        gp.wait_ge(S[f"p_turned{u}"], B)
                    kh = hd if kind == 0 else hd // (HEADS // KV_D)
                    gp.tensor_copy(q_st[u][:, :, 0:d], q[:, :, hd * d:(hd + 1) * d]).then_inc(S[f"staged{u}"], 1)
                    gp.tensor_copy(k_st[u][:, :, 0:d], k[:, :, kh * d:(kh + 1) * d]).then_inc(S[f"staged{u}"], 1)
                    if B:
                        gp.wait_ge(S[f"pv{u}"], B)
                    if kind == 0:
                        gp.tensor_copy(v_st[u][:, :, :], v[:, :, P * (hd // 2):P * (hd // 2 + 1)]).then_inc(S[f"v_staged{u}"], 2)
                    else:
                        for w in range(2):
                            gp.tensor_copy(v_st[u][:, :, D_D * w:D_D * (w + 1)], v[:, :, kh * D_D:(kh + 1) * D_D])\
                                .then_inc(S[f"v_staged{u}"], 1)
            gp.wait_ge(S["o_stored"], 16 * 9)
            gp.wait_ge(S["pT_sb0"], 8)
            gp.wait_ge(S["pT_sb1"], 8)
            gp.dma_start(o_all[:, :, :], o_d.rearrange("k p n -> p k n")).then_inc(S["o_landed"], 16)
            gp.wait_ge(S["gates_stored0"], 16 * 13)
            gp.wait_ge(S["gates_stored1"], 16 * 13)
            gp.dma_start(g_all[:, :, :], gates_d[0:KT].rearrange("k p n -> p k n")).then_inc(S["g_landed"], 16)
            gp.dma_start(m_all[:, :, :], gates_d[KT:3 * KT].rearrange("k p n -> p k n")).then_inc(S["m_landed"], 16)
            gp.dma_start(x_fin[:, :, :], x2_d.rearrange("(t p) d -> p t d", p=P)).then_inc(S["x2_landed"], 16)

        @block.scalar
        def _(act):
            a = nc.scalar
            x_tiles = x_in.rearrange("(t p) d -> p t d", p=P)
            for t in range(TB):
                a.dma_start(x_res[:, t], x_tiles[:, t]).then_inc(S[f"x_first{t}"], 16)
            for i, name in enumerate(("o_stored", "gates_stored0", "gates_stored1")):
                a.dma_start(tick[:, 24 + 3 * i:27 + 3 * i], c_gains).then_inc(S[name], 16)
            a.preload_act_table_set("natural_log_exp_and_others")
            a.wait_ge(S["consts"], 7)
            for t in range(TB):
                a.wait_ge(S[f"x_first{t}"], 16)
                norm_rstd(0, t)
            for hf in (0, 1):
                split_hi(0, 0, hf, first=True)
            for u in range(2):
                a.activation(mx[:, u, 0:1], eps[:, :], ACT.Copy).then_inc(S[f"o_sb{u}"], 1)
            a.wait_ge(S["par_landed"], 128)
            for k in range(KT):
                norm_hi(0, k)
            for hf in (0, 1):
                split_hi(1, 1, hf, first=True)
            a.wait_ge(S["tile_made"], 1)
            a.activation(g_i[:, :], proj[0:HEADS, 0], ACT.Identity, bias=bif[:, 0:1]).then_inc(S["tile_free"], 1)
            a.wait_ge(S["tile_made"], 2)
            a.activation(g_f[:, :], proj[0:HEADS, 1], ACT.Identity, bias=bif[:, 1:2]).then_inc(S["tile_free"], 1)
            a.wait_ge(S["tile_free"], 2)
            a.activation(g_abs[:, :], g_f[:, :], ACT.Abs).then_inc(S["rows_act"], 1)
            a.wait_ge(S["rows_act"], 1)
            a.activation(g_abs[:, :], g_abs[:, :], ACT.Exp, scale=-1.0).then_inc(S["rows_act"], 1)
            a.wait_ge(S["rows_act"], 2)
            a.activation(g_abs[:, :], g_abs[:, :], ACT.Ln, bias=1.0).then_inc(S["rows_act"], 1)
            a.wait_ge(S["angles"], len(ANGLES))
            a.activation(sine[:, :, :], A3, ACT.Sin).then_inc(S["rope_tables"], 1)
            a.activation(cosine[:, :, :], C3, ACT.Sin).then_inc(S["rope_tables"], 1)
            a.preload_act_table_set("natural_log_exp_and_others")
            a.wait_ge(S["rows_m"], 1)
            a.activation(g_out[:, 1, :], g_m[:, :], ACT.Exp, scale=-1.0).then_inc(S["rows_act"], 1)
            a.wait_ge(S["rows_stored"], 16)
            with a.Fori(0, HEADS) as h:
                n = T_HEADS + 8 * h
                ga = G_HEADS + 2 * h
                a.preload_act_table_set("natural_log_exp_and_others")
                split_hi(ga + 1, 0, 0)
                for j, (raw, sq) in enumerate(((q_b, sq_q), (k_b, sq_k))):
                    a.wait_ge(S["tile_made"], n + j + 1)
                    a.wait_ge(S["head_done"], h + 1)
                    a.activation(raw[:, :], proj[:, j], ACT.Copy).then_inc(S["qk_raw"], 1)
                    a.activation(sq[:, :], proj[:, j], ACT.Square).then_inc(S["tile_free"], 1)
                split_hi(ga + 1, 0, 1)
                a.wait_ge(S["tile_made"], n + 3)
                a.wait_ge(S["head_done"], h + 1)
                a.activation(qk_pad[:, 3:3 + SEQ], proj[:, 0], ACT.Copy).then_inc(S["tile_free"], 1)
                for j, sq in enumerate((sq_q, sq_k)):
                    a.wait_ge(S["ssq_made"], 2 * h + j + 1)
                    a.activation(sq[:, :], pa[:, 512 * j:512 * (j + 1)], ACT.Ln, bias=eps[:, 0:1]).then_inc(S["rms_ln"], 1)
                    a.wait_ge(S["rms_ln"], 2 * h + j + 1)
                    a.activation(sq[:, :], sq[:, :], ACT.Exp, scale=-0.5).then_inc(S["rms_b"], 1)
                a.wait_ge(S["tile_made"], n + 4)
                a.activation(v_bT[:, :], proj[:, 1], ACT.Copy).then_inc(S["tile_free"], 1)
                split_hi(ga + 2, 1, 0)
                a.wait_ge(S["z_made"], h + 1)
                a.activation(z[:, :], pa[:, 0:TRI_COLS], ACT.Copy, scale=HD_B ** -0.5).then_inc(S["z_sb"], 1)
                a.wait_ge(S["z_sb"], h + 1)
                a.wait_ge(S["conv"], 4 * h + 4)
                a.activation(sp[:, :], z[:, :], ACT.Abs).then_inc(S["sp_abs"], 1)
                a.wait_ge(S["sp_abs"], h + 1)
                a.activation(sp[:, :], sp[:, :], ACT.Exp, scale=-1.0).then_inc(S["sp_exp"], 1)
                a.wait_ge(S["sp_exp"], h + 1)
                a.activation(sp[:, :], sp[:, :], ACT.Ln, bias=1.0).then_inc(S["sp_ln"], 1)
                a.wait_ge(S["tile_made"], n + 5)
                a.activation(v_aT[:, :], proj[:, 0], ACT.Copy).then_inc(S["tile_free"], 1)
                a.activation(silu[:, :], conv[:, :], ACT.Sigmoid).then_inc(S["silu_sig"], 1)
                a.preload_act_table_set("natural_log_exp_and_others")
                a.wait_ge(S["v_turned"], h + 1)
                a.activation(v_b[:, :], pm[:, 0:512], ACT.Copy).then_inc(S["v_sb"], 1)
                a.activation(v_a[:, :], pm[:, 512:1024], ACT.Copy).then_inc(S["v_sb"], 1)
                split_hi(ga + 2, 1, 1)
                a.wait_ge(S["tile_made"], n + 6)
                a.activation(gate_o[:, :], proj[:, 1], ACT.Copy).then_inc(S["tile_free"], 1)
                a.wait_ge(S["arg_a"], 4 * h + 4)
                a.activation(decay[:, :], decay[:, :], ACT.Exp).then_inc(S["decay_exp"], 1)
                a.wait_ge(S["tile_made"], n + 7)
                a.activation(gate_a[:, :], proj[:, 0], ACT.Copy).then_inc(S["tile_free"], 1)
                a.wait_ge(S["arg_b_masked"], 4 * h + 4)
                a.activation(z[:, :], z[:, :], ACT.Exp).then_inc(S["a_b"], 1)
                a.wait_ge(S["num_made"], h + 1)
                a.activation(num2[:, :], pm[:, 0:512], ACT.Square).then_inc(S["num_sq"], 1)
                a.activation(den[:, :], pm[:, 512:1024], ACT.Abs).then_inc(S["den_abs"], 1)
                a.wait_ge(S["var_a"], h + 1)
                a.activation(scl[:, :], scl[:, :], ACT.Ln).then_inc(S["var_ln"], 1)
                a.wait_ge(S["var_ln"], h + 1)
                a.activation(scl[:, :], scl[:, :], ACT.Exp, scale=-0.5).then_inc(S["rms_a"], 1)
                a.wait_ge(S["tile_free"], n + 7)
                a.activation(gate_o[:, :], gate_o[:, :], ACT.Sigmoid).then_inc(S["gate_sig"], 1)
                a.activation(gate_a[:, :], gate_a[:, :], ACT.Sigmoid, bias=par[:, 5:6]).then_inc(S["gate_sig"], 1)
                a.wait_ge(S["tile_made"], n + 8)
                a.activation(gate_b[:, :], proj[:, 1], ACT.Sigmoid, bias=par[:, 6:7]).then_inc(S["tile_free"], 1)
            a.preload_act_table_set("natural_log_exp_and_others")
            for g in range(G_OUT, G_MLP):
                for hf in (0, 1):
                    split_hi(g + 1, (g + 1) % 2, hf)
            for t in range(TB):
                a.wait_ge(S["tile_free"], T_MLP - TB + t + 1)
                norm_rstd(1, t)
            for k in range(KT):
                norm_hi(1, k)
            with a.Fori(0, CHUNKS) as c:
                g = G_MLP + 4 * c
                n = T_MLP + 16 * c
                for gg in range(2):
                    split_hi(g + gg + 1, gg % 2, 0)
                    for j in range(4):
                        i = 4 * gg + j
                        a.wait_ge(S["tile_made"], n + i + 1)
                        if i == 0:
                            a.wait_ge(S["tile_free"], n)
                        if i >= 2:
                            a.wait_ge(S["a_lo_done"], 8 * c + i - 1)
                        a.activation(relu[:, i % 2], proj[:, i % 2], ACT.Relu).then_inc(S["tile_free"], 1)
                        a.wait_ge(S["tile_free"], n + i + 1)
                        a.activation(act_hi[:, i], relu[:, i % 2], ACT.Square).then_inc(S["a_hi_done"], 1)
                        if j == 1:
                            split_hi(g + gg + 1, gg % 2, 1)
                for gg in range(2, 4):
                    for hf in (0, 1):
                        split_hi(g + gg + 1, gg % 2, hf)
            a.preload_act_table_set("natural_log_exp_and_others")
            for t in range(TB):
                a.wait_ge(S["tile_free"], T_END1 - TB + t + 1)
                norm_rstd(2, t)
            for k in range(KT):
                norm_hi(2, k)
            a.wait_ge(S["x2_stored"], 16)

            def evac(n, dst, src=None, wait=None):
                a.wait_ge(S["tile_made"], n + 1)
                a.activation(dst, proj[:, n % 2, 0:512] if src is None else src, ACT.Copy).then_inc(S["tile_free"], 1)

            def split(g):
                for hf in (0, 1):
                    split_hi(g, g % 2, hf)

            def norm_squares(m):
                x, h, d = NORMS[m]
                if m:
                    a.wait_ge(S["c_summed"], m)
                o = squares[:, 0:TB * h * d]
                a.activation(o.rearrange("p (t h d) -> p t h d", t=TB, h=h), x, ACT.Square).then_inc(S["c_squared"], 1)

            def norm_root(m):
                x, h, d = NORMS[m]
                r = c_ss[:, m, 0:TB * h]
                a.wait_ge(S["c_summed"], m + 1)
                a.activation(c_rstd[:, m, 0:TB * h], r, ACT.Ln, bias=eps[:, 0:1], scale=1.0 / d).then_inc(S["c_ln"], 1)
                a.wait_ge(S["c_ln"], m + 1)
                a.activation(c_rstd[:, m, 0:TB * h], c_rstd[:, m, 0:TB * h], ACT.Exp, scale=-0.5).then_inc(S["c_root"], 1)

            split(G_C + 1)
            for t in range(TB):
                evac(T_C + t, t_c[:, t])
            a.wait_ge(S["tile_free"], T_C + 4)
            norm_squares(0)
            norm_squares(1)
            split(G_C + 2)
            norm_root(0)
            norm_root(1)
            for t in range(TB):
                evac(T_Q + t, q_b2[:, t])
            for m in range(3):
                a.wait_ge(S["c_turned"], m + 1)
                dst = cq_hi[:, m] if m < 2 else ckv_hi[:, 0]
                a.activation(dst, pa[:, 512 * m:512 * (m + 1)], ACT.Copy, scale=c_gain[:, m:m + 1]).then_inc(S["c_hi"], 1)
            a.wait_ge(S["tile_free"], T_Q + 4)
            norm_squares(2)
            split(G_U)
            norm_root(2)
            for t in range(TB):
                evac(T_K + t, t_k[:, t])
            a.wait_ge(S["kv_b"], 1)
            norm_squares(3)
            split(G_L)
            norm_root(3)
            for t in range(TB):
                n = T_U + 4 * t
                evac(n, q_a2[:, t, 0:512])
                a.wait_ge(S["tile_made"], n + 2)
                a.activation(q_a2[:, t, 512:768], proj[:, 1, 0:256], ACT.Copy).then_inc(S["tile_free"], 1)
                a.wait_ge(S["tile_made"], n + 3)
                a.activation(k_a3[:, t, :, 0:NOPE], proj[:, 0].rearrange("p (h d) -> p h d", h=HEADS), ACT.Copy)\
                    .then_inc(S["tile_free"], 1)
                evac(n + 3, v_a2[:, t])
            a.wait_ge(S["tile_free"], T_U + 16)
            a.wait_ge(S["rope"], 24)
            norm_squares(4)
            norm_root(4)
            a.wait_ge(S["k_pe_spread"], 1)
            norm_squares(5)
            norm_root(5)
            a.wait_ge(S["ki_turned"], 1)
            a.activation(kiT[:, :], pa[0:IDX_D, 0:512], ACT.Copy).then_inc(S["ki_sb"], 1)
            a.wait_ge(S["rope"], 36)
            for h in range(HEADS):
                a.wait_ge(S["qi_turned"], h + 1)
                a.activation(qiT[h % 2][:, :], (pm if h % 2 else pa)[0:IDX_D, 0:512], ACT.Copy).then_inc(S["qi_sb"], 1)
                a.wait_ge(S["idx_made"], h + 1)
                if h >= 2:
                    a.wait_ge(S["idx_sum"], 4 * (h - 1))
                a.activation(rel[h % 2][:, :], (pm if h % 2 else pa)[:, 0:TRI_COLS], ACT.Relu).then_inc(S["idx_relu"], 1)

            a.wait_ge(S["idx_done"], 1)
            a.wait_ge(S["idx_causal"], 4)

            def head_turns(u, B, d):
                X = (pa, pm)[u]
                a.wait_ge(S[f"qk_turned{u}"], B + 1)
                a.activation(qT[u][0:d, :], X[0:d, 0:512], ACT.Copy).then_inc(S[f"qk_sb{u}"], 1)
                a.activation(kT[u][0:d, :], X[0:d, 512:1024], ACT.Copy).then_inc(S[f"qk_sb{u}"], 1)

            def head_exp(u, B):
                a.wait_ge(S[f"nmax{u}"], B + 1)
                for i in range(TB):
                    x = p_sb[u][:, LOW[i]:LOW[i] + P * (i + 1)]
                    a.activation(x, x, ACT.Exp, bias=mx[:, u, i:i + 1], accum_out=row_sum[:, u, i:i + 1])\
                        .then_inc(S[f"p_exp{u}"], 1)

            def head_pT(u, B):
                X = (pa, pm)[u]
                a.wait_ge(S[f"p_turned{u}"], B + 1)
                a.activation(pT[u][:, :], X[:, 0:TRI_COLS], ACT.Copy).then_inc(S[f"pT_sb{u}"], 1)

            def head_out(u, B):
                X = (pa, pm)[u]
                a.wait_ge(S[f"pv{u}"], B + 1)
                if u == 0:
                    a.wait_ge(S["o_stored"], 16 * B + 16)
                a.activation(o_st[D_D * u:D_D * (u + 1), :], X[D_D * u:D_D * (u + 1), 0:512], ACT.Copy).then_inc(S[f"o_sb{u}"], 1)

            def gate(c, s, i):
                n = T_L + 6 * c + 3 * s + i
                q = (s + i) % 2
                a.wait_ge(S["tile_made"], n + 1)
                a.wait_ge(S[f"gates_stored{q}"], 16 * (3 * c + (3 * s + i) // 2) + 16)
                a.activation(gate_st[:, q], proj[:, q], ACT.Copy).then_inc(S["tile_free"], 1)
                a.wait_ge(S["tile_free"], n + 1)
                a.dma_start(gates_d[bass.ds(n - T_L, 1)].rearrange("a p n -> p (a n)"), gate_st[:, q])\
                    .then_inc(S[f"gates_stored{q}"], 16)

            for kind, d in enumerate((QK_M, D_D)):
                with a.Fori(0, 2) as b:
                    for s in range(2):
                        c = 2 * kind + b
                        B = 2 * c + s
                        split_hi(G_L + B + 1, s, 0, used=T_L + 3 * B)
                        head_turns(0, B, d)
                        head_turns(1, B, d)
                        gate(c, s, 0)
                        head_exp(0, B)
                        split_hi(G_L + B + 1, s, 1, used=T_L + 3 * B)
                        head_exp(1, B)
                        gate(c, s, 1)
                        head_pT(0, B)
                        head_pT(1, B)
                        gate(c, s, 2)
                        head_out(0, B)
                        head_out(1, B)
                        a.wait_ge(S["o_sb0"], B + 2)
                        a.wait_ge(S["o_sb1"], B + 2)
                        a.dma_start(o_d[bass.ds(B, 1)].rearrange("a p n -> p (a n)"), o_st[:, :]).then_inc(S["o_stored"], 16)
            for hf in (0, 1):
                split_hi(G_BR + 1, 0, hf, used=T_BR)
            for kind in range(2):
                ks = slice(4 * kind, 4 * kind + 4)
                a.wait_ge(S["o_times_g"], kind + 1)
                a.wait_ge(S["tile_free"], T_BR)
                a.activation(g_all[:, ks], g_all[:, ks], ACT.Sigmoid).then_inc(S["g_sig"], 1)
            for kind in range(2):
                ks = slice(4 * kind, 4 * kind + 4)
                a.wait_ge(S["o_gated"], kind + 1)
                a.activation(h_hi[:, ks], o_all[:, ks], ACT.Copy).then_inc(S["oh_hi"], 1)
            a.wait_ge(S["m_landed"], 16)
            for j in range(2 * KT):
                a.activation(m_all[:, j], m_all[:, j], ACT.Sigmoid, bias=merge_bias[:, j:j + 1]).then_inc(S["m_sig"], 1)
            for hf in (0, 1):
                split_hi(G_FIN, 1, hf, used=T_BR + 8)
            for j in range(KT):
                a.wait_ge(S["merged"], j + 1)
                a.activation(mg_hi[:, j], m_all[:, KT + j], ACT.Copy).then_inc(S["mg_hi"], 1)
            for hf in (0, 1):
                split_hi(G_FIN + 1, 0, hf, used=T_BR + 16)

        @block.vector
        def _(dve):
            v = nc.vector
            v.memset(tick[:, 0:1], 0.0).then_inc(S["head_done"], 1)
            v.memset(tick[:, 1:2], 0.0).then_inc(S["top_out"], 1)
            v.memset(tick[:, 2:3], 0.0).then_inc(S["pad_zero"], 1)
            for t in range(TB):
                v.wait_ge(S[f"x_first{t}"], 16)
                norm_scale(0, t)
            split_lo(0, 0, 0)
            split_lo(0, 0, 1)
            v.wait_ge(S["par_landed"], 128)
            for k in range(KT):
                norm_lo(0, k)
            for hf in (0, 1):
                split_lo(1, 1, hf)
            for i, (dst, op) in enumerate(ANGLES):
                if i:
                    v.wait_ge(S["angles"], i)
                op(v).then_inc(S["angles"], 1)
            v.wait_ge(S["rows_act"], 3)
            v.scalar_tensor_tensor(g_ls[:, :], g_f[:, :], 0.0, g_abs[:, :], ALU.min, ALU.subtract).then_inc(S["rows_dve"], 1)
            v.wait_ge(S["rows_dve"], 1)
            v.tensor_tensor_scan(g_F[:, :], one_row[:, :], g_ls[:, :], 0.0, ALU.mult, ALU.add).then_inc(S["rows_dve"], 1)
            v.wait_ge(S["rows_dve"], 2)
            v.tensor_tensor(g_a[:, :], g_i[:, :], g_F[:, :], ALU.subtract).then_inc(S["rows_a"], 1)
            v.wait_ge(S["rows_a"], 1)
            v.tensor_tensor_scan(g_G[:, :], g_a[:, :], g_a[:, :], 0.0, ALU.max, ALU.max).then_inc(S["rows_dve"], 1)
            v.wait_ge(S["rows_dve"], 3)
            v.tensor_tensor(g_m[:, :], g_F[:, :], g_G[:, :], ALU.add).then_inc(S["rows_m"], 1)
            v.wait_ge(S["rows_act"], 4)
            v.tensor_scalar(g_out[:, 0, :], g_G[:, :], -1.0, None, ALU.mult).then_inc(S["rows_ready"], 1)
            v.wait_ge(S["a_turned"], 1)
            v.tensor_copy(a_col[:, :, :], pm[:, 0:TB * HEADS].rearrange("p (t h) -> p t h", h=HEADS)).then_inc(S["a_col"], 1)
            v.wait_ge(S["a_col"], 1)
            with v.Fori(0, HEADS) as h:
                ga = G_HEADS + 2 * h
                v.wait_ge(S["head_done"], h + 1)
                v.tensor_copy(par[:, :], hp[:, bass.ds(h, 1), :].rearrange("p a n -> p (a n)")).then_inc(S["par_head"], 1)
                v.tensor_copy(col[:, :], a_col[:, :, bass.ds(h, 1)].rearrange("p t a -> p (t a)")).then_inc(S["par_head"], 1)
                v.memset(qk_pad[:, 0:3], 0.0).then_inc(S["pad_zero"], 1)
                split_lo(ga + 1, 0, 0)
                split_lo(ga + 1, 0, 1)
                for j, (raw, r) in enumerate(((q_b, sq_q), (k_b, sq_k))):
                    v.wait_ge(S["rms_b"], 2 * h + j + 1)
                    v.scalar_tensor_tensor(raw[:, :], raw[:, :], sbg[:, j:j + 1], r[:, :], ALU.mult, ALU.mult)\
                        .then_inc(S["qk_normed"], 1)
                v.wait_ge(S["par_head"], 2 * h + 2)
                v.wait_ge(S["pad_zero"], h + 2)
                v.wait_ge(S["tile_free"], T_HEADS + 8 * h + 3)
                v.tensor_scalar(conv[:, :], qk_pad[:, 0:SEQ], par[:, 0:1], None, ALU.mult).then_inc(S["conv"], 1)
                for j in range(1, 4):
                    v.wait_ge(S["conv"], 4 * h + j)
                    v.scalar_tensor_tensor(conv[:, :], qk_pad[:, j:j + SEQ], par[:, j:j + 1], conv[:, :],
                                           ALU.mult, ALU.add).then_inc(S["conv"], 1)
                split_lo(ga + 2, 1, 0)
                v.wait_ge(S["bc_landed"], 16 * h + 16)
                for i in range(TB):
                    v.tensor_scalar(decay[:, TRI[i]:TRI[i] + SEQ - P * i], bc[:, 0, P * i:], col[:, i:i + 1], 0.0,
                                    ALU.add, ALU.min).then_inc(S["arg_a"], 1)
                v.wait_ge(S["sp_ln"], h + 1)
                v.scalar_tensor_tensor(sp[:, :], z[:, :], 0.0, sp[:, :], ALU.max, ALU.add).then_inc(S["sp_done"], 1)
                v.wait_ge(S["silu_sig"], h + 1)
                v.tensor_tensor(silu[:, :], silu[:, :], conv[:, :], ALU.mult).then_inc(S["silu_done"], 1)
                v.wait_ge(S["sp_masked"], 4 * h + 4)
                v.tensor_copy(sp_hi[:, :], sp[:, :]).then_inc(S["sp_hi"], 1)
                v.wait_ge(S["sp_hi"], h + 1)
                v.tensor_tensor(sp_lo[:, :], sp[:, :], sp_hi[:, :], ALU.subtract).then_inc(S["sp_lo"], 1)
                split_lo(ga + 2, 1, 1)
                v.wait_ge(S["s_made"], h + 1)
                v.wait_ge(S["decay_exp"], h + 1)
                v.scalar_tensor_tensor(decay[:, :], pm[:, 0:TRI_COLS], DQK_A ** -0.5, decay[:, :], ALU.mult, ALU.mult)\
                    .then_inc(S["p_done"], 1)
                v.wait_ge(S["c_made"], h + 1)
                v.tensor_tensor(z[:, :], z[:, :], pa[:, 0:TRI_COLS], ALU.subtract).then_inc(S["arg_b_done"], 1)
                v.wait_ge(S["den_abs"], h + 1)
                v.tensor_tensor(den[:, :], den[:, :], bc[:, 1, :], ALU.max).then_inc(S["den_max"], 1)
                v.wait_ge(S["den_max"], h + 1)
                v.tensor_tensor(den[:, :], den[:, :], den[:, :], ALU.mult).then_inc(S["den_sq"], 1)
                v.wait_ge(S["den_sq"], h + 1)
                v.wait_ge(S["num_ssq"], h + 1)
                v.scalar_tensor_tensor(scl[:, :], den[:, :], EPS, pm[:, 1024:1536], ALU.mult, ALU.add).then_inc(S["var_a"], 1)
                v.wait_ge(S["rms_a"], h + 1)
                v.scalar_tensor_tensor(scl[:, :], pm[:, 0:512], par[:, 4:5], scl[:, :], ALU.mult, ALU.mult).then_inc(S["y"], 1)
                v.wait_ge(S["gate_sig"], 2 * h + 1)
                v.wait_ge(S["y"], 5 * h + 1)
                v.tensor_tensor(scl[:, :], scl[:, :], gate_o[:, :], ALU.mult).then_inc(S["y"], 1)
                v.wait_ge(S["gate_sig"], 2 * h + 2)
                v.wait_ge(S["y"], 5 * h + 2)
                v.tensor_tensor(scl[:, :], scl[:, :], gate_a[:, :], ALU.mult).then_inc(S["y"], 1)
                v.wait_ge(S["pv_b_made"], h + 1)
                v.wait_ge(S["tile_free"], T_HEADS + 8 * h + 8)
                v.tensor_tensor(gate_b[:, :], pa[:, 0:512], gate_b[:, :], ALU.mult).then_inc(S["y"], 1)
                v.wait_ge(S["y"], 5 * h + 4)
                v.tensor_tensor(scl[:, :], scl[:, :], gate_b[:, :], ALU.add).then_inc(S["y"], 1)
                v.wait_ge(S["y"], 5 * h + 5)
                yh = y_hi[:, bass.ds(h, 1), :].rearrange("p a n -> p (a n)")
                v.tensor_copy(yh, scl[:, :]).then_inc(S["y_hi"], 1)
                v.wait_ge(S["y_hi"], h + 1)
                v.tensor_tensor(y_lo[:, bass.ds(h, 1), :].rearrange("p a n -> p (a n)"), scl[:, :], yh, ALU.subtract)\
                    .then_inc(S["head_done"], 1)
            v.wait_ge(S["head_done"], HEADS + 1)
            v.memset(eps[:, :], EPS).then_inc(S["x_area_free"], 1)
            for g in range(G_OUT, G_MLP):
                for hf in (0, 1):
                    split_lo(g + 1, (g + 1) % 2, hf)
                for t in range(TB):
                    n = T_OUT + 4 * (g - G_OUT) + t
                    v.wait_ge(S["x_landed"], 16)
                    v.wait_ge(S["tile_free"], n)
                    v.wait_ge(S["tile_made"], n + 1)
                    xx = x_res[:, t, 512 * (g - G_OUT):512 * (g - G_OUT + 1)]
                    v.tensor_tensor(xx, xx, proj[:, t % 2], ALU.add).then_inc(S["tile_free"], 1)
                    if g == G_MLP - 1:
                        norm_scale(1, t)
            for k in range(KT):
                norm_lo(1, k)
            with v.Fori(0, CHUNKS) as c:
                g = G_MLP + 4 * c
                n = T_MLP + 16 * c
                for gg in range(2):
                    split_lo(g + gg + 1, gg % 2, 0)
                    for j in range(4):
                        i = 4 * gg + j
                        v.wait_ge(S["tile_free"], n + i + 1)
                        v.tensor_tensor(relu_sq[:, i % 2], relu[:, i % 2], relu[:, i % 2], ALU.mult).then_inc(S["a_sq"], 1)
                        v.wait_ge(S["a_hi_done"], 8 * c + i + 1)
                        v.wait_ge(S["a_sq"], 8 * c + i + 1)
                        v.tensor_tensor(act_lo[:, i], relu_sq[:, i % 2], act_hi[:, i], ALU.subtract).then_inc(S["a_lo_done"], 1)
                        if j == 1:
                            split_lo(g + gg + 1, gg % 2, 1)
                for gg in range(2, 4):
                    for hf in (0, 1):
                        split_lo(g + gg + 1, gg % 2, hf)
                    for t in range(TB):
                        i = 4 * gg + t
                        v.wait_ge(S["tile_free"], n + i)
                        v.wait_ge(S["tile_made"], n + i + 1)
                        xx = x_res[:, t, 512 * (gg - 2):512 * (gg - 1)]
                        v.tensor_tensor(xx, xx, proj[:, t % 2], ALU.add).then_inc(S["tile_free"], 1)
            for t in range(TB):
                norm_scale(2, t)
            for k in range(KT):
                norm_lo(2, k)

            def norm_sum(m):
                x, h, d = NORMS[m]
                v.wait_ge(S["c_squared"], m + 1)
                v.tensor_reduce(c_ss[:, m, 0:TB * h], squares[:, 0:TB * h * d].rearrange("p (r d) -> p r d", d=d),
                                AX.X, ALU.add).then_inc(S["c_summed"], 1)

            def norm_mult(m, gain_row=None):
                x, h, d = NORMS[m]
                v.wait_ge(S["c_root"], m + 1)
                r = c_rstd[:, m, 0:TB * h].rearrange("p (t h) -> p t h", t=TB)[:, :, :, None].broadcast_to([P, TB, h, d])
                v.tensor_tensor(x, x, r, ALU.mult).then_inc(S["c_scaled"], 1)
                v.wait_ge(S["c_scaled"], m + 1)
                if gain_row is not None:
                    gr = gain_row[:, None, None, :].broadcast_to([P, TB, h, d])
                    v.tensor_tensor(x, x, gr, ALU.mult).then_inc(S["c_gained"], 1)

            rope_n = [0]

            def rope(x, h, o, half, f0):
                x1, x2 = x[:, :, :, o:o + half], x[:, :, :, o + half:o + 2 * half]
                c, s_ = [b[:, :, None, f0:f0 + half].broadcast_to([P, TB, h, half]) for b in (cosine, sine)]
                A_, B_, C_, D_ = [b[:, 0:TB * h * half].rearrange("p (t h d) -> p t h d", t=TB, h=h) for b in (ra, rb, rc, rd)]
                if rope_n[0]:
                    v.wait_ge(S["rope"], 6 * rope_n[0])
                for dst, xx, w in ((A_, x1, c), (B_, x2, s_), (C_, x2, c), (D_, x1, s_)):
                    v.tensor_tensor(dst, xx, w, ALU.mult).then_inc(S["rope"], 1)
                v.wait_ge(S["rope"], 6 * rope_n[0] + 4)
                v.tensor_tensor(x1, A_, B_, ALU.subtract).then_inc(S["rope"], 1)
                v.tensor_tensor(x2, C_, D_, ALU.add).then_inc(S["rope"], 1)
                rope_n[0] += 1

            def split(g):
                for hf in (0, 1):
                    split_lo(g, g % 2, hf)

            split(G_C + 1)
            norm_sum(0)
            norm_sum(1)
            split(G_C + 2)
            norm_mult(0)
            norm_mult(1)
            for m in range(3):
                v.wait_ge(S["c_hi"], m + 1)
                dst, hi = (cq_lo[:, m], cq_hi[:, m]) if m < 2 else (ckv_lo[:, 0], ckv_hi[:, 0])
                v.scalar_tensor_tensor(dst, pa[:, 512 * m:512 * (m + 1)], c_gain[:, m:m + 1], hi, ALU.mult, ALU.subtract)\
                    .then_inc(S["c_lo"], 1)
            norm_sum(2)
            split(G_U)
            v.wait_ge(S["wide_landed"], 64)
            norm_mult(2, gain_qb)
            v.wait_ge(S["c_gained"], 1)
            norm_sum(3)
            split(G_L)
            norm_mult(3, gain_kb)
            v.wait_ge(S["c_gained"], 2)
            rope(q_b3, HEADS, 0, 8, 16)
            rope(k_b3, KV_D, 0, 8, 16)
            qi = t_k[:, :, 256:512].rearrange("p t (h d) -> p t h d", h=HEADS)
            ki = t_c[:, :, 416:448].rearrange("p t (h d) -> p t h d", h=1)
            rope(qi, HEADS, 0, 4, 24)
            rope(ki, 1, 0, 4, 24)
            v.tensor_scalar(w_idx[:, :, :], t_c[:, :, 448:456], (HEADS ** -0.5) * (IDX_D ** -0.5), None, ALU.mult)\
                .then_inc(S["qi_ready"], 1)
            v.wait_ge(S["tile_free"], T_U + 16)
            v.tensor_copy(k_a3[:, :, :, NOPE:QK_M], t_c[:, :, None, 384:416].broadcast_to([P, TB, HEADS, 32]))\
                .then_inc(S["k_pe_spread"], 1)
            norm_sum(4)
            norm_mult(4, gain_qa)
            norm_sum(5)
            norm_mult(5, gain_ka)
            v.wait_ge(S["c_gained"], 4)
            rope(q_a3, HEADS, NOPE, 16, 0)
            v.wait_ge(S["rope"], 6 * rope_n[0])
            rope(k_a3, HEADS, NOPE, 16, 0)
            v.wait_ge(S["rope"], 6 * rope_n[0])
            v.tensor_copy(mx[:, 0, :], w_idx[:, :, 0]).then_inc(S["q_a_ready"], 1)
            v.tensor_copy(mx[:, 1, :], w_idx[:, :, 0]).then_inc(S["k_a_ready"], 1)
            for h in range(HEADS):
                v.wait_ge(S["idx_relu"], h + 1)
                if h:
                    v.wait_ge(S["idx_sum"], 4 * h)
                for i in range(TB):
                    c = slice(LOW[i], LOW[i] + P * (i + 1))
                    if h == 0:
                        ins = v.tensor_scalar(idx[:, c], rel[0][:, c], w_idx[:, i, 0:1], None, ALU.mult)
                    else:
                        ins = v.scalar_tensor_tensor(idx[:, c], rel[h % 2][:, c], w_idx[:, i, h:h + 1], idx[:, c],
                                                     ALU.mult, ALU.add)
                    ins.then_inc(S["idx_sum"], 1)
            v.wait_ge(S["idx_sum"], 4 * HEADS)
            v.tensor_copy(mx[:, 0, :], mx[:, 0, :]).then_inc(S["idx_done"], 1)
            v.wait_ge(S["idx_causal"], 4)
            v.wait_ge(S["causal_made"], 1)

            holds = [0]

            def held(value, name):
                v.wait_ge(S[name], value)
                v.memset(tick[:, holds[0]:holds[0] + 1], 0.0)
                holds[0] = holds[0] + 1

            def head_max(u, B, mask, scale):
                X = (pa, pm)[u]
                held(B + 1, f"scores{u}")
                for i in range(TB):
                    c = slice(LOW[i], LOW[i] + P * (i + 1))
                    v.tensor_tensor_reduce(p_sb[u][:, c], X[:, c], mask(i), scale, -3.0e38, ALU.add, ALU.max,
                                           mx[:, u, i:i + 1]).then_inc(S[f"smax{u}"], 1)
                v.wait_ge(S[f"smax{u}"], 4 * B + 4)
                v.tensor_scalar(mx[:, u, :], mx[:, u, :], -1.0, None, ALU.mult).then_inc(S[f"nmax{u}"], 1)

            def head_norm(u, B):
                v.wait_ge(S[f"p_exp{u}"], 4 * B + 4)
                v.reciprocal(row_sum[:, u, :], row_sum[:, u, :]).then_inc(S[f"rden{u}"], 1)
                v.wait_ge(S[f"rden{u}"], B + 1)
                for i in range(TB):
                    x = p_sb[u][:, LOW[i]:LOW[i] + P * (i + 1)]
                    v.tensor_scalar(x, x, row_sum[:, u, i:i + 1], None, ALU.mult).then_inc(S[f"p_norm{u}"], 1)

            def top(b, r):
                held(12 * b + 3 * r + 1, "top_out")
                for i in range(1, TB):
                    v.max(top8[:, i - 1, :], idx[:, LOW[i]:LOW[i] + P * (i + 1)]).then_inc(S["top_max"], 1)
                held(12 * b + 3 * r + 3, "top_max")
                for i in range(1, TB):
                    x = idx[:, LOW[i]:LOW[i] + P * (i + 1)]
                    v.match_replace(x, top8[:, i - 1, :], x, TAKEN).then_inc(S["top_out"], 1)

            for kind in range(2):
                scale = (QK_M if kind == 0 else D_D) ** -0.5
                mask = (lambda i: causal[:, 384 - P * i:512]) if kind == 0 else (lambda i: idx[:, LOW[i]:LOW[i] + P * (i + 1)])
                with v.Fori(0, 2) as b:
                    for s in range(2):
                        c = 2 * b + s
                        B = 4 * kind + c
                        split_lo(G_L + B + 1, s, 0)
                        if kind == 0:
                            top(c, 0)
                        head_max(0, B, mask, scale)
                        head_max(1, B, mask, scale)
                        split_lo(G_L + B + 1, s, 1)
                        head_norm(0, B)
                        if kind == 0:
                            top(c, 1)
                        head_norm(1, B)
                        if kind == 0:
                            top(c, 2)
                            top(c, 3)
                if kind == 0:
                    v.wait_ge(S["top_out"], 49)
                    v.tensor_copy(idx[:, LOW[0]:LOW[0] + P], causal[:, 384:512]).then_inc(S["mask"], 1)
                    for i in range(1, TB):
                        x = idx[:, LOW[i]:LOW[i] + P * (i + 1)]
                        v.tensor_scalar(x, x, TAKEN / 2, NEG, ALU.is_gt, ALU.mult).then_inc(S["mask"], 1)
                    v.wait_ge(S["mask"], 4)
            for hf in (0, 1):
                split_lo(G_BR + 1, 0, hf)
            v.wait_ge(S["o_landed"], 16)
            v.wait_ge(S["g_landed"], 16)
            for kind in range(2):
                ks = slice(4 * kind, 4 * kind + 4)
                v.tensor_tensor(o_all[:, ks], o_all[:, ks], g_all[:, ks], ALU.mult).then_inc(S["o_times_g"], 1)
            for kind in range(2):
                ks = slice(4 * kind, 4 * kind + 4)
                v.wait_ge(S["g_sig"], kind + 1)
                v.wait_ge(S["o_times_g"], kind + 1)
                v.tensor_tensor(o_all[:, ks], o_all[:, ks], g_all[:, ks], ALU.mult).then_inc(S["o_gated"], 1)
            for kind in range(2):
                ks = slice(4 * kind, 4 * kind + 4)
                v.wait_ge(S["oh_hi"], kind + 1)
                v.tensor_tensor(h_lo[:, ks], o_all[:, ks], h_hi[:, ks], ALU.subtract).then_inc(S["oh_lo"], 1)
            for j in range(2 * KT):
                n = T_BR + j
                if j == 8:
                    for hf in (0, 1):
                        split_lo(G_FIN, 1, hf)
                v.wait_ge(S["tile_free"], n)
                v.wait_ge(S["tile_made"], n + 1)
                v.wait_ge(S["m_sig"], j + 1)
                v.tensor_tensor(m_all[:, j], proj[:, j % 2], m_all[:, j], ALU.mult).then_inc(S["tile_free"], 1)
                if j >= KT:
                    i = j - KT
                    v.wait_ge(S["tile_free"], n + 1)
                    v.tensor_tensor(m_all[:, j], m_all[:, j], m_all[:, i], ALU.add).then_inc(S["merged"], 1)
                    v.wait_ge(S["mg_hi"], i + 1)
                    v.tensor_tensor(mg_lo[:, i], m_all[:, j], mg_hi[:, i], ALU.subtract).then_inc(S["mg_lo"], 1)
            for hf in (0, 1):
                split_lo(G_FIN + 1, 0, hf)
            v.wait_ge(S["x2_landed"], 16)
            for j in range(KT):
                n = T_FIN + j
                v.wait_ge(S["tile_free"], n)
                v.wait_ge(S["tile_made"], n + 1)
                xx = x_fin[:, j % 4, 512 * (j // 4):512 * (j // 4 + 1)]
                v.tensor_tensor(xx, xx, proj[:, j % 2], ALU.add).then_inc(S["tile_free"], 1)

        @block.tensor
        def _(pe):
            t_ = nc.tensor
            t_.wait_ge(S["consts"], 7)
            norm_pe(0, 0)
            for j in (0, 1):
                made(project(G_GATES, 0, j, j, j, first=True, norm=0 if j == 0 else None))
            t_.wait_ge(S["rows_a"], 1)
            for t in range(TB):
                mm = t_.transpose(pm[:, HEADS * t:HEADS * (t + 1)], g_a[:, t * P:(t + 1) * P], ident[0:HEADS, 0:HEADS])
            mm.then_inc(S["a_turned"], 1)
            t_.wait_ge(S["a_col"], 1)
            with t_.Fori(0, HEADS) as h:
                n = T_HEADS + 8 * h
                ga = G_HEADS + 2 * h

                def tile(j):
                    made(project(ga + j // 4, (1 + j // 4) % 2, n + j, j % 2, j % 4))

                def triangle(out_, lhsT, rhs, rows=P):
                    for i in range(TB):
                        mm = t_.matmul(out_[:, TRI[i]:TRI[i] + SEQ - P * i], lhsT[0:rows, P * i:P * (i + 1)],
                                       rhs[0:rows, P * i:], start=True, stop=True)
                    return mm

                def weighted(out_, keys, weights):
                    for i in range(TB):
                        mm = t_.matmul(out_[:, P * i:SEQ], keys(i), weights[:, TRI[i]:TRI[i] + SEQ - P * i],
                                       start=(i == 0), stop=(i == TB - 1))
                    return mm

                tile(0)
                tile(1)
                tile(2)
                t_.wait_ge(S["head_done"], h + 1)
                for j, sq in enumerate((sq_q, sq_k)):
                    t_.wait_ge(S["tile_free"], n + j + 1)
                    t_.matmul(pa[:, 512 * j:512 * (j + 1)], mean[:, :], sq[:, :], start=True, stop=True).then_inc(S["ssq_made"], 1)
                tile(3)
                t_.wait_ge(S["qk_normed"], 2 * h + 2)
                triangle(pa, k_b, q_b).then_inc(S["z_made"], 1)
                tile(4)
                t_.wait_ge(S["tile_free"], n + 5)
                for m, vT in enumerate((v_bT, v_aT)):
                    for i in range(TB):
                        mm = t_.transpose(pm[:, 512 * m + P * i:512 * m + P * (i + 1)], vT[:, P * i:P * (i + 1)], ident[:, :])
                mm.then_inc(S["v_turned"], 1)
                tile(5)
                t_.wait_ge(S["v_sb"], 2 * h + 2)
                t_.wait_ge(S["ka_landed"], 16 * h + 16)
                triangle(pm, k_a, silu, DQK_A).then_inc(S["s_made"], 1)
                tile(6)
                t_.wait_ge(S["sp_lo"], h + 1)
                for i in range(TB):
                    mms = [(tri_r if i2 == i else ones_r, i2, s_) for i2 in range(i, TB - 1) for s_ in (sp_hi, sp_lo)]
                    mms.append((tri if i == TB - 1 else ones, TB - 1, sp))
                    for q, (w, i2, s_) in enumerate(mms):
                        mm = t_.matmul(pa[:, TRI[i] + P * (i2 - i):TRI[i] + SEQ - P * i], w[:, :],
                                       s_[:, TRI[i2]:TRI[i2] + SEQ - P * i2], start=(q == 0), stop=(q == len(mms) - 1))
                mm.then_inc(S["c_made"], 1)
                t_.wait_ge(S["p_masked"], 4 * h + 4)
                weighted(pm[:, 0:512], lambda i: v_a[:, P * i:P * (i + 1)], decay)
                weighted(pm[:, 512:1024], lambda i: ones[:, :], decay).then_inc(S["num_made"], 1)
                tile(7)
                t_.wait_ge(S["num_sq"], h + 1)
                t_.matmul(pm[:, 1024:1536], mean[:, :], num2[:, :], start=True, stop=True).then_inc(S["num_ssq"], 1)
                t_.wait_ge(S["a_b"], h + 1)
                weighted(pa[:, 0:512], lambda i: v_b[:, P * i:P * (i + 1)], z).then_inc(S["pv_b_made"], 1)
            t_.wait_ge(S["head_done"], HEADS)
            for g in range(G_OUT, G_MLP):
                for t in range(TB):
                    i = 4 * (g - G_OUT) + t
                    made(project(g, g % 2, T_OUT + i, i % 2, t, tokens=True, act=(y_hi, y_lo),
                                 last=("head_done", HEADS + 1) if i == 0 else None))
            norm_pe(1, T_MLP)
            with t_.Fori(0, CHUNKS) as c:
                g = G_MLP + 4 * c
                n = T_MLP + 16 * c
                for i in range(8):
                    made(project(g + i // 4, (1 + i // 4) % 2, n + i, i % 2, i % 4, norm=1 if i == 0 else None))
                t_.wait_ge(S["a_lo_done"], 8 * c + 8)
                for i in range(8, 16):
                    made(project(g + i // 4, (1 + i // 4) % 2, n + i, i % 2, i % 4,
                                 tokens=True, act=(act_hi, act_lo)))
            norm_pe(2, T_END1)
            t_.wait_ge(S["norm_lo"], 3 * KT)

            def tokens(g, n0):
                for t in range(TB):
                    made(project(g, g % 2, n0 + t, (n0 + t) % 2, t, tokens=True))

            tokens(G_C, T_C)
            tokens(G_C + 1, T_Q)
            t_.wait_ge(S["c_scaled"], 2)
            for m in range(3):
                for t in range(TB):
                    mm = t_.transpose(pa[:, 512 * m + P * t:512 * m + P * (t + 1)], t_c[:, t, P * m:P * (m + 1)], ident[:, :])
                mm.then_inc(S["c_turned"], 1)
            tokens(G_C + 2, T_K)
            t_.wait_ge(S["c_lo"], 3)
            for t in range(TB):
                for q, (act_, kts, k0) in enumerate((((cq_hi, cq_lo), 2, 0), ((cq_hi, cq_lo), 2, 2),
                                                     ((ckv_hi, ckv_lo), 1, 4), ((ckv_hi, ckv_lo), 1, 5))):
                    n = T_U + 4 * t + q
                    made(project(G_U, 0, n, q % 2, t, tokens=True, act=act_, kts=kts, k0=k0))
            t_.wait_ge(S["qi_ready"], 1)
            for t in range(TB):
                mm = t_.transpose(pa[0:IDX_D, P * t:P * (t + 1)], t_c[:, t, 416:448], ident[:, :])
            mm.then_inc(S["ki_turned"], 1)
            for h in range(HEADS):
                X = pm if h % 2 else pa
                if h == 0:
                    t_.wait_ge(S["ki_sb"], 1)
                if h >= 2:
                    t_.wait_ge(S["idx_relu"], h - 1)
                for t in range(TB):
                    mm = t_.transpose(X[0:IDX_D, P * t:P * (t + 1)], t_k[:, t, 256 + IDX_D * h:256 + IDX_D * (h + 1)], ident[:, :])
                mm.then_inc(S["qi_turned"], 1)
                t_.wait_ge(S["qi_sb"], h + 1)
                for i in range(TB):
                    mm = t_.matmul(X[:, LOW[i]:LOW[i] + P * (i + 1)], qiT[h % 2][:, P * i:P * (i + 1)],
                                   kiT[:, 0:P * (i + 1)], start=True, stop=True)
                mm.then_inc(S["idx_made"], 1)
            t_.wait_ge(S["idx_relu"], HEADS)

            def gate(B, s, i):
                made(project(G_L + B, 1 - s, T_L + 3 * B + i, (s + i) % 2, i))

            def head_turn(u, B, d):
                X = (pa, pm)[u]
                t_.wait_ge(S[f"staged{u}"], 2 * B + 2)
                t_.wait_ge(S[f"o_sb{u}"], B + 1)
                d = QK_M
                for w, st in enumerate((q_st[u], k_st[u])):
                    for t in range(TB):
                        mm = t_.transpose(X[0:d, 512 * w + P * t:512 * w + P * (t + 1)], st[:, t, 0:d], ident[:, :])
                mm.then_inc(S[f"qk_turned{u}"], 1)

            def head_scores(u, B, d):
                X = (pa, pm)[u]
                t_.wait_ge(S[f"qk_sb{u}"], 2 * B + 2)
                for i in range(TB):
                    mm = t_.matmul(X[:, LOW[i]:LOW[i] + P * (i + 1)], qT[u][0:d, P * i:P * (i + 1)],
                                   kT[u][0:d, 0:P * (i + 1)], start=True, stop=True)
                mm.then_inc(S[f"scores{u}"], 1)

            def head_pT(u, B):
                X = (pa, pm)[u]
                t_.wait_ge(S[f"p_norm{u}"], 4 * B + 4)
                for j in range(TB):
                    for i in range(j, TB):
                        o = TRI[j] + P * (i - j)
                        mm = t_.transpose(X[:, o:o + P], p_sb[u][:, LOW[i] + P * j:LOW[i] + P * (j + 1)], ident[:, :])
                mm.then_inc(S[f"p_turned{u}"], 1)

            def head_pv(u, B):
                X = (pa, pm)[u]
                t_.wait_ge(S[f"pT_sb{u}"], B + 1)
                t_.wait_ge(S[f"v_staged{u}"], 2 * B + 2)
                for i in range(TB):
                    mm = t_.matmul(X[:, P * i:SEQ], v_st[u][:, i, :], pT[u][:, TRI[i]:TRI[i] + SEQ - P * i],
                                   start=(i == 0), stop=(i == TB - 1))
                mm.then_inc(S[f"pv{u}"], 1)

            for kind, d in enumerate((QK_M, D_D)):
                with t_.Fori(0, 2) as b:
                    for s in range(2):
                        B = 4 * kind + 2 * b + s
                        head_turn(0, B, d)
                        head_turn(1, B, d)
                        gate(B, s, 0)
                        head_scores(0, B, d)
                        head_scores(1, B, d)
                        gate(B, s, 1)
                        head_pT(0, B)
                        head_pT(1, B)
                        gate(B, s, 2)
                        head_pv(0, B)
                        head_pv(1, B)
            for kind in range(2):
                t_.wait_ge(S["oh_lo"], kind + 1)
                for j in range(KT):
                    n = T_BR + KT * kind + j
                    made(project(G_BR + kind, (1 + kind) % 2, n, j % 2, j % 4, kts=4, k0=4 * (j // 4),
                                 act=(h_hi[:, 4 * kind:4 * kind + 4], h_lo[:, 4 * kind:4 * kind + 4])))
            t_.wait_ge(S["mg_lo"], KT)
            for g in range(2):
                for t in range(TB):
                    n = T_FIN + 4 * g + t
                    made(project(G_FIN + g, (1 + g) % 2, n, t % 2, t, tokens=True, act=(mg_hi, mg_lo)))


def k_tiles(a):
    return a.reshape(-1, P, a.shape[1]).transpose(1, 0, 2)


def lay_out(v):
    v = {name: np.asarray(a) for name, a in v.items()}
    one = {name: a[0] for name, a in v.items()}
    wall = np.zeros((N_GROUPS, P, KT, 512), np.float32)

    sizes = (512, 512, 1024, 1024, HEADS, HEADS, 1024, 1024, 1024, 1024, 1024)
    q_a, k_a, v_a, o_a, i_a, f_a, q_b, k_b, v_b, g_a, g_b = np.split(k_tiles(one["w_in"]), np.cumsum(sizes)[:-1], axis=2)
    wall[G_GATES, :, :, 0:HEADS] = i_a
    wall[G_GATES, :, :, P:P + HEADS] = f_a
    for h in range(HEADS):
        wide, narrow = slice(P * h, P * (h + 1)), slice(DQK_A * h, DQK_A * (h + 1))
        wall[G_HEADS + 2 * h] = np.concatenate(
            [q_b[:, :, wide], k_b[:, :, wide], q_a[:, :, narrow], k_a[:, :, narrow], v_b[:, :, wide]], axis=2)
        wall[G_HEADS + 2 * h + 1] = np.concatenate([w[:, :, wide] for w in (v_a, o_a, g_a, g_b)], axis=2)
    for j in range(2):
        half = slice(512 * j, 512 * (j + 1))
        wall[G_OUT + j] = k_tiles(one["w_out"])[:, :, half]
        wall[G_FIN + j] = k_tiles(one["w_out_2"])[:, :, half]
        for c in range(CHUNKS):
            wall[G_MLP + 4 * c + j] = k_tiles(one["w_up"])[:, :, DM * c + 512 * j:DM * c + 512 * (j + 1)]
            wall[G_MLP + 4 * c + 2 + j] = k_tiles(one["w_down"][DM * c:DM * (c + 1)])[:, :, half]
    head_par = np.zeros((P, HEADS, 7), np.float32)
    taps = one["conv_w"].reshape(4, 2, HEADS, DQK_A)
    head_par[0:DQK_A, :, 0:4] = taps[:, 0].transpose(2, 1, 0)
    head_par[DQK_A:P, :, 0:4] = taps[:, 1].transpose(2, 1, 0)
    head_par[:, :, 4] = one["mlstm_norm_g"].reshape(HEADS, P).T
    head_par[:, :, 5:7] = one["b_gate"].reshape(2, HEADS, P).transpose(2, 1, 0)

    sizes = (256, 128, 32, 512, 512, 128, 128, 512, 256, 32, 8, 1024, 1024)
    (c_q, c_kv, k_pe, gate_a, q_b, k_b, v_b, gate_b, q_i, k_i, w_i, m_a, m_b) = np.split(
        k_tiles(one["w_in_2"]), np.cumsum(sizes)[:-1], axis=2)
    wall[G_C, :, :, 0:456] = np.concatenate([c_q, c_kv, k_pe, k_i, w_i], axis=2)
    wall[G_C + 1] = q_b
    wall[G_C + 2] = np.concatenate([k_b, v_b, q_i], axis=2)
    uq = k_tiles(one["mla_w_uq_2"])
    ukv = one["mla_w_ukv_2"].reshape(P, HEADS, 2, NOPE)
    for k in range(2):
        wall[G_U, :, k] = uq[:, k, 0:512]
        wall[G_U, :, 2 + k, 0:256] = uq[:, k, 512:768]
        wall[G_U, :, 4 + k] = ukv[:, :, k].reshape(P, 512)
    gates = np.concatenate([gate_a, gate_b, m_a, m_b], axis=2)
    for j in range(8):
        wall[G_L + j, :, :, 0:384] = gates[:, :, 384 * j:384 * (j + 1)]
    for j, name in enumerate(("w_branch_mla_2", "w_branch_dsa_2")):
        wall[G_BR + j] = one[name].reshape(4, P, 2, 512).transpose(1, 2, 0, 3).reshape(P, 8, 512)
    wide_gains = np.zeros((4, QK_M), np.float32)
    for j, name in enumerate(("mla_q_gain_2", "mla_k_gain_2", "dsa_q_gain_2", "dsa_k_gain_2")):
        wide_gains[j, 0:one[name].size] = one[name]
    inv_freq = np.concatenate([np.float32(500000.0) ** (-np.arange(0, r, 2, dtype=np.float32) / np.float32(r))
                               for r in (32, 16, 8)])

    gains = np.concatenate([one[n].reshape(KT, P).T for n in ("norm_mix_g", "norm_mlp_g", "norm_gain_2")], axis=1)
    c_gains = np.concatenate([one["mla_q_norm_2"].reshape(2, P), one["mla_kv_norm_2"].reshape(1, P)]).T
    return {
        "x": one["x"], "wall": wall, "gains": gains, "head_par": head_par,
        "sb_gains": np.stack([one["sb_q_norm_g"], one["sb_k_norm_g"]], axis=1),
        "b_if": one["b_if"].reshape(2, HEADS).T,
        "positions": one["positions_2"].astype(np.int32).reshape(TB, P).T,
        "inv_freq": inv_freq.astype(np.float32).reshape(1, N_FREQ), "wide_gains": wide_gains, "c_gains": c_gains,
        "b_merge": one["b_merge_2"].reshape(2 * KT, P).T,
    }


def kernel(**inputs):
    import concourse.bacc as bacc
    from concourse.bass_utils import run_bass_kernel_spmd

    nc = bacc.Bacc("TRN2", target_bir_lowering=False, num_devices=1)
    arrays, args = {}, []
    for name, a in lay_out(inputs).items():
        a = np.ascontiguousarray(a)
        arrays[f"in_{name}"] = a
        args.append(nc.dram_tensor(f"in_{name}", a.shape, mybir.dt.from_np(a.dtype), kind="ExternalInput").ap())
    args.append(nc.dram_tensor("result", (SEQ, DM), F32, kind="ExternalOutput").ap())
    program(nc, *args)
    r = run_bass_kernel_spmd(nc, [arrays], core_ids=[0])
    return r.results[0]["result"].reshape(1, SEQ, DM)
```

```python
from contextlib import ExitStack

import numpy as np

import concourse.bass as bass
from concourse import mybir

F32 = mybir.dt.float32
F32R = mybir.dt.float32r
ALU = mybir.AluOpType
ACT = mybir.ActivationFunctionType
AX = mybir.AxisListType

P = 128
SEQ = 512
TB = SEQ // P
DM = 1024
KT = DM // P
HEADS = 8
FF = 4096
CHUNKS = FF // DM
EPS = 1e-6
DQK_A = 64
HD_B = 128
NEG = -1.0e30

G_GATES = 0
G_HEADS = 1
G_OUT = G_HEADS + 2 * HEADS
G_MLP = G_OUT + 2
G_END1 = G_MLP + 4 * CHUNKS
T_HEADS = 2
T_OUT = T_HEADS + 8 * HEADS
T_MLP = T_OUT + 8
T_END1 = T_MLP + 16 * CHUNKS

TRI = {0: 0, 1: 512, 3: 896, 2: 1024}
TRI_COLS = 1280

QK_M = 96
NOPE = 64
D_D = 64
KV_D = 2
IDX_D = 32
N_FREQ = 28
TAKEN = -3.0e38
PI = float(np.pi)
TWO_PI_HI = 6.28125
TWO_PI_LO = 2 * PI - TWO_PI_HI
ROUND = 1.5 * 2.0 ** 23
G_C = G_END1
G_K = G_C + 1
G_U = G_K + 1
G_Q = G_U + 1
G_L = G_Q + 1
G_BR = G_L + 8
G_FIN = G_BR + 2
N_GROUPS = G_FIN + 2
T_C = T_END1
T_K = T_C + 4
T_U = T_K + 4
T_Q = T_U + 16
T_L = T_Q + 4
T_BR = T_L + 24
T_FIN = T_BR + 16
T_END = T_FIN + 8
SIN_MAX = 3.1415925


def program(nc, x_in, wall, gains, head_par, sb_gains, b_if, *rest):
    *block2_in, out = rest
    with ExitStack() as ctx:
        def sb(name, shape, dt=F32):
            return ctx.enter_context(nc.sbuf_tensor(name, shape, dt))

        class Signals(dict):
            def __missing__(self, name):
                self[name] = ctx.enter_context(nc.semaphore(name))
                return self[name]

        S = Signals()

        w_raw = sb("w_raw", [P, 2, 4, 512])
        w_hi = sb("w_hi", [P, 2, KT, 512], F32R)
        w_lo = sb("w_lo", [P, 2, KT, 512], F32R)
        h_hi = sb("h_hi", [P, KT, SEQ], F32R)
        h_lo = sb("h_lo", [P, KT, SEQ], F32R)
        ident = sb("ident", [P, P])
        mean = sb("mean", [P, P])
        ones = sb("ones", [P, P])
        ones_r = sb("ones_r", [P, P], F32R)
        eps = sb("eps", [P, 1])
        gain = sb("gain", [P, 3 * KT])
        ss = sb("ss", [P, 3, TB])
        lnv = sb("lnv", [P, 3, TB])
        rstd = sb("rstd", [P, 3, TB])
        K = 1024
        base = (nc.sbuf_base + 31) // 32 * 32
        slab = sb("slab", [P, 90 * 256])

        def at(name, offset, shape, dt=F32):
            return nc.alloc_sbuf_tensor_at(name, shape, dt, offset=base + int(offset))

        y_hi = at("y_hi", 0, [P, KT, SEQ], F32R)
        y_lo = at("y_lo", 16 * K, [P, KT, SEQ], F32R)
        sp_hi = at("sp_hi", 32 * K, [P, TRI_COLS], F32R)
        sp_lo = at("sp_lo", 37 * K, [P, TRI_COLS], F32R)
        z = at("z", 42 * K, [P, TRI_COLS])
        sp = at("sp", 47 * K, [P, TRI_COLS])
        decay = at("decay", 52 * K, [P, TRI_COLS])
        bc = at("bc", 57 * K, [P, 2, SEQ])
        names = "q_b k_b sq_q sq_k conv silu k_a v_bT v_aT v_b v_a gate_a gate_b".split()
        (q_b, k_b, sq_q, sq_k, conv, silu, k_a, v_bT, v_aT, v_b, v_a, gate_a, gate_b) = [
            at(n, (61 + 2 * i) * K, [P, SEQ]) for i, n in enumerate(names)]
        gate_o = at("gate_o", 87 * K + 128, [P, SEQ])
        den, num2, scl = sq_q, sq_k, silu
        qk_pad = at("qk_pad", 47 * K, [P, 3 + SEQ])
        tri_r = sb("tri_r", [P, P], F32R)
        tri = at("tri", 89.25 * K, [P, P])
        par = sb("par", [P, 7])
        hp = sb("hp", [P, HEADS, 7])
        col = sb("col", [P, TB])
        a_col = sb("a_col", [P, TB, HEADS])
        sbg = sb("sbg", [P, 2])
        x_res = at("x_res", 61 * K, [P, TB, DM])
        xs = at("xs", 44 * K, [P, TB, DM])
        act_hi = at("act_hi", 0, [P, KT, SEQ], F32R)
        act_lo = at("act_lo", 16 * K, [P, KT, SEQ], F32R)
        relu = at("relu", 32 * K, [P, 2, SEQ])
        relu_sq = at("relu_sq", 36 * K, [P, 2, SEQ])
        (g_i, g_f, g_abs, g_ls, g_F, g_a, g_G, g_m, one_row) = [
            at(f"gate_row{i}", (16 + 2 * i) * K, [HEADS, SEQ]) for i in range(9)]
        g_out = at("g_out", 40 * K, [HEADS, 2, SEQ])
        bif = sb("bif", [HEADS, 2])

        (positions, inv_freq, wide_gains, c_gains, b_merge) = block2_in
        cosine = sb("cosine", [P, TB, N_FREQ])
        sine = sb("sine", [P, TB, N_FREQ])
        c_gain = sb("c_gain", [P, 3])
        merge_bias = sb("merge_bias", [P, 2 * KT])
        c_ss = sb("c_ss", [P, 21, HEADS])
        w_idx = sb("w_idx", [P, TB, HEADS])
        top8 = sb("top8", [P, 3, 8])
        tick = sb("tick", [P, 33])
        mx = sb("mx", [P, 2, TB])
        row_sum = sb("row_sum", [P, 2, TB])
        (ang, turns, angles_c) = [at(f"angles{i}", (34 + i) * K, [P, TB, N_FREQ]) for i in range(3)]
        pos_i = at("pos_i", 43 * K, [P, TB], mybir.dt.int32)
        pos_f = at("pos_f", 43 * K + 32, [P, TB])
        freqs = at("freqs", 43 * K + 64, [P, N_FREQ])
        q_a2 = at("q_a2", 0, [P, TB, HEADS * QK_M])
        k_a2 = at("k_a2", 12 * K, [P, TB, HEADS * QK_M])
        v_a2 = at("v_a2", 24 * K, [P, TB, HEADS * D_D])
        q_b2 = at("q_b2", 32 * K, [P, TB, HEADS * D_D])
        k_b2 = at("k_b2", 40 * K, [P, TB, KV_D * D_D])
        v_b2 = at("v_b2", 42 * K, [P, TB, KV_D * D_D])
        idx = at("idx", 44 * K, [P, TRI_COLS])
        causal = at("causal", 49 * K, [P, SEQ])
        pT = [at(f"pT{u}", (51 + 16 * u) * K, [P, TRI_COLS]) for u in range(2)]
        kT = [at(f"kT{u}", (56, 79)[u] * K, [P, SEQ]) for u in range(2)]
        qT = [at(f"qT{u}", (58, 72)[u] * K, [P, SEQ]) for u in range(2)]
        p_sb = [at(f"p_sb{u}", (60 + 14 * u) * K, [P, TRI_COLS]) for u in range(2)]
        q_st = [at(f"q_st{u}", (60 + 14 * u) * K, [P, TB, QK_M]) for u in range(2)]
        k_st = [at(f"k_st{u}", (61.5 + 14 * u) * K, [P, TB, QK_M]) for u in range(2)]
        v_st = [at(f"v_st{u}", (65 + 16 * u) * K, [P, TB, P]) for u in range(2)]
        gate_st = at("gate_st", 83 * K, [P, 2, SEQ])
        o_st = at("o_st", 87 * K, [P, SEQ])
        t_c = at("t_c", 51 * K, [P, TB, 512])
        t_k = at("t_k", 59 * K, [P, TB, 512])
        squares = [at(f"squares{i}", (67 + 3 * i) * K, [P, HEADS * QK_M]) for i in range(2)]
        ra, rb, rc, rd = [at(f"rope{i}", (49 + i / 2) * K, [P, P]) for i in range(4)]
        cq_hi = at("cq_hi", 79 * K, [P, 2, SEQ], F32R)
        cq_lo = at("cq_lo", 83 * K, [P, 2, SEQ], F32R)
        ckv_hi = at("ckv_hi", 44 * K, [P, 1, SEQ], F32R)
        ckv_lo = at("ckv_lo", 46 * K, [P, 1, SEQ], F32R)
        rel = [at(f"rel{u}", (77 + 5 * u) * K, [P, TRI_COLS]) for u in range(2)]
        gain_qa, gain_ka, gain_qb, gain_kb = [at(f"gain_w{i}", (88 * 1024 + 384 * i), [P, d])
                                              for i, d in enumerate((96, 96, 64, 64))]
        o_all = at("o_all", 0, [P, KT, SEQ])
        g_all = at("g_all", 16 * K, [P, KT, SEQ])
        m_all = at("m_all", 32 * K, [P, 2 * KT, SEQ])
        x_fin = at("x_fin", 74 * K, [P, TB, DM])
        mg_hi = at("mg_hi", 0, [P, KT, SEQ], F32R)
        mg_lo = at("mg_lo", 16 * K, [P, KT, SEQ], F32R)
        x2_d = nc.dram_tensor("x2", [SEQ, DM], F32, kind="Internal").ap()
        gates_d = nc.dram_tensor("gates", [3 * KT, P, SEQ], F32, kind="Internal").ap()
        o_d = nc.dram_tensor("heads_out", [KT, P, SEQ], F32, kind="Internal").ap()

        def bcast(ap, shape):
            return ap.broadcast_to(shape)

        q_a3, k_a3 = [b[:, :, :].rearrange("p t (h d) -> p t h d", h=HEADS) for b in (q_a2, k_a2)]
        q_b3 = q_b2[:, :, :].rearrange("p t (h d) -> p t h d", h=HEADS)
        k_b3 = k_b2[:, :, :].rearrange("p t (h d) -> p t h d", h=KV_D)
        PIECES = []
        for t in range(TB):
            PIECES.append((t_c[:, t:t + 1, 0:256].rearrange("p t (h d) -> p t h d", h=1), 1, 1, 256))
            PIECES.append((t_c[:, t:t + 1, 256:384].rearrange("p t (h d) -> p t h d", h=1), 1, 1, 128))
        PIECES.append((k_b3, TB, KV_D, D_D))
        for t in range(TB):
            PIECES.append((q_a3[:, t:t + 1], 1, HEADS, QK_M))
            PIECES.append((k_a3[:, t:t + 1], 1, HEADS, QK_M))
        for t in range(TB):
            PIECES.append((q_b3[:, t:t + 1], 1, HEADS, D_D))
        P_KB, P_A, P_QB = 8, 9, 17

        LOW = {3: 0, 2: 512, 0: 896, 1: 1024}
        TOPB = {1: 1024, 2: 512, 3: 0}

        proj = ctx.enter_context(nc.psum_tensor("proj", [P, 2, 512], F32))
        pa = ctx.enter_context(nc.psum_tensor("pa", [P, 3 * 512], F32))
        pm = ctx.enter_context(nc.psum_tensor("pm", [P, 3 * 512], F32))
        rows_d = nc.dram_tensor("gate_rows", [HEADS, 2, SEQ], F32, kind="Internal").ap()

        block = ctx.enter_context(nc.Block())

        def tiles_by(g):
            return 2 + 4 * g

        def load_half(g, half, first=False):
            if not first:
                nc.sync.wait_ge(S["w_lo_done"], 2 * g + half - 1)
            nc.sync.dma_start(w_raw[:, half], wall[bass.ds(g, 1), :, 4 * half:4 * half + 4, :]
                              .rearrange("a p k n -> p (a k) n")).then_inc(S[f"w_landed{half}"], 16)

        def split_hi(g, slot, half, first=False, used=None):
            nc.scalar.wait_ge(S[f"w_landed{half}"], 16 * g + 16)
            if not first:
                nc.scalar.wait_ge(S["tile_made"], tiles_by(g - 2) if used is None else used)
            nc.scalar.activation(w_hi[:, slot, 4 * half:4 * half + 4, :], w_raw[:, half], ACT.Copy)\
                .then_inc(S["w_hi_done"], 1)

        def split_lo(g, slot, half):
            nc.vector.wait_ge(S[f"w_landed{half}"], 16 * g + 16)
            nc.vector.wait_ge(S["w_hi_done"], 2 * g + half + 1)
            nc.vector.tensor_tensor(w_lo[:, slot, 4 * half:4 * half + 4, :], w_raw[:, half],
                                    w_hi[:, slot, 4 * half:4 * half + 4, :], ALU.subtract)\
                .then_inc(S["w_lo_done"], 1)

        def project(g, slot, n, bank, j, tokens=False, act=None, kts=KT, k0=0, first=False, norm=None,
                    last=None):
            a_hi, a_lo = act or (h_hi, h_lo)
            if not first:
                nc.tensor.wait_ge(S["tile_free"], n - 1)
            c = slice(j * P, (j + 1) * P)
            for k in range(kts):
                if k == 0:
                    nc.tensor.wait_ge(S["w_lo_done"], 2 * g + 1 + k0 // 4)
                elif k + k0 == 4:
                    nc.tensor.wait_ge(S["w_lo_done"], 2 * g + 2)
                if norm is not None:
                    nc.tensor.wait_ge(S["norm_lo"], KT * norm + k + 1)
                if last and k == kts - 1:
                    nc.tensor.wait_ge(S[last[0]], last[1])
                for q, (w, a) in enumerate(((w_hi, a_hi), (w_hi, a_lo), (w_lo, a_hi))):
                    if tokens:
                        lhsT, rhs = a[:, k, c], w[:, slot, k0 + k, :]
                    else:
                        lhsT, rhs = w[:, slot, k0 + k, c], a[:, k, :]
                    mm = nc.tensor.matmul(proj[:, bank, :], lhsT, rhs, start=(k == 0 and q == 0),
                                          stop=(k == kts - 1 and q == 2))
            return mm

        def made(mm):
            mm.then_inc(S["tile_made"], 1)

        def norm_bank(k):
            if k < 2:
                return proj[:, k]
            return (pa, pm)[(k - 2) // 3][:, 512 * ((k - 2) % 3):512 * ((k - 2) % 3 + 1)]

        def norm_rstd(r, t):
            nc.scalar.activation(xs[:, t], x_res[:, t], ACT.Square, accum_out=ss[:, r, t:t + 1])\
                .then_inc(S["norm_ss"], 1)
            nc.scalar.wait_ge(S["norm_ss"], TB * r + t + 1)
            nc.scalar.activation(lnv[:, r, t:t + 1], ss[:, r, t:t + 1], ACT.Ln, bias=eps[:, 0:1], scale=1.0 / DM)\
                .then_inc(S["norm_ln"], 1)
            nc.scalar.wait_ge(S["norm_ln"], TB * r + t + 1)
            nc.scalar.activation(rstd[:, r, t:t + 1], lnv[:, r, t:t + 1], ACT.Exp, scale=-0.5).then_inc(S["norm_rstd"], 1)

        def norm_hi(r, k):
            nc.scalar.wait_ge(S["norm_turned"], KT * r + k + 1)
            nc.scalar.activation(h_hi[:, k], norm_bank(k), ACT.Copy, scale=gain[:, KT * r + k:KT * r + k + 1])\
                .then_inc(S["norm_hi"], 1)

        def norm_scale(r, t):
            nc.vector.wait_ge(S["norm_rstd"], TB * r + t + 1)
            nc.vector.tensor_scalar(xs[:, t], x_res[:, t], rstd[:, r, t:t + 1], None, ALU.mult)\
                .then_inc(S["norm_scaled"], 1)

        def norm_lo(r, k):
            nc.vector.wait_ge(S["norm_hi"], KT * r + k + 1)
            nc.vector.scalar_tensor_tensor(h_lo[:, k], norm_bank(k), gain[:, KT * r + k:KT * r + k + 1],
                                           h_hi[:, k], ALU.mult, ALU.subtract).then_inc(S["norm_lo"], 1)

        def norm_pe(r, tiles_before):
            if tiles_before:
                nc.tensor.wait_ge(S["tile_free"], tiles_before)
            for t in range(TB):
                nc.tensor.wait_ge(S["norm_scaled"], TB * r + t + 1)
                for k in range(KT):
                    mm = nc.tensor.transpose(norm_bank(k)[:, t * P:(t + 1) * P], xs[:, t, k * P:(k + 1) * P], ident[:, :])
                    if t == TB - 1:
                        mm.then_inc(S["norm_turned"], 1)

        pos_b = pos_f[:, :, None].broadcast_to([P, TB, N_FREQ])
        freq_b = freqs[:, None, :].broadcast_to([P, TB, N_FREQ])
        A3, T3, C3 = ang[:, :, :], turns[:, :, :], angles_c[:, :, :]
        ANGLES = [
            (pos_f, lambda v: v.tensor_copy(pos_f[:, :], pos_i[:, :])),
            (ang, lambda v: v.tensor_tensor(A3, pos_b, freq_b, ALU.mult)),
            (turns, lambda v: v.tensor_scalar(T3, A3, 1 / (2 * PI), ROUND, ALU.mult, ALU.add)),
            (turns, lambda v: v.tensor_scalar(T3, T3, ROUND, None, ALU.subtract)),
            (ang, lambda v: v.scalar_tensor_tensor(A3, T3, -TWO_PI_HI, A3, ALU.mult, ALU.add)),
            (ang, lambda v: v.scalar_tensor_tensor(A3, T3, -TWO_PI_LO, A3, ALU.mult, ALU.add)),
            (angles_c, lambda v: v.tensor_scalar(C3, A3, PI / 2, None, ALU.add)),
            (turns, lambda v: v.tensor_scalar(T3, C3, PI, 2 * PI, ALU.is_gt, ALU.mult)),
            (angles_c, lambda v: v.tensor_tensor(C3, C3, T3, ALU.subtract)),
            (ang, lambda v: v.tensor_scalar(A3, A3, SIN_MAX, -SIN_MAX, ALU.min, ALU.max)),
            (angles_c, lambda v: v.tensor_scalar(C3, C3, SIN_MAX, -SIN_MAX, ALU.min, ALU.max)),
        ]

        @block.sync
        def _(sp_):
            load_half(0, 0, first=True)
            load_half(0, 1, first=True)
            with nc.sync.Fori(1, N_GROUPS) as g:
                for half in (0, 1):
                    load_half(g, half)
            o_v, x_v = out.rearrange("(t p) d -> p t d", p=P), x_fin[:, :, :]
            for half in range(2):
                nc.sync.wait_ge(S["tile_free"], T_FIN + 4 * (half + 1))
                nc.sync.dma_start(o_v[:, :, 512 * half:512 * (half + 1)], x_v[:, :, 512 * half:512 * (half + 1)])\
                    .then_inc(S["out_stored"], 16)
            nc.sync.wait_ge(S["out_stored"], 32)

        @block.gpsimd
        def _(pool):
            gp = nc.gpsimd
            for dst, src in ((gain, gains), (hp, head_par), (sbg, sb_gains), (bif, b_if), (c_gain, c_gains), (merge_bias, b_merge),
                             (pos_i, positions), (freqs, inv_freq.broadcast_to([P, N_FREQ]))):
                gp.dma_start(dst[:], src).then_inc(S["par_landed"], 16)
            gp.memset(ident[:, :], 0.0).then_inc(S["c0"], 1)
            gp.memset(ones[:, :], 1.0).then_inc(S["c0"], 1)
            gp.memset(mean[:, :], 1.0 / P).then_inc(S["consts"], 1)
            gp.memset(eps[:, :], EPS).then_inc(S["consts"], 1)
            gp.memset(one_row[:, :], 1.0).then_inc(S["consts"], 1)
            gp.wait_ge(S["c0"], 2)
            gp.affine_select(out=ident[:, :], in_=ident[:, :], compare_op=ALU.not_equal, fill=1.0, base=0,
                             pattern=[[-1, P]], channel_multiplier=1).then_inc(S["consts"], 1)
            gp.tensor_copy(ones_r[:, :], ones[:, :]).then_inc(S["consts"], 1)
            gp.affine_select(out=tri[:, :], in_=ones[:, :], compare_op=ALU.is_ge, fill=0.0, base=0,
                             pattern=[[-1, P]], channel_multiplier=1).then_inc(S["consts"], 1)
            gp.affine_select(out=tri_r[:, :], in_=ones[:, :], compare_op=ALU.is_ge, fill=0.0, base=0,
                             pattern=[[-1, P]], channel_multiplier=1).then_inc(S["consts"], 1)
            gp.wait_ge(S["rows_ready"], 1)
            gp.dma_start(rows_d, g_out[:, :, :]).then_inc(S["rows_stored"], 16)
            gp.wait_ge(S["rows_stored"], 16)
            for h in range(HEADS):
                if h:
                    gp.wait_ge(S["head_done"], h + 1)
                gp.dma_start(bc[:, :, :], rows_d[bass.ds(h, 1)].broadcast_to([P, 2, SEQ])).then_inc(S["bc_landed"], 16)
                gp.wait_ge(S["silu_done"], h + 1)
                gp.dma_start(k_a[0:DQK_A, :], silu[DQK_A:P, :]).then_inc(S["ka_landed"], 16)
                gp.wait_ge(S["sp_done"], h + 1)
                for i in range(TB):
                    d = sp[:, TRI[i]:TRI[i] + P]
                    gp.affine_select(out=d, in_=d, compare_op=ALU.is_gt, fill=0.0, base=0,
                                     pattern=[[1, P]], channel_multiplier=-1).then_inc(S["sp_masked"], 1)
                gp.wait_ge(S["p_done"], h + 1)
                for i in range(TB):
                    d = decay[:, TRI[i]:TRI[i] + P]
                    gp.affine_select(out=d, in_=d, compare_op=ALU.is_ge, fill=0.0, base=0,
                                     pattern=[[1, P]], channel_multiplier=-1).then_inc(S["p_masked"], 1)
                gp.wait_ge(S["arg_b_done"], h + 1)
                for i in range(TB):
                    d = z[:, TRI[i]:TRI[i] + P]
                    gp.affine_select(out=d, in_=d, compare_op=ALU.is_gt, fill=NEG, base=0,
                                     pattern=[[1, P]], channel_multiplier=-1).then_inc(S["arg_b_masked"], 1)
            gp.wait_ge(S["head_done"], HEADS + 1)
            gp.wait_ge(S["x_area_free"], 1)
            gp.dma_start(x_res[:, :, :], x_in.rearrange("(t p) d -> p t d", p=P)).then_inc(S["x_landed"], 16)

            gp.wait_ge(S["tile_free"], T_END1)
            gp.dma_start(x2_d.rearrange("(t p) d -> p t d", p=P), x_res[:, :, :]).then_inc(S["x2_stored"], 16)
            gp.wait_ge(S["norm_turned"], KT * 3)
            for i, dst in enumerate((gain_qa, gain_ka, gain_qb, gain_kb)):
                d = dst.shape[1]
                gp.dma_start(dst[:, :], wide_gains[i:i + 1, 0:d].broadcast_to([P, d])).then_inc(S["wide_landed"], 16)
            gp.wait_ge(S["tile_free"], T_K + 4)
            gp.tensor_copy(k_b2[:, :, :], t_k[:, :, 0:128]).then_inc(S["kv_b"], 1)
            gp.tensor_copy(v_b2[:, :, :], t_k[:, :, 128:256]).then_inc(S["kv_b"], 1)
            gp.wait_ge(S["wide_landed"], 64)
            for t in range(TB):
                gp.wait_ge(S["c_scaled"], P_A + 2 * t + 2)
                gp.tensor_tensor(k_a3[:, t:t + 1], k_a3[:, t:t + 1],
                                 gain_ka[:, None, None, :].broadcast_to([P, 1, HEADS, QK_M]), ALU.mult)\
                    .then_inc(S["ka_gained"], 1)
            for kind, (q, k, v, d) in enumerate(((q_a2, k_a2, v_a2, QK_M), (q_b2, k_b2, v_b2, D_D))):
                for hd in range(HEADS):
                    u, B = hd % 2, 4 * kind + hd // 2
                    if hd == 0 and kind == 0:
                        gp.wait_ge(S["rope"], 6 * 11)
                        gp.wait_ge(S["kv_b"], 2)
                        gp.wait_ge(S["qi_sb"], 3)
                    if hd == 0 and kind == 1:
                        gp.wait_ge(S["rope"], 6 * 15)
                    if B:
                        gp.wait_ge(S[f"p_turned{u}"], B)
                    kh = hd if kind == 0 else hd // (HEADS // KV_D)
                    gp.tensor_copy(q_st[u][:, :, 0:d], q[:, :, hd * d:(hd + 1) * d]).then_inc(S[f"staged{u}"], 1)
                    gp.tensor_copy(k_st[u][:, :, 0:d], k[:, :, kh * d:(kh + 1) * d]).then_inc(S[f"staged{u}"], 1)
                    if hd == 1 and kind == 0:
                        gp.wait_ge(S["idx_done"], 1)
                        for i in range(TB):
                            x = idx[:, LOW[i] + P * i:LOW[i] + P * (i + 1)]
                            gp.affine_select(out=x, in_=x, compare_op=ALU.is_ge, fill=NEG, base=0,
                                             pattern=[[-1, P]], channel_multiplier=1).then_inc(S["idx_causal"], 1)
                        gp.wait_ge(S["rope"], 6 * 15)
                        gp.memset(causal[:, :], 0.0).then_inc(S["causal0"], 1)
                        gp.wait_ge(S["causal0"], 1)
                        gp.affine_select(out=causal[:, 384:512], in_=causal[:, 384:512], compare_op=ALU.is_ge, fill=NEG,
                                         base=0, pattern=[[-1, P]], channel_multiplier=1).then_inc(S["causal_made"], 1)
                    if B:
                        gp.wait_ge(S[f"pv{u}"], B)
                    if kind == 0:
                        gp.tensor_copy(v_st[u][:, :, :], v[:, :, P * (hd // 2):P * (hd // 2 + 1)]).then_inc(S[f"v_staged{u}"], 2)
                    else:
                        for w in range(2):
                            gp.tensor_copy(v_st[u][:, :, D_D * w:D_D * (w + 1)], v[:, :, kh * D_D:(kh + 1) * D_D])\
                                .then_inc(S[f"v_staged{u}"], 1)
            gp.wait_ge(S["o_stored"], 16 * 9)
            gp.wait_ge(S["pT_sb0"], 8)
            gp.wait_ge(S["pT_sb1"], 8)
            gp.dma_start(o_all[:, :, :], o_d.rearrange("k p n -> p k n")).then_inc(S["o_landed"], 16)
            gp.wait_ge(S["gates_stored0"], 16 * 13)
            gp.wait_ge(S["gates_stored1"], 16 * 13)
            gp.dma_start(g_all[:, :, :], gates_d[0:KT].rearrange("k p n -> p k n")).then_inc(S["g_landed"], 16)
            gp.dma_start(m_all[:, :, :], gates_d[KT:3 * KT].rearrange("k p n -> p k n")).then_inc(S["m_landed"], 16)
            gp.dma_start(x_fin[:, :, :], x2_d.rearrange("(t p) d -> p t d", p=P)).then_inc(S["x2_landed"], 16)

        @block.scalar
        def _(act):
            a = nc.scalar
            x_tiles = x_in.rearrange("(t p) d -> p t d", p=P)
            for t in range(TB):
                a.dma_start(x_res[:, t], x_tiles[:, t]).then_inc(S[f"x_first{t}"], 16)
            for i, name in enumerate(("o_stored", "gates_stored0", "gates_stored1")):
                a.dma_start(tick[:, 24 + 3 * i:27 + 3 * i], c_gains).then_inc(S[name], 16)
            a.preload_act_table_set("natural_log_exp_and_others")
            a.wait_ge(S["consts"], 7)
            for t in range(TB):
                a.wait_ge(S[f"x_first{t}"], 16)
                norm_rstd(0, t)
            for hf in (0, 1):
                split_hi(0, 0, hf, first=True)
            for u in range(2):
                a.activation(mx[:, u, 0:1], eps[:, :], ACT.Copy).then_inc(S[f"o_sb{u}"], 1)
            a.wait_ge(S["par_landed"], 128)
            for k in range(KT):
                norm_hi(0, k)
            for hf in (0, 1):
                split_hi(1, 1, hf, first=True)
            a.wait_ge(S["tile_made"], 1)
            a.activation(g_i[:, :], proj[0:HEADS, 0], ACT.Identity, bias=bif[:, 0:1]).then_inc(S["tile_free"], 1)
            a.wait_ge(S["tile_made"], 2)
            a.activation(g_f[:, :], proj[0:HEADS, 1], ACT.Identity, bias=bif[:, 1:2]).then_inc(S["tile_free"], 1)
            a.wait_ge(S["tile_free"], 2)
            a.activation(g_abs[:, :], g_f[:, :], ACT.Abs).then_inc(S["rows_act"], 1)
            a.wait_ge(S["rows_act"], 1)
            a.activation(g_abs[:, :], g_abs[:, :], ACT.Exp, scale=-1.0).then_inc(S["rows_act"], 1)
            a.wait_ge(S["rows_act"], 2)
            a.activation(g_abs[:, :], g_abs[:, :], ACT.Ln, bias=1.0).then_inc(S["rows_act"], 1)
            a.wait_ge(S["angles"], len(ANGLES))
            a.activation(sine[:, :, :], A3, ACT.Sin).then_inc(S["rope_tables"], 1)
            a.activation(cosine[:, :, :], C3, ACT.Sin).then_inc(S["rope_tables"], 1)
            a.preload_act_table_set("natural_log_exp_and_others")
            a.wait_ge(S["rows_m"], 1)
            a.activation(g_out[:, 1, :], g_m[:, :], ACT.Exp, scale=-1.0).then_inc(S["rows_act"], 1)
            a.wait_ge(S["rows_stored"], 16)
            with a.Fori(0, HEADS) as h:
                n = T_HEADS + 8 * h
                ga = G_HEADS + 2 * h
                a.preload_act_table_set("natural_log_exp_and_others")
                split_hi(ga + 1, 0, 0)
                for j, (raw, sq) in enumerate(((q_b, sq_q), (k_b, sq_k))):
                    a.wait_ge(S["tile_made"], n + j + 1)
                    a.wait_ge(S["head_done"], h + 1)
                    a.activation(raw[:, :], proj[:, j], ACT.Copy).then_inc(S["qk_raw"], 1)
                    a.activation(sq[:, :], proj[:, j], ACT.Square).then_inc(S["tile_free"], 1)
                split_hi(ga + 1, 0, 1)
                a.wait_ge(S["tile_made"], n + 3)
                a.wait_ge(S["head_done"], h + 1)
                a.activation(qk_pad[:, 3:3 + SEQ], proj[:, 0], ACT.Copy).then_inc(S["tile_free"], 1)
                for j, sq in enumerate((sq_q, sq_k)):
                    a.wait_ge(S["ssq_made"], 2 * h + j + 1)
                    a.activation(sq[:, :], pa[:, 512 * j:512 * (j + 1)], ACT.Ln, bias=eps[:, 0:1]).then_inc(S["rms_ln"], 1)
                    a.wait_ge(S["rms_ln"], 2 * h + j + 1)
                    a.activation(sq[:, :], sq[:, :], ACT.Exp, scale=-0.5).then_inc(S["rms_b"], 1)
                a.wait_ge(S["tile_made"], n + 4)
                a.activation(v_bT[:, :], proj[:, 1], ACT.Copy).then_inc(S["tile_free"], 1)
                split_hi(ga + 2, 1, 0)
                a.wait_ge(S["z_made"], h + 1)
                a.activation(z[:, :], pa[:, 0:TRI_COLS], ACT.Copy, scale=HD_B ** -0.5).then_inc(S["z_sb"], 1)
                a.wait_ge(S["z_sb"], h + 1)
                a.wait_ge(S["conv"], 4 * h + 4)
                a.activation(sp[:, :], z[:, :], ACT.Abs).then_inc(S["sp_abs"], 1)
                a.wait_ge(S["sp_abs"], h + 1)
                a.activation(sp[:, :], sp[:, :], ACT.Exp, scale=-1.0).then_inc(S["sp_exp"], 1)
                a.wait_ge(S["sp_exp"], h + 1)
                a.activation(sp[:, :], sp[:, :], ACT.Ln, bias=1.0).then_inc(S["sp_ln"], 1)
                a.wait_ge(S["tile_made"], n + 5)
                a.activation(v_aT[:, :], proj[:, 0], ACT.Copy).then_inc(S["tile_free"], 1)
                a.activation(silu[:, :], conv[:, :], ACT.Sigmoid).then_inc(S["silu_sig"], 1)
                a.preload_act_table_set("natural_log_exp_and_others")
                a.wait_ge(S["v_turned"], h + 1)
                a.activation(v_b[:, :], pm[:, 0:512], ACT.Copy).then_inc(S["v_sb"], 1)
                a.activation(v_a[:, :], pm[:, 512:1024], ACT.Copy).then_inc(S["v_sb"], 1)
                split_hi(ga + 2, 1, 1)
                a.wait_ge(S["tile_made"], n + 6)
                a.activation(gate_o[:, :], proj[:, 1], ACT.Copy).then_inc(S["tile_free"], 1)
                a.wait_ge(S["arg_a"], 4 * h + 4)
                a.activation(decay[:, :], decay[:, :], ACT.Exp).then_inc(S["decay_exp"], 1)
                a.wait_ge(S["tile_made"], n + 7)
                a.activation(gate_a[:, :], proj[:, 0], ACT.Copy).then_inc(S["tile_free"], 1)
                a.wait_ge(S["arg_b_masked"], 4 * h + 4)
                a.activation(z[:, :], z[:, :], ACT.Exp).then_inc(S["a_b"], 1)
                a.wait_ge(S["num_made"], h + 1)
                a.activation(num2[:, :], pm[:, 0:512], ACT.Square).then_inc(S["num_sq"], 1)
                a.activation(den[:, :], pm[:, 512:1024], ACT.Abs).then_inc(S["den_abs"], 1)
                a.wait_ge(S["var_a"], h + 1)
                a.activation(scl[:, :], scl[:, :], ACT.Ln).then_inc(S["var_ln"], 1)
                a.wait_ge(S["var_ln"], h + 1)
                a.activation(scl[:, :], scl[:, :], ACT.Exp, scale=-0.5).then_inc(S["rms_a"], 1)
                a.wait_ge(S["tile_free"], n + 7)
                a.activation(gate_o[:, :], gate_o[:, :], ACT.Sigmoid).then_inc(S["gate_sig"], 1)
                a.activation(gate_a[:, :], gate_a[:, :], ACT.Sigmoid, bias=par[:, 5:6]).then_inc(S["gate_sig"], 1)
                a.wait_ge(S["tile_made"], n + 8)
                a.activation(gate_b[:, :], proj[:, 1], ACT.Sigmoid, bias=par[:, 6:7]).then_inc(S["tile_free"], 1)
            a.preload_act_table_set("natural_log_exp_and_others")
            for g in range(G_OUT, G_MLP):
                for hf in (0, 1):
                    split_hi(g + 1, (g + 1) % 2, hf)
            for t in range(TB):
                a.wait_ge(S["tile_free"], T_MLP - TB + t + 1)
                norm_rstd(1, t)
            for k in range(KT):
                norm_hi(1, k)
            with a.Fori(0, CHUNKS) as c:
                g = G_MLP + 4 * c
                n = T_MLP + 16 * c
                for gg in range(2):
                    split_hi(g + gg + 1, gg % 2, 0)
                    for j in range(4):
                        i = 4 * gg + j
                        a.wait_ge(S["tile_made"], n + i + 1)
                        if i == 0:
                            a.wait_ge(S["tile_free"], n)
                        if i >= 2:
                            a.wait_ge(S["a_lo_done"], 8 * c + i - 1)
                        a.activation(relu[:, i % 2], proj[:, i % 2], ACT.Relu).then_inc(S["tile_free"], 1)
                        a.wait_ge(S["tile_free"], n + i + 1)
                        a.activation(act_hi[:, i], relu[:, i % 2], ACT.Square).then_inc(S["a_hi_done"], 1)
                        if j == 1:
                            split_hi(g + gg + 1, gg % 2, 1)
                for gg in range(2, 4):
                    for hf in (0, 1):
                        split_hi(g + gg + 1, gg % 2, hf)
            a.preload_act_table_set("natural_log_exp_and_others")
            for t in range(TB):
                a.wait_ge(S["tile_free"], T_END1 - TB + t + 1)
                norm_rstd(2, t)
            for k in range(KT):
                norm_hi(2, k)

            def evac(n, dst, src=None, wait=None):
                a.wait_ge(S["tile_made"], n + 1)
                a.activation(dst, proj[:, n % 2, 0:512] if src is None else src, ACT.Copy).then_inc(S["tile_free"], 1)

            def split(g):
                for hf in (0, 1):
                    split_hi(g, g % 2, hf)

            def square(p):
                x, T, h, d = PIECES[p]
                if p >= 2:
                    a.wait_ge(S["c_summed"], p - 1)
                o = squares[p % 2][:, 0:T * h * d]
                a.activation(o.rearrange("p (t h d) -> p t h d", t=T, h=h), x, ACT.Square).then_inc(S["c_squared"], 1)

            def root(p):
                x, T, h, d = PIECES[p]
                r = c_ss[:, p, 0:T * h]
                a.wait_ge(S["c_summed"], p + 1)
                a.activation(r, r, ACT.Ln, bias=eps[:, 0:1], scale=1.0 / d).then_inc(S["c_ln"], 1)
                a.wait_ge(S["c_ln"], p + 1)
                a.activation(r, r, ACT.Exp, scale=-0.5).then_inc(S["c_root"], 1)

            split(G_K)
            a.wait_ge(S["x2_stored"], 16)
            for t in range(TB):
                evac(T_C + t, t_c[:, t])
                a.wait_ge(S["tile_free"], T_C + t + 1)
                for p in (2 * t, 2 * t + 1):
                    square(p)
                for p in (2 * t, 2 * t + 1):
                    root(p)
            evac(T_K, t_k[:, 0])
            split(G_U)
            evac(T_K + 1, t_k[:, 1])
            for m in range(3):
                a.wait_ge(S["c_turned"], m + 1)
                dst = cq_hi[:, m] if m < 2 else ckv_hi[:, 0]
                a.activation(dst, pa[:, 512 * m:512 * (m + 1)], ACT.Copy, scale=c_gain[:, m:m + 1]).then_inc(S["c_hi"], 1)
            evac(T_K + 2, t_k[:, 2])
            evac(T_K + 3, t_k[:, 3])
            a.wait_ge(S["kv_b"], 1)
            square(P_KB)
            split(G_Q)
            root(P_KB)
            a.wait_ge(S["k_pe_spread"], 1)
            for t in range(TB):
                n = T_U + 4 * t
                evac(n, q_a2[:, t, 0:512])
                a.wait_ge(S["tile_made"], n + 2)
                a.activation(q_a2[:, t, 512:768], proj[:, 1, 0:256], ACT.Copy).then_inc(S["tile_free"], 1)
                a.wait_ge(S["tile_made"], n + 3)
                a.activation(k_a3[:, t, :, 0:NOPE], proj[:, 0].rearrange("p (h d) -> p h d", h=HEADS), ACT.Copy)\
                    .then_inc(S["tile_free"], 1)
                evac(n + 3, v_a2[:, t])
                a.wait_ge(S["tile_free"], n + 4)
                for p in (P_A + 2 * t, P_A + 2 * t + 1):
                    square(p)
                    if t:
                        root(p - 2)
            for hf in (0, 1):
                split_hi(G_L, G_L % 2, hf, used=T_Q)
            for p in (P_QB - 2, P_QB - 1):
                root(p)
            evac(T_Q, q_b2[:, 0])
            a.wait_ge(S["ki_turned"], 1)
            a.activation(t_c[:, :, 256:384], pa[:, 0:512].rearrange("p (t n) -> p t n", t=TB), ACT.Copy).then_inc(S["qi_sb"], 1)
            a.wait_ge(S["qi_turned"], 1)
            for g in range(2):
                a.activation(t_c[:, :, P * g:P * (g + 1)], pm[:, 512 * g:512 * (g + 1)].rearrange("p (t n) -> p t n", t=TB),
                             ACT.Copy).then_inc(S["qi_sb"], 1)
            evac(T_Q + 1, q_b2[:, 1])
            for h in range(HEADS):
                if h in (2, 4):
                    evac(T_Q + 1 + h // 2, q_b2[:, 1 + h // 2])
                a.wait_ge(S["idx_made"], h + 1)
                if h >= 2:
                    a.wait_ge(S["idx_sum"], 4 * (h - 1))
                a.activation(rel[h % 2][:, :], (pm if h % 2 else pa)[:, 0:TRI_COLS], ACT.Relu).then_inc(S["idx_relu"], 1)
                if h >= 4:
                    if h > 4:
                        root(P_QB + h - 5)
                    a.wait_ge(S["tile_free"], T_L)
                    square(P_QB + h - 4)
            root(P_QB + 3)

            a.wait_ge(S["idx_done"], 1)
            a.wait_ge(S["idx_causal"], 4)

            def head_turns(u, B, d):
                X = (pa, pm)[u]
                a.wait_ge(S[f"qk_turned{u}"], B + 1)
                a.activation(qT[u][0:d, :], X[0:d, 0:512], ACT.Copy).then_inc(S[f"qk_sb{u}"], 1)
                a.activation(kT[u][0:d, :], X[0:d, 512:1024], ACT.Copy).then_inc(S[f"qk_sb{u}"], 1)

            def head_exp(u, B):
                a.wait_ge(S[f"nmax{u}"], B + 1)
                for i in range(TB):
                    x = p_sb[u][:, LOW[i]:LOW[i] + P * (i + 1)]
                    a.activation(x, x, ACT.Exp, bias=mx[:, u, i:i + 1], accum_out=row_sum[:, u, i:i + 1])\
                        .then_inc(S[f"p_exp{u}"], 1)

            def head_pT(u, B):
                X = (pa, pm)[u]
                a.wait_ge(S[f"p_turned{u}"], B + 1)
                a.activation(pT[u][:, :], X[:, 0:TRI_COLS], ACT.Copy).then_inc(S[f"pT_sb{u}"], 1)

            def head_out(u, B):
                X = (pa, pm)[u]
                a.wait_ge(S[f"pv{u}"], B + 1)
                if u == 0:
                    a.wait_ge(S["o_stored"], 16 * B + 16)
                a.activation(o_st[D_D * u:D_D * (u + 1), :], X[D_D * u:D_D * (u + 1), 0:512], ACT.Copy).then_inc(S[f"o_sb{u}"], 1)

            def gate(c, s, i):
                n = T_L + 6 * c + 3 * s + i
                q = (s + i) % 2
                a.wait_ge(S["tile_made"], n + 1)
                a.wait_ge(S[f"gates_stored{q}"], 16 * (3 * c + (3 * s + i) // 2) + 16)
                a.activation(gate_st[:, q], proj[:, q], ACT.Copy).then_inc(S["tile_free"], 1)
                a.wait_ge(S["tile_free"], n + 1)
                a.dma_start(gates_d[bass.ds(n - T_L, 1)].rearrange("a p n -> p (a n)"), gate_st[:, q])\
                    .then_inc(S[f"gates_stored{q}"], 16)

            for kind, d in enumerate((QK_M, D_D)):
                with a.Fori(0, 2) as b:
                    for s in range(2):
                        c = 2 * kind + b
                        B = 2 * c + s
                        split_hi(G_L + B + 1, s, 0, used=T_L + 3 * B)
                        head_turns(0, B, d)
                        head_turns(1, B, d)
                        gate(c, s, 0)
                        head_exp(0, B)
                        split_hi(G_L + B + 1, s, 1, used=T_L + 3 * B)
                        head_exp(1, B)
                        gate(c, s, 1)
                        head_pT(0, B)
                        head_pT(1, B)
                        gate(c, s, 2)
                        head_out(0, B)
                        head_out(1, B)
                        a.wait_ge(S["o_sb0"], B + 2)
                        a.wait_ge(S["o_sb1"], B + 2)
                        a.dma_start(o_d[bass.ds(B, 1)].rearrange("a p n -> p (a n)"), o_st[:, :]).then_inc(S["o_stored"], 16)
            for hf in (0, 1):
                split_hi(G_BR + 1, 0, hf, used=T_BR)
            for kind in range(2):
                ks = slice(4 * kind, 4 * kind + 4)
                a.wait_ge(S["o_times_g"], kind + 1)
                a.wait_ge(S["tile_free"], T_BR)
                a.activation(g_all[:, ks], g_all[:, ks], ACT.Sigmoid).then_inc(S["g_sig"], 1)
            for kind in range(2):
                ks = slice(4 * kind, 4 * kind + 4)
                a.wait_ge(S["o_gated"], kind + 1)
                a.activation(h_hi[:, ks], o_all[:, ks], ACT.Copy).then_inc(S["oh_hi"], 1)
            a.wait_ge(S["m_landed"], 16)
            for j in range(2 * KT):
                a.activation(m_all[:, j], m_all[:, j], ACT.Sigmoid, bias=merge_bias[:, j:j + 1]).then_inc(S["m_sig"], 1)
            for hf in (0, 1):
                split_hi(G_FIN, 1, hf, used=T_BR + 8)
            for j in range(KT):
                a.wait_ge(S["merged"], j + 1)
                a.activation(mg_hi[:, j], m_all[:, KT + j], ACT.Copy).then_inc(S["mg_hi"], 1)
            for hf in (0, 1):
                split_hi(G_FIN + 1, 0, hf, used=T_BR + 16)

        @block.vector
        def _(dve):
            v = nc.vector
            v.memset(tick[:, 0:1], 0.0).then_inc(S["head_done"], 1)
            v.memset(tick[:, 1:2], 0.0).then_inc(S["top_out"], 1)
            v.memset(tick[:, 2:3], 0.0).then_inc(S["pad_zero"], 1)
            for t in range(TB):
                v.wait_ge(S[f"x_first{t}"], 16)
                norm_scale(0, t)
            split_lo(0, 0, 0)
            split_lo(0, 0, 1)
            v.wait_ge(S["par_landed"], 128)
            for k in range(KT):
                norm_lo(0, k)
            for hf in (0, 1):
                split_lo(1, 1, hf)
            for i, (dst, op) in enumerate(ANGLES):
                if i:
                    v.wait_ge(S["angles"], i)
                op(v).then_inc(S["angles"], 1)
            v.wait_ge(S["rows_act"], 3)
            v.scalar_tensor_tensor(g_ls[:, :], g_f[:, :], 0.0, g_abs[:, :], ALU.min, ALU.subtract).then_inc(S["rows_dve"], 1)
            v.wait_ge(S["rows_dve"], 1)
            v.tensor_tensor_scan(g_F[:, :], one_row[:, :], g_ls[:, :], 0.0, ALU.mult, ALU.add).then_inc(S["rows_dve"], 1)
            v.wait_ge(S["rows_dve"], 2)
            v.tensor_tensor(g_a[:, :], g_i[:, :], g_F[:, :], ALU.subtract).then_inc(S["rows_a"], 1)
            v.wait_ge(S["rows_a"], 1)
            v.tensor_tensor_scan(g_G[:, :], g_a[:, :], g_a[:, :], 0.0, ALU.max, ALU.max).then_inc(S["rows_dve"], 1)
            v.wait_ge(S["rows_dve"], 3)
            v.tensor_tensor(g_m[:, :], g_F[:, :], g_G[:, :], ALU.add).then_inc(S["rows_m"], 1)
            v.wait_ge(S["rows_act"], 4)
            v.tensor_scalar(g_out[:, 0, :], g_G[:, :], -1.0, None, ALU.mult).then_inc(S["rows_ready"], 1)
            v.wait_ge(S["a_turned"], 1)
            v.tensor_copy(a_col[:, :, :], pm[:, 0:TB * HEADS].rearrange("p (t h) -> p t h", h=HEADS)).then_inc(S["a_col"], 1)
            v.wait_ge(S["a_col"], 1)
            with v.Fori(0, HEADS) as h:
                ga = G_HEADS + 2 * h
                v.wait_ge(S["head_done"], h + 1)
                v.tensor_copy(par[:, :], hp[:, bass.ds(h, 1), :].rearrange("p a n -> p (a n)")).then_inc(S["par_head"], 1)
                v.tensor_copy(col[:, :], a_col[:, :, bass.ds(h, 1)].rearrange("p t a -> p (t a)")).then_inc(S["par_head"], 1)
                v.memset(qk_pad[:, 0:3], 0.0).then_inc(S["pad_zero"], 1)
                split_lo(ga + 1, 0, 0)
                split_lo(ga + 1, 0, 1)
                for j, (raw, r) in enumerate(((q_b, sq_q), (k_b, sq_k))):
                    v.wait_ge(S["rms_b"], 2 * h + j + 1)
                    v.scalar_tensor_tensor(raw[:, :], raw[:, :], sbg[:, j:j + 1], r[:, :], ALU.mult, ALU.mult)\
                        .then_inc(S["qk_normed"], 1)
                v.wait_ge(S["par_head"], 2 * h + 2)
                v.wait_ge(S["pad_zero"], h + 2)
                v.wait_ge(S["tile_free"], T_HEADS + 8 * h + 3)
                v.tensor_scalar(conv[:, :], qk_pad[:, 0:SEQ], par[:, 0:1], None, ALU.mult).then_inc(S["conv"], 1)
                for j in range(1, 4):
                    v.wait_ge(S["conv"], 4 * h + j)
                    v.scalar_tensor_tensor(conv[:, :], qk_pad[:, j:j + SEQ], par[:, j:j + 1], conv[:, :],
                                           ALU.mult, ALU.add).then_inc(S["conv"], 1)
                split_lo(ga + 2, 1, 0)
                v.wait_ge(S["bc_landed"], 16 * h + 16)
                for i in range(TB):
                    v.tensor_scalar(decay[:, TRI[i]:TRI[i] + SEQ - P * i], bc[:, 0, P * i:], col[:, i:i + 1], 0.0,
                                    ALU.add, ALU.min).then_inc(S["arg_a"], 1)
                v.wait_ge(S["sp_ln"], h + 1)
                v.scalar_tensor_tensor(sp[:, :], z[:, :], 0.0, sp[:, :], ALU.max, ALU.add).then_inc(S["sp_done"], 1)
                v.wait_ge(S["silu_sig"], h + 1)
                v.tensor_tensor(silu[:, :], silu[:, :], conv[:, :], ALU.mult).then_inc(S["silu_done"], 1)
                v.wait_ge(S["sp_masked"], 4 * h + 4)
                v.tensor_copy(sp_hi[:, :], sp[:, :]).then_inc(S["sp_hi"], 1)
                v.wait_ge(S["sp_hi"], h + 1)
                v.tensor_tensor(sp_lo[:, :], sp[:, :], sp_hi[:, :], ALU.subtract).then_inc(S["sp_lo"], 1)
                split_lo(ga + 2, 1, 1)
                v.wait_ge(S["s_made"], h + 1)
                v.wait_ge(S["decay_exp"], h + 1)
                v.scalar_tensor_tensor(decay[:, :], pm[:, 0:TRI_COLS], DQK_A ** -0.5, decay[:, :], ALU.mult, ALU.mult)\
                    .then_inc(S["p_done"], 1)
                v.wait_ge(S["c_made"], h + 1)
                v.tensor_tensor(z[:, :], z[:, :], pa[:, 0:TRI_COLS], ALU.subtract).then_inc(S["arg_b_done"], 1)
                v.wait_ge(S["den_abs"], h + 1)
                v.tensor_tensor(den[:, :], den[:, :], bc[:, 1, :], ALU.max).then_inc(S["den_max"], 1)
                v.wait_ge(S["den_max"], h + 1)
                v.tensor_tensor(den[:, :], den[:, :], den[:, :], ALU.mult).then_inc(S["den_sq"], 1)
                v.wait_ge(S["den_sq"], h + 1)
                v.wait_ge(S["num_ssq"], h + 1)
                v.scalar_tensor_tensor(scl[:, :], den[:, :], EPS, pm[:, 1024:1536], ALU.mult, ALU.add).then_inc(S["var_a"], 1)
                v.wait_ge(S["rms_a"], h + 1)
                v.scalar_tensor_tensor(scl[:, :], pm[:, 0:512], par[:, 4:5], scl[:, :], ALU.mult, ALU.mult).then_inc(S["y"], 1)
                v.wait_ge(S["gate_sig"], 2 * h + 1)
                v.wait_ge(S["y"], 5 * h + 1)
                v.tensor_tensor(scl[:, :], scl[:, :], gate_o[:, :], ALU.mult).then_inc(S["y"], 1)
                v.wait_ge(S["gate_sig"], 2 * h + 2)
                v.wait_ge(S["y"], 5 * h + 2)
                v.tensor_tensor(scl[:, :], scl[:, :], gate_a[:, :], ALU.mult).then_inc(S["y"], 1)
                v.wait_ge(S["pv_b_made"], h + 1)
                v.wait_ge(S["tile_free"], T_HEADS + 8 * h + 8)
                v.tensor_tensor(gate_b[:, :], pa[:, 0:512], gate_b[:, :], ALU.mult).then_inc(S["y"], 1)
                v.wait_ge(S["y"], 5 * h + 4)
                v.tensor_tensor(scl[:, :], scl[:, :], gate_b[:, :], ALU.add).then_inc(S["y"], 1)
                v.wait_ge(S["y"], 5 * h + 5)
                yh = y_hi[:, bass.ds(h, 1), :].rearrange("p a n -> p (a n)")
                v.tensor_copy(yh, scl[:, :]).then_inc(S["y_hi"], 1)
                v.wait_ge(S["y_hi"], h + 1)
                v.tensor_tensor(y_lo[:, bass.ds(h, 1), :].rearrange("p a n -> p (a n)"), scl[:, :], yh, ALU.subtract)\
                    .then_inc(S["head_done"], 1)
            v.wait_ge(S["head_done"], HEADS + 1)
            v.memset(eps[:, :], EPS).then_inc(S["x_area_free"], 1)
            for g in range(G_OUT, G_MLP):
                for hf in (0, 1):
                    split_lo(g + 1, (g + 1) % 2, hf)
                for t in range(TB):
                    n = T_OUT + 4 * (g - G_OUT) + t
                    v.wait_ge(S["x_landed"], 16)
                    v.wait_ge(S["tile_free"], n)
                    v.wait_ge(S["tile_made"], n + 1)
                    xx = x_res[:, t, 512 * (g - G_OUT):512 * (g - G_OUT + 1)]
                    v.tensor_tensor(xx, xx, proj[:, t % 2], ALU.add).then_inc(S["tile_free"], 1)
                    if g == G_MLP - 1:
                        norm_scale(1, t)
            for k in range(KT):
                norm_lo(1, k)
            with v.Fori(0, CHUNKS) as c:
                g = G_MLP + 4 * c
                n = T_MLP + 16 * c
                for gg in range(2):
                    split_lo(g + gg + 1, gg % 2, 0)
                    for j in range(4):
                        i = 4 * gg + j
                        v.wait_ge(S["tile_free"], n + i + 1)
                        v.tensor_tensor(relu_sq[:, i % 2], relu[:, i % 2], relu[:, i % 2], ALU.mult).then_inc(S["a_sq"], 1)
                        v.wait_ge(S["a_hi_done"], 8 * c + i + 1)
                        v.wait_ge(S["a_sq"], 8 * c + i + 1)
                        v.tensor_tensor(act_lo[:, i], relu_sq[:, i % 2], act_hi[:, i], ALU.subtract).then_inc(S["a_lo_done"], 1)
                        if j == 1:
                            split_lo(g + gg + 1, gg % 2, 1)
                for gg in range(2, 4):
                    for hf in (0, 1):
                        split_lo(g + gg + 1, gg % 2, hf)
                    for t in range(TB):
                        i = 4 * gg + t
                        v.wait_ge(S["tile_free"], n + i)
                        v.wait_ge(S["tile_made"], n + i + 1)
                        xx = x_res[:, t, 512 * (gg - 2):512 * (gg - 1)]
                        v.tensor_tensor(xx, xx, proj[:, t % 2], ALU.add).then_inc(S["tile_free"], 1)
            for t in range(TB):
                norm_scale(2, t)
            for k in range(KT):
                norm_lo(2, k)

            def norm_sum(p):
                x, T, h, d = PIECES[p]
                v.wait_ge(S["c_squared"], p + 1)
                v.tensor_reduce(c_ss[:, p, 0:T * h], squares[p % 2][:, 0:T * h * d].rearrange("p (r d) -> p r d", d=d),
                                AX.X, ALU.add).then_inc(S["c_summed"], 1)

            def norm_mult(p):
                x, T, h, d = PIECES[p]
                v.wait_ge(S["c_root"], p + 1)
                r = c_ss[:, p, 0:T * h].rearrange("p (t h) -> p t h", t=T)[:, :, :, None].broadcast_to([P, T, h, d])
                v.tensor_tensor(x, x, r, ALU.mult).then_inc(S["c_scaled"], 1)

            def norm_gain(p, row):
                x, T, h, d = PIECES[p]
                v.wait_ge(S["c_scaled"], p + 1)
                v.tensor_tensor(x, x, row[:, None, None, :].broadcast_to([P, T, h, d]), ALU.mult).then_inc(S["c_gained"], 1)

            rope_n = [0]

            def rope(x, h, o, half, f0, tiles=slice(0, TB)):
                x1, x2 = x[:, :, :, o:o + half], x[:, :, :, o + half:o + 2 * half]
                T = tiles.stop - tiles.start
                c, s_ = [b[:, tiles, None, f0:f0 + half].broadcast_to([P, T, h, half]) for b in (cosine, sine)]
                A_, B_, C_, D_ = [b[:, 0:T * h * half].rearrange("p (t h d) -> p t h d", t=T, h=h) for b in (ra, rb, rc, rd)]
                if rope_n[0]:
                    v.wait_ge(S["rope"], 6 * rope_n[0])
                for dst, xx, w in ((A_, x1, c), (B_, x2, s_), (C_, x2, c), (D_, x1, s_)):
                    v.tensor_tensor(dst, xx, w, ALU.mult).then_inc(S["rope"], 1)
                v.wait_ge(S["rope"], 6 * rope_n[0] + 4)
                v.tensor_tensor(x1, A_, B_, ALU.subtract).then_inc(S["rope"], 1)
                v.tensor_tensor(x2, C_, D_, ALU.add).then_inc(S["rope"], 1)
                rope_n[0] += 1

            def split(g):
                for hf in (0, 1):
                    split_lo(g, g % 2, hf)

            split(G_K)
            for t in range(TB):
                for p in (2 * t, 2 * t + 1):
                    norm_sum(p)
                for p in (2 * t, 2 * t + 1):
                    norm_mult(p)
            v.tensor_copy(k_a3[:, :, :, NOPE:QK_M], t_c[:, :, None, 384:416].broadcast_to([P, TB, HEADS, 32]))\
                .then_inc(S["k_pe_spread"], 1)
            split(G_U)
            for m in range(3):
                v.wait_ge(S["c_hi"], m + 1)
                dst, hi = (cq_lo[:, m], cq_hi[:, m]) if m < 2 else (ckv_lo[:, 0], ckv_hi[:, 0])
                v.scalar_tensor_tensor(dst, pa[:, 512 * m:512 * (m + 1)], c_gain[:, m:m + 1], hi, ALU.mult, ALU.subtract)\
                    .then_inc(S["c_lo"], 1)
            ki = t_c[:, :, 416:448].rearrange("p t (h d) -> p t h d", h=1)
            rope(ki, 1, 0, 4, 24)
            v.tensor_scalar(w_idx[:, :, :], t_c[:, :, 448:456], (HEADS ** -0.5) * (IDX_D ** -0.5), None, ALU.mult)\
                .then_inc(S["w_idx"], 1)
            v.wait_ge(S["wide_landed"], 64)
            norm_sum(P_KB)
            v.wait_ge(S["rope"], 6)
            v.wait_ge(S["kv_b"], 2)
            v.tensor_copy(t_k[:, :, 0:P].rearrange("p t (r d) -> p t r d", d=IDX_D),
                          t_c[:, :, None, 416:448].broadcast_to([P, TB, P // IDX_D, IDX_D])).then_inc(S["ki_spread"], 1)
            qi = t_k[:, :, 256:512].rearrange("p t (h d) -> p t h d", h=HEADS)
            rope(qi, HEADS, 0, 4, 24)
            split(G_Q)
            norm_mult(P_KB)
            norm_gain(P_KB, gain_kb)
            v.wait_ge(S["c_gained"], 1)
            rope(k_b3, KV_D, 0, 8, 16)
            for p in range(P_A, P_QB):
                norm_sum(p)
            for p in range(P_A, P_QB):
                norm_mult(p)
            for p in range(P_A, P_QB, 2):
                norm_gain(p, gain_qa)
            split(G_L)
            for t in range(TB):
                v.wait_ge(S["c_gained"], 2 + t)
                rope(q_a3[:, t:t + 1], HEADS, NOPE, 16, 0, slice(t, t + 1))
                v.wait_ge(S["ka_gained"], t + 1)
                rope(k_a3[:, t:t + 1], HEADS, NOPE, 16, 0, slice(t, t + 1))
            v.wait_ge(S["w_idx"], 1)
            for h in range(HEADS):
                v.wait_ge(S["idx_relu"], h + 1)
                if h:
                    v.wait_ge(S["idx_sum"], 4 * h)
                for i in range(TB):
                    c = slice(LOW[i], LOW[i] + P * (i + 1))
                    if h == 0:
                        ins = v.tensor_scalar(idx[:, c], rel[0][:, c], w_idx[:, i, 0:1], None, ALU.mult)
                    else:
                        ins = v.scalar_tensor_tensor(idx[:, c], rel[h % 2][:, c], w_idx[:, i, h:h + 1], idx[:, c],
                                                     ALU.mult, ALU.add)
                    ins.then_inc(S["idx_sum"], 1)
                if h >= 4:
                    norm_sum(P_QB + h - 4)
            v.wait_ge(S["idx_sum"], 4 * HEADS)
            v.memset(mx[:, 0, 0:1], 0.0).then_inc(S["idx_done"], 1)
            for t in range(TB):
                norm_mult(P_QB + t)
            for t in range(TB):
                norm_gain(P_QB + t, gain_qb)
            for t in range(TB):
                v.wait_ge(S["c_gained"], 6 + t)
                rope(q_b3[:, t:t + 1], HEADS, 0, 8, 16, slice(t, t + 1))
            v.wait_ge(S["idx_causal"], 4)
            v.wait_ge(S["causal_made"], 1)

            holds = [0]

            def held(value, name):
                v.wait_ge(S[name], value)
                v.memset(tick[:, holds[0]:holds[0] + 1], 0.0)
                holds[0] = holds[0] + 1

            def head_max(u, B, mask, scale):
                X = (pa, pm)[u]
                held(B + 1, f"scores{u}")
                for i in range(TB):
                    c = slice(LOW[i], LOW[i] + P * (i + 1))
                    v.tensor_tensor_reduce(p_sb[u][:, c], X[:, c], mask(i), scale, -3.0e38, ALU.add, ALU.max,
                                           mx[:, u, i:i + 1]).then_inc(S[f"smax{u}"], 1)
                v.wait_ge(S[f"smax{u}"], 4 * B + 4)
                v.tensor_scalar(mx[:, u, :], mx[:, u, :], -1.0, None, ALU.mult).then_inc(S[f"nmax{u}"], 1)

            def head_norm(u, B):
                v.wait_ge(S[f"p_exp{u}"], 4 * B + 4)
                v.reciprocal(row_sum[:, u, :], row_sum[:, u, :]).then_inc(S[f"rden{u}"], 1)
                v.wait_ge(S[f"rden{u}"], B + 1)
                for i in range(TB):
                    x = p_sb[u][:, LOW[i]:LOW[i] + P * (i + 1)]
                    v.tensor_scalar(x, x, row_sum[:, u, i:i + 1], None, ALU.mult).then_inc(S[f"p_norm{u}"], 1)

            def top(b, r):
                held(12 * b + 3 * r + 1, "top_out")
                for i in range(1, TB):
                    v.max(top8[:, i - 1, :], idx[:, LOW[i]:LOW[i] + P * (i + 1)]).then_inc(S["top_max"], 1)
                held(12 * b + 3 * r + 3, "top_max")
                for i in range(1, TB):
                    x = idx[:, LOW[i]:LOW[i] + P * (i + 1)]
                    v.match_replace(x, top8[:, i - 1, :], x, TAKEN).then_inc(S["top_out"], 1)

            for kind in range(2):
                scale = (QK_M if kind == 0 else D_D) ** -0.5
                mask = (lambda i: causal[:, 384 - P * i:512]) if kind == 0 else (lambda i: idx[:, LOW[i]:LOW[i] + P * (i + 1)])
                with v.Fori(0, 2) as b:
                    for s in range(2):
                        c = 2 * b + s
                        B = 4 * kind + c
                        split_lo(G_L + B + 1, s, 0)
                        if kind == 0:
                            top(c, 0)
                        head_max(0, B, mask, scale)
                        head_max(1, B, mask, scale)
                        split_lo(G_L + B + 1, s, 1)
                        head_norm(0, B)
                        if kind == 0:
                            top(c, 1)
                        head_norm(1, B)
                        if kind == 0:
                            top(c, 2)
                            top(c, 3)
                if kind == 0:
                    v.wait_ge(S["top_out"], 49)
                    v.tensor_copy(idx[:, LOW[0]:LOW[0] + P], causal[:, 384:512]).then_inc(S["mask"], 1)
                    for i in range(1, TB):
                        x = idx[:, LOW[i]:LOW[i] + P * (i + 1)]
                        v.tensor_scalar(x, x, TAKEN / 2, NEG, ALU.is_gt, ALU.mult).then_inc(S["mask"], 1)
                    v.wait_ge(S["mask"], 4)
            for hf in (0, 1):
                split_lo(G_BR + 1, 0, hf)
            v.wait_ge(S["o_landed"], 16)
            v.wait_ge(S["g_landed"], 16)
            for kind in range(2):
                ks = slice(4 * kind, 4 * kind + 4)
                v.tensor_tensor(o_all[:, ks], o_all[:, ks], g_all[:, ks], ALU.mult).then_inc(S["o_times_g"], 1)
            for kind in range(2):
                ks = slice(4 * kind, 4 * kind + 4)
                v.wait_ge(S["g_sig"], kind + 1)
                v.wait_ge(S["o_times_g"], kind + 1)
                v.tensor_tensor(o_all[:, ks], o_all[:, ks], g_all[:, ks], ALU.mult).then_inc(S["o_gated"], 1)
            for kind in range(2):
                ks = slice(4 * kind, 4 * kind + 4)
                v.wait_ge(S["oh_hi"], kind + 1)
                v.tensor_tensor(h_lo[:, ks], o_all[:, ks], h_hi[:, ks], ALU.subtract).then_inc(S["oh_lo"], 1)
            for j in range(2 * KT):
                n = T_BR + j
                if j == 8:
                    for hf in (0, 1):
                        split_lo(G_FIN, 1, hf)
                v.wait_ge(S["tile_free"], n)
                v.wait_ge(S["tile_made"], n + 1)
                v.wait_ge(S["m_sig"], j + 1)
                v.tensor_tensor(m_all[:, j], proj[:, j % 2], m_all[:, j], ALU.mult).then_inc(S["tile_free"], 1)
                if j >= KT:
                    i = j - KT
                    v.wait_ge(S["tile_free"], n + 1)
                    v.tensor_tensor(m_all[:, j], m_all[:, j], m_all[:, i], ALU.add).then_inc(S["merged"], 1)
                    v.wait_ge(S["mg_hi"], i + 1)
                    v.tensor_tensor(mg_lo[:, i], m_all[:, j], mg_hi[:, i], ALU.subtract).then_inc(S["mg_lo"], 1)
            for hf in (0, 1):
                split_lo(G_FIN + 1, 0, hf)
            v.wait_ge(S["x2_landed"], 16)
            for j in range(KT):
                n = T_FIN + j
                v.wait_ge(S["tile_free"], n)
                v.wait_ge(S["tile_made"], n + 1)
                xx = x_fin[:, j % 4, 512 * (j // 4):512 * (j // 4 + 1)]
                v.tensor_tensor(xx, xx, proj[:, j % 2], ALU.add).then_inc(S["tile_free"], 1)

        @block.tensor
        def _(pe):
            t_ = nc.tensor
            t_.wait_ge(S["consts"], 7)
            norm_pe(0, 0)
            for j in (0, 1):
                made(project(G_GATES, 0, j, j, j, first=True, norm=0 if j == 0 else None))
            t_.wait_ge(S["rows_a"], 1)
            for t in range(TB):
                mm = t_.transpose(pm[:, HEADS * t:HEADS * (t + 1)], g_a[:, t * P:(t + 1) * P], ident[0:HEADS, 0:HEADS])
            mm.then_inc(S["a_turned"], 1)
            t_.wait_ge(S["a_col"], 1)
            with t_.Fori(0, HEADS) as h:
                n = T_HEADS + 8 * h
                ga = G_HEADS + 2 * h

                def tile(j):
                    made(project(ga + j // 4, (1 + j // 4) % 2, n + j, j % 2, j % 4))

                def triangle(out_, lhsT, rhs, rows=P):
                    for i in range(TB):
                        mm = t_.matmul(out_[:, TRI[i]:TRI[i] + SEQ - P * i], lhsT[0:rows, P * i:P * (i + 1)],
                                       rhs[0:rows, P * i:], start=True, stop=True)
                    return mm

                def weighted(out_, keys, weights):
                    for i in range(TB):
                        mm = t_.matmul(out_[:, P * i:SEQ], keys(i), weights[:, TRI[i]:TRI[i] + SEQ - P * i],
                                       start=(i == 0), stop=(i == TB - 1))
                    return mm

                tile(0)
                tile(1)
                tile(2)
                t_.wait_ge(S["head_done"], h + 1)
                for j, sq in enumerate((sq_q, sq_k)):
                    t_.wait_ge(S["tile_free"], n + j + 1)
                    t_.matmul(pa[:, 512 * j:512 * (j + 1)], mean[:, :], sq[:, :], start=True, stop=True).then_inc(S["ssq_made"], 1)
                tile(3)
                t_.wait_ge(S["qk_normed"], 2 * h + 2)
                triangle(pa, k_b, q_b).then_inc(S["z_made"], 1)
                tile(4)
                t_.wait_ge(S["tile_free"], n + 5)
                for m, vT in enumerate((v_bT, v_aT)):
                    for i in range(TB):
                        mm = t_.transpose(pm[:, 512 * m + P * i:512 * m + P * (i + 1)], vT[:, P * i:P * (i + 1)], ident[:, :])
                mm.then_inc(S["v_turned"], 1)
                tile(5)
                t_.wait_ge(S["v_sb"], 2 * h + 2)
                t_.wait_ge(S["ka_landed"], 16 * h + 16)
                triangle(pm, k_a, silu, DQK_A).then_inc(S["s_made"], 1)
                tile(6)
                t_.wait_ge(S["sp_lo"], h + 1)
                for i in range(TB):
                    mms = [(tri_r if i2 == i else ones_r, i2, s_) for i2 in range(i, TB - 1) for s_ in (sp_hi, sp_lo)]
                    mms.append((tri if i == TB - 1 else ones, TB - 1, sp))
                    for q, (w, i2, s_) in enumerate(mms):
                        mm = t_.matmul(pa[:, TRI[i] + P * (i2 - i):TRI[i] + SEQ - P * i], w[:, :],
                                       s_[:, TRI[i2]:TRI[i2] + SEQ - P * i2], start=(q == 0), stop=(q == len(mms) - 1))
                mm.then_inc(S["c_made"], 1)
                t_.wait_ge(S["p_masked"], 4 * h + 4)
                weighted(pm[:, 0:512], lambda i: v_a[:, P * i:P * (i + 1)], decay)
                weighted(pm[:, 512:1024], lambda i: ones[:, :], decay).then_inc(S["num_made"], 1)
                tile(7)
                t_.wait_ge(S["num_sq"], h + 1)
                t_.matmul(pm[:, 1024:1536], mean[:, :], num2[:, :], start=True, stop=True).then_inc(S["num_ssq"], 1)
                t_.wait_ge(S["a_b"], h + 1)
                weighted(pa[:, 0:512], lambda i: v_b[:, P * i:P * (i + 1)], z).then_inc(S["pv_b_made"], 1)
            t_.wait_ge(S["head_done"], HEADS)
            for g in range(G_OUT, G_MLP):
                for t in range(TB):
                    i = 4 * (g - G_OUT) + t
                    made(project(g, g % 2, T_OUT + i, i % 2, t, tokens=True, act=(y_hi, y_lo),
                                 last=("head_done", HEADS + 1) if i == 0 else None))
            norm_pe(1, T_MLP)
            with t_.Fori(0, CHUNKS) as c:
                g = G_MLP + 4 * c
                n = T_MLP + 16 * c
                for i in range(8):
                    made(project(g + i // 4, (1 + i // 4) % 2, n + i, i % 2, i % 4, norm=1 if i == 0 else None))
                t_.wait_ge(S["a_lo_done"], 8 * c + 8)
                for i in range(8, 16):
                    made(project(g + i // 4, (1 + i // 4) % 2, n + i, i % 2, i % 4,
                                 tokens=True, act=(act_hi, act_lo)))
            norm_pe(2, T_END1)

            def tokens(g, n0, tiles):
                for t in tiles:
                    made(project(g, g % 2, n0 + t, (n0 + t) % 2, t, tokens=True,
                                 norm=2 if g == G_C and t == 0 else None))

            tokens(G_C, T_C, range(TB))
            tokens(G_K, T_K, (0, 1))
            t_.wait_ge(S["c_scaled"], 2 * TB)
            for m in range(3):
                for t in range(TB):
                    mm = t_.transpose(pa[:, 512 * m + P * t:512 * m + P * (t + 1)], t_c[:, t, P * m:P * (m + 1)], ident[:, :])
                mm.then_inc(S["c_turned"], 1)
            tokens(G_K, T_K, (2, 3))
            t_.wait_ge(S["c_lo"], 3)
            for t in range(TB):
                for q, (act_, kts, k0) in enumerate((((cq_hi, cq_lo), 2, 0), ((cq_hi, cq_lo), 2, 2),
                                                     ((ckv_hi, ckv_lo), 1, 4), ((ckv_hi, ckv_lo), 1, 5))):
                    n = T_U + 4 * t + q
                    made(project(G_U, G_U % 2, n, q % 2, t, tokens=True, act=act_, kts=kts, k0=k0))
            tokens(G_Q, T_Q, (0,))
            t_.wait_ge(S["ki_spread"], 1)
            t_.wait_ge(S["rope"], 12)
            for t in range(TB):
                mm = t_.transpose(pa[:, P * t:P * (t + 1)], t_k[:, t, 0:P], ident[:, :])
            mm.then_inc(S["ki_turned"], 1)
            for g in range(2):
                for t in range(TB):
                    mm = t_.transpose(pm[:, 512 * g + P * t:512 * g + P * (t + 1)], t_k[:, t, P * (g + 2):P * (g + 3)], ident[:, :])
            mm.then_inc(S["qi_turned"], 1)
            tokens(G_Q, T_Q, (1,))
            for h in range(HEADS):
                X = pm if h % 2 else pa
                if h in (2, 4):
                    tokens(G_Q, T_Q, (1 + h // 2,))
                if h == 0:
                    t_.wait_ge(S["qi_sb"], 3)
                if h >= 2:
                    t_.wait_ge(S["idx_relu"], h - 1)
                g, rows = h // 4, slice(IDX_D * (h % 4), IDX_D * (h % 4 + 1))
                for i in range(TB):
                    mm = t_.matmul(X[:, LOW[i]:LOW[i] + P * (i + 1)], t_c[rows, i, P * g:P * (g + 1)],
                                   t_c[rows, 0:i + 1, 256:384], start=True, stop=True)
                mm.then_inc(S["idx_made"], 1)
            t_.wait_ge(S["idx_relu"], HEADS)

            def gate(B, s, i):
                made(project(G_L + B, 1 - s, T_L + 3 * B + i, (s + i) % 2, i))

            def head_turn(u, B, d):
                X = (pa, pm)[u]
                t_.wait_ge(S[f"staged{u}"], 2 * B + 2)
                t_.wait_ge(S[f"o_sb{u}"], B + 1)
                d = QK_M
                for w, st in enumerate((q_st[u], k_st[u])):
                    for t in range(TB):
                        mm = t_.transpose(X[0:d, 512 * w + P * t:512 * w + P * (t + 1)], st[:, t, 0:d], ident[:, :])
                mm.then_inc(S[f"qk_turned{u}"], 1)

            def head_scores(u, B, d):
                X = (pa, pm)[u]
                t_.wait_ge(S[f"qk_sb{u}"], 2 * B + 2)
                for i in range(TB):
                    mm = t_.matmul(X[:, LOW[i]:LOW[i] + P * (i + 1)], qT[u][0:d, P * i:P * (i + 1)],
                                   kT[u][0:d, 0:P * (i + 1)], start=True, stop=True)
                mm.then_inc(S[f"scores{u}"], 1)

            def head_pT(u, B):
                X = (pa, pm)[u]
                t_.wait_ge(S[f"p_norm{u}"], 4 * B + 4)
                for j in range(TB):
                    for i in range(j, TB):
                        o = TRI[j] + P * (i - j)
                        mm = t_.transpose(X[:, o:o + P], p_sb[u][:, LOW[i] + P * j:LOW[i] + P * (j + 1)], ident[:, :])
                mm.then_inc(S[f"p_turned{u}"], 1)

            def head_pv(u, B):
                X = (pa, pm)[u]
                t_.wait_ge(S[f"pT_sb{u}"], B + 1)
                t_.wait_ge(S[f"v_staged{u}"], 2 * B + 2)
                for i in range(TB):
                    mm = t_.matmul(X[:, P * i:SEQ], v_st[u][:, i, :], pT[u][:, TRI[i]:TRI[i] + SEQ - P * i],
                                   start=(i == 0), stop=(i == TB - 1))
                mm.then_inc(S[f"pv{u}"], 1)

            for kind, d in enumerate((QK_M, D_D)):
                with t_.Fori(0, 2) as b:
                    for s in range(2):
                        B = 4 * kind + 2 * b + s
                        head_turn(0, B, d)
                        head_turn(1, B, d)
                        gate(B, s, 0)
                        head_scores(0, B, d)
                        head_scores(1, B, d)
                        gate(B, s, 1)
                        head_pT(0, B)
                        head_pT(1, B)
                        gate(B, s, 2)
                        head_pv(0, B)
                        head_pv(1, B)
            for kind in range(2):
                t_.wait_ge(S["oh_lo"], kind + 1)
                for j in range(KT):
                    n = T_BR + KT * kind + j
                    made(project(G_BR + kind, (1 + kind) % 2, n, j % 2, j % 4, kts=4, k0=4 * (j // 4),
                                 act=(h_hi[:, 4 * kind:4 * kind + 4], h_lo[:, 4 * kind:4 * kind + 4])))
            t_.wait_ge(S["mg_lo"], KT)
            for g in range(2):
                for t in range(TB):
                    n = T_FIN + 4 * g + t
                    made(project(G_FIN + g, (1 + g) % 2, n, t % 2, t, tokens=True, act=(mg_hi, mg_lo)))


def k_tiles(a):
    return a.reshape(-1, P, a.shape[1]).transpose(1, 0, 2)


def lay_out(v):
    v = {name: np.asarray(a) for name, a in v.items()}
    one = {name: a[0] for name, a in v.items()}
    wall = np.zeros((N_GROUPS, P, KT, 512), np.float32)

    sizes = (512, 512, 1024, 1024, HEADS, HEADS, 1024, 1024, 1024, 1024, 1024)
    q_a, k_a, v_a, o_a, i_a, f_a, q_b, k_b, v_b, g_a, g_b = np.split(k_tiles(one["w_in"]), np.cumsum(sizes)[:-1], axis=2)
    wall[G_GATES, :, :, 0:HEADS] = i_a
    wall[G_GATES, :, :, P:P + HEADS] = f_a
    for h in range(HEADS):
        wide, narrow = slice(P * h, P * (h + 1)), slice(DQK_A * h, DQK_A * (h + 1))
        wall[G_HEADS + 2 * h] = np.concatenate(
            [q_b[:, :, wide], k_b[:, :, wide], q_a[:, :, narrow], k_a[:, :, narrow], v_b[:, :, wide]], axis=2)
        wall[G_HEADS + 2 * h + 1] = np.concatenate([w[:, :, wide] for w in (v_a, o_a, g_a, g_b)], axis=2)
    for j in range(2):
        half = slice(512 * j, 512 * (j + 1))
        wall[G_OUT + j] = k_tiles(one["w_out"])[:, :, half]
        wall[G_FIN + j] = k_tiles(one["w_out_2"])[:, :, half]
        for c in range(CHUNKS):
            wall[G_MLP + 4 * c + j] = k_tiles(one["w_up"])[:, :, DM * c + 512 * j:DM * c + 512 * (j + 1)]
            wall[G_MLP + 4 * c + 2 + j] = k_tiles(one["w_down"][DM * c:DM * (c + 1)])[:, :, half]
    head_par = np.zeros((P, HEADS, 7), np.float32)
    taps = one["conv_w"].reshape(4, 2, HEADS, DQK_A)
    head_par[0:DQK_A, :, 0:4] = taps[:, 0].transpose(2, 1, 0)
    head_par[DQK_A:P, :, 0:4] = taps[:, 1].transpose(2, 1, 0)
    head_par[:, :, 4] = one["mlstm_norm_g"].reshape(HEADS, P).T
    head_par[:, :, 5:7] = one["b_gate"].reshape(2, HEADS, P).transpose(2, 1, 0)

    sizes = (256, 128, 32, 512, 512, 128, 128, 512, 256, 32, 8, 1024, 1024)
    (c_q, c_kv, k_pe, gate_a, q_b, k_b, v_b, gate_b, q_i, k_i, w_i, m_a, m_b) = np.split(
        k_tiles(one["w_in_2"]), np.cumsum(sizes)[:-1], axis=2)
    wall[G_C, :, :, 0:456] = np.concatenate([c_q, c_kv, k_pe, k_i, w_i], axis=2)
    wall[G_Q] = q_b
    wall[G_K] = np.concatenate([k_b, v_b, q_i], axis=2)
    uq = k_tiles(one["mla_w_uq_2"])
    ukv = one["mla_w_ukv_2"].reshape(P, HEADS, 2, NOPE)
    for k in range(2):
        wall[G_U, :, k] = uq[:, k, 0:512]
        wall[G_U, :, 2 + k, 0:256] = uq[:, k, 512:768]
        wall[G_U, :, 4 + k] = ukv[:, :, k].reshape(P, 512)
    gates = np.concatenate([gate_a, gate_b, m_a, m_b], axis=2)
    for j in range(8):
        wall[G_L + j, :, :, 0:384] = gates[:, :, 384 * j:384 * (j + 1)]
    for j, name in enumerate(("w_branch_mla_2", "w_branch_dsa_2")):
        wall[G_BR + j] = one[name].reshape(4, P, 2, 512).transpose(1, 2, 0, 3).reshape(P, 8, 512)
    wide_gains = np.zeros((4, QK_M), np.float32)
    for j, name in enumerate(("mla_q_gain_2", "mla_k_gain_2", "dsa_q_gain_2", "dsa_k_gain_2")):
        wide_gains[j, 0:one[name].size] = one[name]
    inv_freq = np.concatenate([np.float32(500000.0) ** (-np.arange(0, r, 2, dtype=np.float32) / np.float32(r))
                               for r in (32, 16, 8)])

    gains = np.concatenate([one[n].reshape(KT, P).T for n in ("norm_mix_g", "norm_mlp_g", "norm_gain_2")], axis=1)
    c_gains = np.concatenate([one["mla_q_norm_2"].reshape(2, P), one["mla_kv_norm_2"].reshape(1, P)]).T
    return {
        "x": one["x"], "wall": wall, "gains": gains, "head_par": head_par,
        "sb_gains": np.stack([one["sb_q_norm_g"], one["sb_k_norm_g"]], axis=1),
        "b_if": one["b_if"].reshape(2, HEADS).T,
        "positions": one["positions_2"].astype(np.int32).reshape(TB, P).T,
        "inv_freq": inv_freq.astype(np.float32).reshape(1, N_FREQ), "wide_gains": wide_gains, "c_gains": c_gains,
        "b_merge": one["b_merge_2"].reshape(2 * KT, P).T,
    }


def kernel(**inputs):
    import concourse.bacc as bacc
    from concourse.bass_utils import run_bass_kernel_spmd

    nc = bacc.Bacc("TRN2", target_bir_lowering=False, num_devices=1)
    arrays, args = {}, []
    for name, a in lay_out(inputs).items():
        a = np.ascontiguousarray(a)
        arrays[f"in_{name}"] = a
        args.append(nc.dram_tensor(f"in_{name}", a.shape, mybir.dt.from_np(a.dtype), kind="ExternalInput").ap())
    args.append(nc.dram_tensor("result", (SEQ, DM), F32, kind="ExternalOutput").ap())
    program(nc, *args)
    r = run_bass_kernel_spmd(nc, [arrays], core_ids=[0])
    return r.results[0]["result"].reshape(1, SEQ, DM)
```

```python
from contextlib import ExitStack

import numpy as np

import concourse.bass as bass
from concourse import mybir

F32 = mybir.dt.float32
F32R = mybir.dt.float32r
ALU = mybir.AluOpType
ACT = mybir.ActivationFunctionType
AX = mybir.AxisListType

P = 128
SEQ = 512
TB = SEQ // P
DM = 1024
KT = DM // P
HEADS = 8
FF = 4096
CHUNKS = FF // DM
EPS = 1e-6
DQK_A = 64
HD_B = 128
NEG = -1.0e30

G_GATES = 0
G_HEADS = 1
G_OUT = G_HEADS + 2 * HEADS
G_MLP = G_OUT + 2
G_END1 = G_MLP + 4 * CHUNKS
T_HEADS = 2
T_OUT = T_HEADS + 8 * HEADS
T_MLP = T_OUT + 8
T_END1 = T_MLP + 16 * CHUNKS

TRI = {0: 0, 1: 512, 3: 896, 2: 1024}
TRI_COLS = 1280

QK_M = 96
NOPE = 64
D_D = 64
KV_D = 2
IDX_D = 32
N_FREQ = 28
TAKEN = -3.0e38
PI = float(np.pi)
TWO_PI_HI = 6.28125
TWO_PI_LO = 2 * PI - TWO_PI_HI
ROUND = 1.5 * 2.0 ** 23
G_C = G_END1
G_K = G_C + 1
G_U = G_K + 1
G_Q = G_U + 1
G_L = G_Q + 1
G_BR = G_L + 8
G_FIN = G_BR + 2
N_GROUPS = G_FIN + 2
T_C = T_END1
T_K = T_C + 4
T_U = T_K + 4
T_Q = T_U + 16
T_L = T_Q + 4
T_BR = T_L + 24
T_FIN = T_BR + 16
T_END = T_FIN + 8
SIN_MAX = 3.1415925


def program(nc, x_in, wall, gains, head_par, sb_gains, b_if, *rest):
    *block2_in, out = rest
    with ExitStack() as ctx:
        def sb(name, shape, dt=F32):
            return ctx.enter_context(nc.sbuf_tensor(name, shape, dt))

        class Signals(dict):
            def __missing__(self, name):
                self[name] = ctx.enter_context(nc.semaphore(name))
                return self[name]

        S = Signals()

        w_raw = sb("w_raw", [P, 2, 4, 512])
        w_hi = sb("w_hi", [P, 2, KT, 512], F32R)
        w_lo = sb("w_lo", [P, 2, KT, 512], F32R)
        h_hi = sb("h_hi", [P, KT, SEQ], F32R)
        h_lo = sb("h_lo", [P, KT, SEQ], F32R)
        ident = sb("ident", [P, P])
        mean = sb("mean", [P, P])
        ones = sb("ones", [P, P])
        ones_r = sb("ones_r", [P, P], F32R)
        eps = sb("eps", [P, 1])
        gain = sb("gain", [P, 3 * KT])
        ss = sb("ss", [P, 3, TB])
        lnv = sb("lnv", [P, 3, TB])
        rstd = sb("rstd", [P, 3, TB])
        K = 1024
        base = (nc.sbuf_base + 31) // 32 * 32
        slab = sb("slab", [P, 90 * 256])

        def at(name, offset, shape, dt=F32):
            return nc.alloc_sbuf_tensor_at(name, shape, dt, offset=base + int(offset))

        y_hi = at("y_hi", 0, [P, KT, SEQ], F32R)
        y_lo = at("y_lo", 16 * K, [P, KT, SEQ], F32R)
        sp_hi = at("sp_hi", 32 * K, [P, TRI_COLS], F32R)
        sp_lo = at("sp_lo", 37 * K, [P, TRI_COLS], F32R)
        z = at("z", 42 * K, [P, TRI_COLS])
        sp = at("sp", 47 * K, [P, TRI_COLS])
        decay = at("decay", 52 * K, [P, TRI_COLS])
        bc = at("bc", 57 * K, [P, SEQ])
        names = "q_b k_b sq_q sq_k conv silu k_a v_bT v_aT v_b gate_o gate_a gate_b".split()
        (q_b, k_b, sq_q, sq_k, conv, silu, k_a, v_bT, v_aT, v_b, gate_o, gate_a, gate_b) = [
            at(n, (61 + 2 * i) * K, [P, SEQ]) for i, n in enumerate(names)]
        v_a = at("v_a", 87 * K, [P, TB, P + 1])
        y_tok, scl = sq_k, silu
        qk_pad = at("qk_pad", 47 * K, [P, 3 + SEQ])
        tri_r = sb("tri_r", [P, P], F32R)
        tri = at("tri", 89.25 * K, [P, P])
        par = sb("par", [P, 7])
        hp = sb("hp", [P, HEADS, 7])
        col = sb("col", [P, TB])
        a_col = sb("a_col", [P, TB, HEADS])
        e_col = sb("e_col", [P, TB, HEADS])
        tok = sb("tok", [P, 4, TB])
        floor = sb("floor", [P, TB])
        sbg = sb("sbg", [P, 2])
        x_res = at("x_res", 61 * K, [P, TB, DM])
        xs = at("xs", 44 * K, [P, TB, DM])
        act_hi = at("act_hi", 0, [P, KT, SEQ], F32R)
        act_lo = at("act_lo", 16 * K, [P, KT, SEQ], F32R)
        relu = at("relu", 32 * K, [P, 2, SEQ])
        relu_sq = at("relu_sq", 36 * K, [P, 2, SEQ])
        (g_i, g_f, g_abs, g_ls, g_F, g_a, g_G, g_m, one_row) = [
            at(f"gate_row{i}", (16 + 2 * i) * K, [HEADS, SEQ]) for i in range(9)]
        g_out = at("g_out", 40 * K, [HEADS, 2, SEQ])
        bif = sb("bif", [HEADS, 2])

        (positions, inv_freq, wide_gains, c_gains, b_merge) = block2_in
        cosine = sb("cosine", [P, TB, N_FREQ])
        sine = sb("sine", [P, TB, N_FREQ])
        c_gain = sb("c_gain", [P, 3])
        merge_bias = sb("merge_bias", [P, 2 * KT])
        c_ss = sb("c_ss", [P, 21, HEADS])
        w_idx = sb("w_idx", [P, TB, HEADS])
        top8 = sb("top8", [P, 3, 8])
        tick = sb("tick", [P, 33])
        mx = sb("mx", [P, 2, TB])
        row_sum = sb("row_sum", [P, 2, TB])
        (ang, turns, angles_c) = [at(f"angles{i}", (34 + i) * K, [P, TB, N_FREQ]) for i in range(3)]
        pos_i = at("pos_i", 43 * K, [P, TB], mybir.dt.int32)
        pos_f = at("pos_f", 43 * K + 32, [P, TB])
        freqs = at("freqs", 43 * K + 64, [P, N_FREQ])
        q_a2 = at("q_a2", 0, [P, TB, HEADS * QK_M])
        k_a2 = at("k_a2", 12 * K, [P, TB, HEADS * QK_M])
        v_a2 = at("v_a2", 24 * K, [P, TB, HEADS * D_D])
        q_b2 = at("q_b2", 32 * K, [P, TB, HEADS * D_D])
        k_b2 = at("k_b2", 40 * K, [P, TB, KV_D * D_D])
        v_b2 = at("v_b2", 42 * K, [P, TB, KV_D * D_D])
        idx = at("idx", 44 * K, [P, TRI_COLS])
        causal = at("causal", 49 * K, [P, SEQ])
        pT = [at(f"pT{u}", (51 + 16 * u) * K, [P, TRI_COLS]) for u in range(2)]
        kT = [at(f"kT{u}", (56, 79)[u] * K, [P, SEQ]) for u in range(2)]
        qT = [at(f"qT{u}", (58, 72)[u] * K, [P, SEQ]) for u in range(2)]
        p_sb = [at(f"p_sb{u}", (60 + 14 * u) * K, [P, TRI_COLS]) for u in range(2)]
        q_st = [at(f"q_st{u}", (60 + 14 * u) * K, [P, TB, QK_M]) for u in range(2)]
        k_st = [at(f"k_st{u}", (61.5 + 14 * u) * K, [P, TB, QK_M]) for u in range(2)]
        v_st = [at(f"v_st{u}", (65 + 16 * u) * K, [P, TB, P]) for u in range(2)]
        gate_st = at("gate_st", 83 * K, [P, 2, SEQ])
        o_st = at("o_st", 87 * K, [P, SEQ])
        t_c = at("t_c", 51 * K, [P, TB, 512])
        t_k = at("t_k", 59 * K, [P, TB, 512])
        squares = [at(f"squares{i}", (67 + 3 * i) * K, [P, HEADS * QK_M]) for i in range(2)]
        ra, rb, rc, rd = [at(f"rope{i}", (49 + i / 2) * K, [P, P]) for i in range(4)]
        cq_hi = at("cq_hi", 79 * K, [P, 2, SEQ], F32R)
        cq_lo = at("cq_lo", 83 * K, [P, 2, SEQ], F32R)
        ckv_hi = at("ckv_hi", 44 * K, [P, 1, SEQ], F32R)
        ckv_lo = at("ckv_lo", 46 * K, [P, 1, SEQ], F32R)
        rel = [at(f"rel{u}", (77 + 5 * u) * K, [P, TRI_COLS]) for u in range(2)]
        gain_qa, gain_ka, gain_qb, gain_kb = [at(f"gain_w{i}", (88 * 1024 + 384 * i), [P, d])
                                              for i, d in enumerate((96, 96, 64, 64))]
        o_all = at("o_all", 0, [P, KT, SEQ])
        g_all = at("g_all", 16 * K, [P, KT, SEQ])
        m_all = at("m_all", 32 * K, [P, 2 * KT, SEQ])
        x_fin = at("x_fin", 74 * K, [P, TB, DM])
        mg_hi = at("mg_hi", 0, [P, KT, SEQ], F32R)
        mg_lo = at("mg_lo", 16 * K, [P, KT, SEQ], F32R)
        x2_d = nc.dram_tensor("x2", [SEQ, DM], F32, kind="Internal").ap()
        gates_d = nc.dram_tensor("gates", [3 * KT, P, SEQ], F32, kind="Internal").ap()
        o_d = nc.dram_tensor("heads_out", [KT, P, SEQ], F32, kind="Internal").ap()

        q_a3, k_a3 = [b[:, :, :].rearrange("p t (h d) -> p t h d", h=HEADS) for b in (q_a2, k_a2)]
        q_b3 = q_b2[:, :, :].rearrange("p t (h d) -> p t h d", h=HEADS)
        k_b3 = k_b2[:, :, :].rearrange("p t (h d) -> p t h d", h=KV_D)
        PIECES = []
        for t in range(TB):
            PIECES.append((t_c[:, t:t + 1, 0:256].rearrange("p t (h d) -> p t h d", h=1), 1, 1, 256))
            PIECES.append((t_c[:, t:t + 1, 256:384].rearrange("p t (h d) -> p t h d", h=1), 1, 1, 128))
        PIECES.append((k_b3, TB, KV_D, D_D))
        for t in range(TB):
            PIECES.append((q_a3[:, t:t + 1], 1, HEADS, QK_M))
            PIECES.append((k_a3[:, t:t + 1], 1, HEADS, QK_M))
        for t in range(TB):
            PIECES.append((q_b3[:, t:t + 1], 1, HEADS, D_D))
        P_KB, P_A, P_QB = 8, 9, 17

        LOW = {3: 0, 2: 512, 0: 896, 1: 1024}
        TOPB = {1: 1024, 2: 512, 3: 0}

        proj = ctx.enter_context(nc.psum_tensor("proj", [P, 2, 512], F32))
        pa = ctx.enter_context(nc.psum_tensor("pa", [P, 3 * 512], F32))
        pm = ctx.enter_context(nc.psum_tensor("pm", [P, 3 * 512], F32))
        rows_d = nc.dram_tensor("gate_rows", [HEADS, SEQ], F32, kind="Internal").ap()
        by_tok = pm[:, 0:1024].rearrange("p (b n) -> p b n", b=2)[:, :, 0:2 * (P + 1)].rearrange("p b (q n) -> p b q n", q=2)

        block = ctx.enter_context(nc.Block())

        def tiles_by(g):
            return 2 + 4 * g

        def load_half(g, half, first=False):
            if not first:
                nc.sync.wait_ge(S["w_lo_done"], 2 * g + half - 1)
            nc.sync.dma_start(w_raw[:, half], wall[bass.ds(g, 1), :, 4 * half:4 * half + 4, :]
                              .rearrange("a p k n -> p (a k) n")).then_inc(S[f"w_landed{half}"], 16)

        def split_hi(g, slot, half, first=False, used=None):
            nc.scalar.wait_ge(S[f"w_landed{half}"], 16 * g + 16)
            if not first:
                nc.scalar.wait_ge(S["tile_made"], tiles_by(g - 2) if used is None else used)
            nc.scalar.activation(w_hi[:, slot, 4 * half:4 * half + 4, :], w_raw[:, half], ACT.Copy)\
                .then_inc(S["w_hi_done"], 1)

        def split_lo(g, slot, half):
            nc.vector.wait_ge(S[f"w_landed{half}"], 16 * g + 16)
            nc.vector.wait_ge(S["w_hi_done"], 2 * g + half + 1)
            nc.vector.tensor_tensor(w_lo[:, slot, 4 * half:4 * half + 4, :], w_raw[:, half],
                                    w_hi[:, slot, 4 * half:4 * half + 4, :], ALU.subtract)\
                .then_inc(S["w_lo_done"], 1)

        def project(g, slot, n, bank, j, tokens=False, act=None, kts=KT, k0=0, first=False, ready=None,
                    last=None):
            a_hi, a_lo = act or (h_hi, h_lo)
            if not first:
                nc.tensor.wait_ge(S["tile_free"], n - 1)
            c = slice(j * P, (j + 1) * P)
            for k in range(kts):
                if k == 0:
                    nc.tensor.wait_ge(S["w_lo_done"], 2 * g + 1 + k0 // 4)
                elif k + k0 == 4:
                    nc.tensor.wait_ge(S["w_lo_done"], 2 * g + 2)
                if ready:
                    nc.tensor.wait_ge(S[ready[0]], ready[1] + k + 1)
                if last and k == kts - 1:
                    nc.tensor.wait_ge(S[last[0]], last[1])
                for q, (w, a) in enumerate(((w_hi, a_hi), (w_hi, a_lo), (w_lo, a_hi))):
                    if tokens:
                        lhsT, rhs = a[:, k, c], w[:, slot, k0 + k, :]
                    else:
                        lhsT, rhs = w[:, slot, k0 + k, c], a[:, k, :]
                    mm = nc.tensor.matmul(proj[:, bank, :], lhsT, rhs, start=(k == 0 and q == 0),
                                          stop=(k == kts - 1 and q == 2))
            return mm

        def made(mm):
            mm.then_inc(S["tile_made"], 1)

        def norm_bank(k):
            if k < 2:
                return proj[:, k]
            return (pa, pm)[(k - 2) // 3][:, 512 * ((k - 2) % 3):512 * ((k - 2) % 3 + 1)]

        def norm_rstd(r, t):
            nc.scalar.activation(xs[:, t], x_res[:, t], ACT.Square, accum_out=ss[:, r, t:t + 1])\
                .then_inc(S["norm_ss"], 1)
            nc.scalar.wait_ge(S["norm_ss"], TB * r + t + 1)
            nc.scalar.activation(lnv[:, r, t:t + 1], ss[:, r, t:t + 1], ACT.Ln, bias=eps[:, 0:1], scale=1.0 / DM)\
                .then_inc(S["norm_ln"], 1)
            nc.scalar.wait_ge(S["norm_ln"], TB * r + t + 1)
            nc.scalar.activation(rstd[:, r, t:t + 1], lnv[:, r, t:t + 1], ACT.Exp, scale=-0.5).then_inc(S["norm_rstd"], 1)

        def norm_hi(r, k):
            nc.scalar.wait_ge(S["norm_turned"], KT * r + k + 1)
            nc.scalar.activation(h_hi[:, k], norm_bank(k), ACT.Copy, scale=gain[:, KT * r + k:KT * r + k + 1])\
                .then_inc(S["norm_hi"], 1)

        def norm_scale(r, t):
            nc.vector.wait_ge(S["norm_rstd"], TB * r + t + 1)
            nc.vector.tensor_scalar(xs[:, t], x_res[:, t], rstd[:, r, t:t + 1], None, ALU.mult)\
                .then_inc(S["norm_scaled"], 1)

        def norm_lo(r, k):
            nc.vector.wait_ge(S["norm_hi"], KT * r + k + 1)
            nc.vector.scalar_tensor_tensor(h_lo[:, k], norm_bank(k), gain[:, KT * r + k:KT * r + k + 1],
                                           h_hi[:, k], ALU.mult, ALU.subtract).then_inc(S["norm_lo"], 1)

        def norm_pe(r, tiles_before):
            if tiles_before:
                nc.tensor.wait_ge(S["tile_free"], tiles_before)
            for t in range(TB):
                nc.tensor.wait_ge(S["norm_scaled"], TB * r + t + 1)
                for k in range(KT):
                    mm = nc.tensor.transpose(norm_bank(k)[:, t * P:(t + 1) * P], xs[:, t, k * P:(k + 1) * P], ident[:, :])
                    if t == TB - 1:
                        mm.then_inc(S["norm_turned"], 1)

        pos_b = pos_f[:, :, None].broadcast_to([P, TB, N_FREQ])
        freq_b = freqs[:, None, :].broadcast_to([P, TB, N_FREQ])
        A3, T3, C3 = ang[:, :, :], turns[:, :, :], angles_c[:, :, :]
        ANGLES = [
            (pos_f, lambda v: v.tensor_copy(pos_f[:, :], pos_i[:, :])),
            (ang, lambda v: v.tensor_tensor(A3, pos_b, freq_b, ALU.mult)),
            (turns, lambda v: v.tensor_scalar(T3, A3, 1 / (2 * PI), ROUND, ALU.mult, ALU.add)),
            (turns, lambda v: v.tensor_scalar(T3, T3, ROUND, None, ALU.subtract)),
            (ang, lambda v: v.scalar_tensor_tensor(A3, T3, -TWO_PI_HI, A3, ALU.mult, ALU.add)),
            (ang, lambda v: v.scalar_tensor_tensor(A3, T3, -TWO_PI_LO, A3, ALU.mult, ALU.add)),
            (angles_c, lambda v: v.tensor_scalar(C3, A3, PI / 2, None, ALU.add)),
            (turns, lambda v: v.tensor_scalar(T3, C3, PI, 2 * PI, ALU.is_gt, ALU.mult)),
            (angles_c, lambda v: v.tensor_tensor(C3, C3, T3, ALU.subtract)),
            (ang, lambda v: v.tensor_scalar(A3, A3, SIN_MAX, -SIN_MAX, ALU.min, ALU.max)),
            (angles_c, lambda v: v.tensor_scalar(C3, C3, SIN_MAX, -SIN_MAX, ALU.min, ALU.max)),
        ]

        @block.sync
        def _(sp_):
            load_half(0, 0, first=True)
            load_half(0, 1, first=True)
            with nc.sync.Fori(1, N_GROUPS) as g:
                for half in (0, 1):
                    load_half(g, half)
            o_v, x_v = out.rearrange("(t p) d -> p t d", p=P), x_fin[:, :, :]
            nc.sync.wait_ge(S["tile_free"], T_FIN + 4)
            nc.sync.dma_start(o_v[:, :, 0:512], x_v[:, :, 0:512]).then_inc(S["out_stored"], 16)
            for t in range(TB):
                nc.sync.wait_ge(S["tile_free"], T_FIN + 5 + t)
                nc.sync.dma_start(o_v[:, t, 512:1024], x_v[:, t, 512:1024]).then_inc(S["out_stored"], 16)
            nc.sync.wait_ge(S["out_stored"], 16 * 5)

        @block.gpsimd
        def _(pool):
            gp = nc.gpsimd
            for dst, src in ((gain, gains), (hp, head_par), (sbg, sb_gains), (bif, b_if), (c_gain, c_gains), (merge_bias, b_merge),
                             (pos_i, positions), (freqs, inv_freq.broadcast_to([P, N_FREQ]))):
                gp.dma_start(dst[:], src).then_inc(S["par_landed"], 16)
            gp.memset(ident[:, :], 0.0).then_inc(S["c0"], 1)
            gp.memset(ones[:, :], 1.0).then_inc(S["c0"], 1)
            gp.memset(mean[:, :], 1.0 / P).then_inc(S["consts"], 1)
            gp.memset(eps[:, :], EPS).then_inc(S["consts"], 1)
            gp.memset(v_a[:, :, P:P + 1], 1.0).then_inc(S["consts"], 1)
            gp.memset(one_row[:, :], 1.0).then_inc(S["consts"], 1)
            gp.wait_ge(S["c0"], 2)
            gp.affine_select(out=ident[:, :], in_=ident[:, :], compare_op=ALU.not_equal, fill=1.0, base=0,
                             pattern=[[-1, P]], channel_multiplier=1).then_inc(S["consts"], 1)
            gp.tensor_copy(ones_r[:, :], ones[:, :]).then_inc(S["consts"], 1)
            gp.affine_select(out=tri[:, :], in_=ones[:, :], compare_op=ALU.is_ge, fill=0.0, base=0,
                             pattern=[[-1, P]], channel_multiplier=1).then_inc(S["consts"], 1)
            gp.affine_select(out=tri_r[:, :], in_=ones[:, :], compare_op=ALU.is_ge, fill=0.0, base=0,
                             pattern=[[-1, P]], channel_multiplier=1).then_inc(S["consts"], 1)
            gp.wait_ge(S["rows_ready"], 1)
            gp.dma_start(rows_d, g_out[:, 0, :]).then_inc(S["rows_stored"], 16)
            gp.wait_ge(S["rows_stored"], 16)
            for h in range(HEADS):
                if h:
                    gp.wait_ge(S["head_done"], h + 1)
                gp.dma_start(bc[:, :], rows_d[bass.ds(h, 1)].broadcast_to([P, SEQ])).then_inc(S["bc_landed"], 16)
                gp.wait_ge(S["silu_done"], h + 1)
                gp.dma_start(k_a[0:DQK_A, :], silu[DQK_A:P, :]).then_inc(S["ka_landed"], 16)
                gp.wait_ge(S["sp_done"], h + 1)
                for i in range(TB):
                    d = sp[:, TRI[i]:TRI[i] + P]
                    gp.affine_select(out=d, in_=d, compare_op=ALU.is_gt, fill=0.0, base=0,
                                     pattern=[[1, P]], channel_multiplier=-1).then_inc(S["sp_masked"], 1)
                gp.wait_ge(S["p_done"], h + 1)
                for i in range(TB):
                    d = decay[:, TRI[i]:TRI[i] + P]
                    gp.affine_select(out=d, in_=d, compare_op=ALU.is_ge, fill=0.0, base=0,
                                     pattern=[[1, P]], channel_multiplier=-1).then_inc(S["p_masked"], 1)
                gp.wait_ge(S["arg_b_done"], h + 1)
                for i in range(TB):
                    d = z[:, TRI[i]:TRI[i] + P]
                    gp.affine_select(out=d, in_=d, compare_op=ALU.is_gt, fill=NEG, base=0,
                                     pattern=[[1, P]], channel_multiplier=-1).then_inc(S["arg_b_masked"], 1)
            gp.wait_ge(S["head_done"], HEADS + 1)
            gp.wait_ge(S["x_area_free"], 1)
            gp.dma_start(x_res[:, :, :], x_in.rearrange("(t p) d -> p t d", p=P)).then_inc(S["x_landed"], 16)

            gp.wait_ge(S["tile_free"], T_END1)
            gp.dma_start(x2_d.rearrange("(t p) d -> p t d", p=P), x_res[:, :, :]).then_inc(S["x2_stored"], 16)
            gp.wait_ge(S["norm_turned"], KT * 3)
            for i, dst in enumerate((gain_qa, gain_ka, gain_qb, gain_kb)):
                d = dst.shape[1]
                gp.dma_start(dst[:, :], wide_gains[i:i + 1, 0:d].broadcast_to([P, d])).then_inc(S["wide_landed"], 16)
            gp.wait_ge(S["tile_free"], T_K + 4)
            gp.tensor_copy(k_b2[:, :, :], t_k[:, :, 0:128]).then_inc(S["kv_b"], 1)
            gp.tensor_copy(v_b2[:, :, :], t_k[:, :, 128:256]).then_inc(S["kv_b"], 1)
            gp.wait_ge(S["wide_landed"], 64)
            for t in range(TB):
                gp.wait_ge(S["c_scaled"], P_A + 2 * t + 2)
                gp.tensor_tensor(k_a3[:, t:t + 1], k_a3[:, t:t + 1],
                                 gain_ka[:, None, None, :].broadcast_to([P, 1, HEADS, QK_M]), ALU.mult)\
                    .then_inc(S["ka_gained"], 1)
            for kind, (q, k, v, d) in enumerate(((q_a2, k_a2, v_a2, QK_M), (q_b2, k_b2, v_b2, D_D))):
                for c in range(4):
                    B = 4 * kind + c
                    if c == 0 and kind == 0:
                        gp.wait_ge(S["rope"], 6 * 11)
                        gp.wait_ge(S["kv_b"], 2)
                        gp.wait_ge(S["qi_sb"], 3)
                    if c == 0 and kind == 1:
                        gp.wait_ge(S["rope"], 6 * 15)
                    for u in range(2):
                        hd = 2 * c + u
                        kh = hd if kind == 0 else hd // (HEADS // KV_D)
                        if B:
                            gp.wait_ge(S[f"p_turned{u}"], B)
                        gp.tensor_copy(q_st[u][:, :, 0:d], q[:, :, hd * d:(hd + 1) * d]).then_inc(S[f"staged{u}"], 1)
                        gp.tensor_copy(k_st[u][:, :, 0:d], k[:, :, kh * d:(kh + 1) * d]).then_inc(S[f"staged{u}"], 1)
                    if B == 0:
                        gp.wait_ge(S["idx_done"], 1)
                        for i in range(TB):
                            x = idx[:, LOW[i] + P * i:LOW[i] + P * (i + 1)]
                            gp.affine_select(out=x, in_=x, compare_op=ALU.is_ge, fill=NEG, base=0,
                                             pattern=[[-1, P]], channel_multiplier=1).then_inc(S["idx_causal"], 1)
                        gp.wait_ge(S["rope"], 6 * 15)
                        gp.memset(causal[:, :], 0.0).then_inc(S["causal0"], 1)
                        gp.wait_ge(S["causal0"], 1)
                        gp.affine_select(out=causal[:, 384:512], in_=causal[:, 384:512], compare_op=ALU.is_ge, fill=NEG,
                                         base=0, pattern=[[-1, P]], channel_multiplier=1).then_inc(S["causal_made"], 1)
                    for u in range(2):
                        kh = 2 * c + u if kind == 0 else (2 * c + u) // (HEADS // KV_D)
                        if B:
                            gp.wait_ge(S[f"pv{u}"], B)
                        if kind == 0:
                            gp.tensor_copy(v_st[u][:, :, :], v[:, :, P * c:P * (c + 1)]).then_inc(S[f"v_staged{u}"], 2)
                        else:
                            for w in range(2):
                                gp.tensor_copy(v_st[u][:, :, D_D * w:D_D * (w + 1)], v[:, :, kh * D_D:(kh + 1) * D_D])\
                                    .then_inc(S[f"v_staged{u}"], 1)
                    if B == 5:
                        gp.wait_ge(S["o_stored"], 16 * 5)
                        gp.wait_ge(S["gates_stored0"], 16 * 7)
                        gp.wait_ge(S["gates_stored1"], 16 * 7)
                        gp.wait_ge(S["v_staged0"], 8)
                        gp.wait_ge(S["v_staged1"], 8)
                        gp.dma_start(o_all[:, 0:4], o_d[0:4].rearrange("k p n -> p k n")).then_inc(S["o_landed"], 16)
                        gp.dma_start(g_all[:, :, :], gates_d[0:KT].rearrange("k p n -> p k n")).then_inc(S["o_landed"], 16)
                    if B == 6:
                        gp.wait_ge(S["o_landed"], 32)
                        for i in range(4):
                            gp.tensor_tensor(o_all[:, i], o_all[:, i], g_all[:, i], ALU.mult).then_inc(S["o_times_g"], 1)
            gp.wait_ge(S["o_stored"], 16 * 8)
            gp.dma_start(o_all[:, 4:7], o_d[4:7].rearrange("k p n -> p k n")).then_inc(S["o_landed1"], 16)
            gp.wait_ge(S["v_staged0"], 16)
            gp.wait_ge(S["v_staged1"], 16)
            gp.wait_ge(S["gates_stored0"], 16 * 10)
            gp.wait_ge(S["gates_stored1"], 16 * 10)
            gp.dma_start(m_all[:, 0:6], gates_d[KT:KT + 6].rearrange("k p n -> p k n")).then_inc(S["m_landed0"], 16)
            gp.wait_ge(S["o_stored"], 16 * 9)
            gp.dma_start(o_all[:, 7:8], o_d[7:8].rearrange("k p n -> p k n")).then_inc(S["o_landed2"], 16)
            gp.wait_ge(S["gates_stored0"], 16 * 13)
            gp.wait_ge(S["gates_stored1"], 16 * 13)
            gp.dma_start(m_all[:, 6:16], gates_d[KT + 6:3 * KT].rearrange("k p n -> p k n")).then_inc(S["m_landed1"], 16)
            gp.dma_start(x_fin[:, :, :], x2_d.rearrange("(t p) d -> p t d", p=P)).then_inc(S["x2_landed"], 16)
            for i in range(4, 8):
                if i in (4, 7):
                    gp.wait_ge(S["o_landed1" if i == 4 else "o_landed2"], 16)
                gp.tensor_tensor(o_all[:, i], o_all[:, i], g_all[:, i], ALU.mult).then_inc(S["o_times_g"], 1)
            for i in range(KT):
                gp.wait_ge(S["tile_free"], T_BR + KT + i + 1)
                gp.tensor_tensor(m_all[:, KT + i], m_all[:, KT + i], m_all[:, i], ALU.add).then_inc(S["merged"], 1)

        @block.scalar
        def _(act):
            a = nc.scalar
            x_tiles = x_in.rearrange("(t p) d -> p t d", p=P)
            for t in range(TB):
                a.dma_start(x_res[:, t], x_tiles[:, t]).then_inc(S[f"x_first{t}"], 16)
            for i, name in enumerate(("o_stored", "gates_stored0", "gates_stored1")):
                a.dma_start(tick[:, 24 + 3 * i:27 + 3 * i], c_gains).then_inc(S[name], 16)
            a.preload_act_table_set("natural_log_exp_and_others")
            a.wait_ge(S["consts"], 8)
            for t in range(TB):
                a.wait_ge(S[f"x_first{t}"], 16)
                norm_rstd(0, t)
            for hf in (0, 1):
                split_hi(0, 0, hf, first=True)
            for u in range(2):
                a.activation(mx[:, u, 0:1], eps[:, :], ACT.Copy).then_inc(S[f"o_sb{u}"], 1)
            a.wait_ge(S["par_landed"], 128)
            for k in range(KT):
                norm_hi(0, k)
            for hf in (0, 1):
                split_hi(1, 1, hf, first=True)
            a.wait_ge(S["tile_made"], 1)
            a.activation(g_i[:, :], proj[0:HEADS, 0], ACT.Identity, bias=bif[:, 0:1]).then_inc(S["tile_free"], 1)
            a.wait_ge(S["tile_made"], 2)
            a.activation(g_f[:, :], proj[0:HEADS, 1], ACT.Identity, bias=bif[:, 1:2]).then_inc(S["tile_free"], 1)
            a.wait_ge(S["tile_free"], 2)
            a.activation(g_abs[:, :], g_f[:, :], ACT.Abs).then_inc(S["rows_act"], 1)
            a.wait_ge(S["rows_act"], 1)
            a.activation(g_abs[:, :], g_abs[:, :], ACT.Exp, scale=-1.0).then_inc(S["rows_act"], 1)
            a.wait_ge(S["rows_act"], 2)
            a.activation(g_abs[:, :], g_abs[:, :], ACT.Ln, bias=1.0).then_inc(S["rows_act"], 1)
            a.wait_ge(S["angles"], len(ANGLES))
            a.activation(sine[:, :, :], A3, ACT.Sin).then_inc(S["rope_tables"], 1)
            a.activation(cosine[:, :, :], C3, ACT.Sin).then_inc(S["rope_tables"], 1)
            a.preload_act_table_set("natural_log_exp_and_others")
            a.wait_ge(S["rows_m"], 1)
            a.activation(g_out[:, 1, :], g_m[:, :], ACT.Exp, scale=-1.0).then_inc(S["rows_act"], 1)
            a.wait_ge(S["rows_stored"], 16)
            with a.Fori(0, HEADS) as h:
                n = T_HEADS + 8 * h
                ga = G_HEADS + 2 * h
                a.preload_act_table_set("natural_log_exp_and_others")
                split_hi(ga + 1, 0, 0)
                for j, (raw, sq) in enumerate(((q_b, sq_q), (k_b, sq_k))):
                    a.wait_ge(S["tile_made"], n + j + 1)
                    a.wait_ge(S["head_done"], h + 1)
                    a.activation(raw[:, :], proj[:, j], ACT.Copy)
                    a.activation(sq[:, :], proj[:, j], ACT.Square).then_inc(S["tile_free"], 1)
                split_hi(ga + 1, 0, 1)
                a.wait_ge(S["tile_made"], n + 3)
                a.wait_ge(S["head_done"], h + 1)
                a.activation(qk_pad[:, 3:3 + SEQ], proj[:, 0], ACT.Copy).then_inc(S["tile_free"], 1)
                for j, sq in enumerate((sq_q, sq_k)):
                    a.wait_ge(S["ssq_made"], 2 * h + j + 1)
                    a.activation(sq[:, :], pa[:, 512 * j:512 * (j + 1)], ACT.Ln, bias=eps[:, 0:1]).then_inc(S["rms_ln"], 1)
                    a.wait_ge(S["rms_ln"], 2 * h + j + 1)
                    a.activation(sq[:, :], sq[:, :], ACT.Exp, scale=-0.5).then_inc(S["rms_b"], 1)
                a.wait_ge(S["tile_made"], n + 4)
                a.activation(v_bT[:, :], proj[:, 1], ACT.Copy).then_inc(S["tile_free"], 1)
                split_hi(ga + 2, 1, 0)
                a.wait_ge(S["z_made"], h + 1)
                a.activation(z[:, :], pa[:, 0:TRI_COLS], ACT.Copy, scale=HD_B ** -0.5).then_inc(S["z_sb"], 1)
                a.wait_ge(S["z_sb"], h + 1)
                a.wait_ge(S["conv"], 4 * h + 4)
                a.activation(sp[:, :], z[:, :], ACT.Abs).then_inc(S["sp_act"], 1)
                a.wait_ge(S["sp_act"], 3 * h + 1)
                a.activation(sp[:, :], sp[:, :], ACT.Exp, scale=-1.0).then_inc(S["sp_act"], 1)
                a.wait_ge(S["tile_made"], n + 5)
                a.activation(v_aT[:, :], proj[:, 0], ACT.Copy).then_inc(S["tile_free"], 1)
                a.wait_ge(S["sp_act"], 3 * h + 2)
                a.activation(sp[:, :], sp[:, :], ACT.Ln, bias=1.0).then_inc(S["sp_act"], 1)
                a.activation(silu[:, :], conv[:, :], ACT.Sigmoid).then_inc(S["silu_sig"], 1)
                a.preload_act_table_set("natural_log_exp_and_others")
                a.wait_ge(S["v_turned"], h + 1)
                a.activation(v_b[:, :], pm[:, 0:512], ACT.Copy).then_inc(S["v_sb"], 1)
                a.activation(v_a[:, :, 0:P], pm[:, 512:1024].rearrange("p (t n) -> p t n", t=TB), ACT.Copy).then_inc(S["v_sb"], 1)
                split_hi(ga + 2, 1, 1)
                a.wait_ge(S["tile_made"], n + 6)
                a.activation(gate_o[:, :], proj[:, 1], ACT.Copy).then_inc(S["tile_free"], 1)
                a.wait_ge(S["arg_a"], 4 * h + 4)
                a.activation(decay[:, :], decay[:, :], ACT.Exp).then_inc(S["decay_exp"], 1)
                a.wait_ge(S["tile_made"], n + 7)
                a.activation(gate_a[:, :], proj[:, 0], ACT.Copy).then_inc(S["tile_free"], 1)
                a.wait_ge(S["arg_b_masked"], 4 * h + 4)
                a.activation(z[:, :], z[:, :], ACT.Exp).then_inc(S["a_b"], 1)
                a.wait_ge(S["num_made"], h + 1)
                for t in range(TB):
                    a.activation(y_tok[:, P * t:P * (t + 1)], by_tok[:, t // 2, t % 2, 0:P], ACT.Square,
                                 accum_out=tok[:, 2, t:t + 1]).then_inc(S["num_sq"], 1)
                a.wait_ge(S["var_a"], h + 1)
                a.activation(tok[:, 3], tok[:, 3], ACT.Ln, scale=1.0 / P).then_inc(S["var_ln"], 1)
                a.wait_ge(S["var_ln"], h + 1)
                a.activation(tok[:, 3], tok[:, 3], ACT.Exp, scale=-0.5).then_inc(S["rms_a"], 1)
                a.wait_ge(S["tile_free"], n + 7)
                a.activation(gate_o[:, :], gate_o[:, :], ACT.Sigmoid).then_inc(S["gate_sig"], 1)
                a.activation(gate_a[:, :], gate_a[:, :], ACT.Sigmoid, bias=par[:, 5:6]).then_inc(S["gate_sig"], 1)
                a.wait_ge(S["tile_made"], n + 8)
                a.activation(gate_b[:, :], proj[:, 1], ACT.Sigmoid, bias=par[:, 6:7]).then_inc(S["tile_free"], 1)
            a.preload_act_table_set("natural_log_exp_and_others")
            for g in range(G_OUT, G_MLP):
                for hf in (0, 1):
                    split_hi(g + 1, (g + 1) % 2, hf)
            for t in range(TB):
                a.wait_ge(S["tile_free"], T_MLP - TB + t + 1)
                norm_rstd(1, t)
            for k in range(KT):
                norm_hi(1, k)
            with a.Fori(0, CHUNKS) as c:
                g = G_MLP + 4 * c
                n = T_MLP + 16 * c
                for gg in range(2):
                    split_hi(g + gg + 1, gg % 2, 0)
                    for j in range(4):
                        i = 4 * gg + j
                        a.wait_ge(S["tile_made"], n + i + 1)
                        if i == 0:
                            a.wait_ge(S["tile_free"], n)
                        if i >= 2:
                            a.wait_ge(S["a_lo_done"], 8 * c + i - 1)
                        a.activation(relu[:, i % 2], proj[:, i % 2], ACT.Relu).then_inc(S["tile_free"], 1)
                        a.wait_ge(S["tile_free"], n + i + 1)
                        a.activation(act_hi[:, i], relu[:, i % 2], ACT.Square).then_inc(S["a_hi_done"], 1)
                        if j == 1:
                            split_hi(g + gg + 1, gg % 2, 1)
                for gg in range(2, 4):
                    for hf in (0, 1):
                        split_hi(g + gg + 1, gg % 2, hf)
            a.preload_act_table_set("natural_log_exp_and_others")
            for t in range(TB):
                a.wait_ge(S["tile_free"], T_END1 - TB + t + 1)
                norm_rstd(2, t)
            for k in range(KT):
                norm_hi(2, k)

            def evac(n, dst, src=None, wait=None):
                a.wait_ge(S["tile_made"], n + 1)
                a.activation(dst, proj[:, n % 2, 0:512] if src is None else src, ACT.Copy).then_inc(S["tile_free"], 1)

            def split(g):
                for hf in (0, 1):
                    split_hi(g, g % 2, hf)

            def square(p):
                x, T, h, d = PIECES[p]
                if p >= 2:
                    a.wait_ge(S["c_summed"], p - 1)
                o = squares[p % 2][:, 0:T * h * d]
                a.activation(o.rearrange("p (t h d) -> p t h d", t=T, h=h), x, ACT.Square).then_inc(S["c_squared"], 1)

            def root(p):
                x, T, h, d = PIECES[p]
                r = c_ss[:, p, 0:T * h]
                a.wait_ge(S["c_summed"], p + 1)
                a.activation(r, r, ACT.Ln, bias=eps[:, 0:1], scale=1.0 / d).then_inc(S["c_ln"], 1)
                a.wait_ge(S["c_ln"], p + 1)
                a.activation(r, r, ACT.Exp, scale=-0.5).then_inc(S["c_root"], 1)

            split(G_K)
            a.wait_ge(S["x2_stored"], 16)
            for t in range(TB):
                evac(T_C + t, t_c[:, t])
                a.wait_ge(S["tile_free"], T_C + t + 1)
                for p in (2 * t, 2 * t + 1):
                    square(p)
                for p in (2 * t, 2 * t + 1):
                    root(p)
            evac(T_K, t_k[:, 0])
            split(G_U)
            evac(T_K + 1, t_k[:, 1])
            for m in range(3):
                a.wait_ge(S["c_turned"], m + 1)
                dst = cq_hi[:, m] if m < 2 else ckv_hi[:, 0]
                a.activation(dst, pa[:, 512 * m:512 * (m + 1)], ACT.Copy, scale=c_gain[:, m:m + 1]).then_inc(S["c_hi"], 1)
            evac(T_K + 2, t_k[:, 2])
            evac(T_K + 3, t_k[:, 3])
            a.wait_ge(S["kv_b"], 1)
            square(P_KB)
            root(P_KB)
            a.wait_ge(S["k_pe_spread"], 1)
            for t in range(TB):
                n = T_U + 4 * t
                evac(n, q_a2[:, t, 0:512])
                a.wait_ge(S["tile_made"], n + 2)
                a.activation(q_a2[:, t, 512:768], proj[:, 1, 0:256], ACT.Copy).then_inc(S["tile_free"], 1)
                a.wait_ge(S["tile_made"], n + 3)
                a.activation(k_a3[:, t, :, 0:NOPE], proj[:, 0].rearrange("p (h d) -> p h d", h=HEADS), ACT.Copy)\
                    .then_inc(S["tile_free"], 1)
                evac(n + 3, v_a2[:, t])
                a.wait_ge(S["tile_free"], n + 4)
                for p in (P_A + 2 * t, P_A + 2 * t + 1):
                    square(p)
                    if t:
                        root(p - 2)
                if t in (1, 2):
                    split_hi(G_Q, G_Q % 2, t - 1)
            for hf in (0, 1):
                split_hi(G_L, G_L % 2, hf, used=T_Q)
            for p in (P_QB - 2, P_QB - 1):
                root(p)
            evac(T_Q, q_b2[:, 0])
            a.wait_ge(S["ki_turned"], 1)
            a.activation(t_c[:, :, 256:384], pa[:, 0:512].rearrange("p (t n) -> p t n", t=TB), ACT.Copy).then_inc(S["qi_sb"], 1)
            a.wait_ge(S["qi_turned"], 1)
            for g in range(2):
                a.activation(t_c[:, :, P * g:P * (g + 1)], pm[:, 512 * g:512 * (g + 1)].rearrange("p (t n) -> p t n", t=TB),
                             ACT.Copy).then_inc(S["qi_sb"], 1)
            evac(T_Q + 1, q_b2[:, 1])
            for h in range(HEADS):
                if h in (2, 4):
                    evac(T_Q + 1 + h // 2, q_b2[:, 1 + h // 2])
                a.wait_ge(S["idx_made"], h + 1)
                if h >= 2:
                    a.wait_ge(S["idx_sum"], 4 * (h - 1))
                a.activation(rel[h % 2][:, :], (pm if h % 2 else pa)[:, 0:TRI_COLS], ACT.Relu).then_inc(S["idx_relu"], 1)
                if h >= 4:
                    if h > 4:
                        root(P_QB + h - 5)
                    a.wait_ge(S["tile_free"], T_L)
                    square(P_QB + h - 4)
            root(P_QB + 3)

            a.wait_ge(S["idx_done"], 1)
            a.wait_ge(S["idx_causal"], 4)

            def head_turns(u, B, d):
                X = (pa, pm)[u]
                a.wait_ge(S[f"qk_turned{u}"], B + 1)
                a.activation(qT[u][0:d, :], X[0:d, 0:512], ACT.Copy).then_inc(S[f"qk_sb{u}"], 1)
                a.activation(kT[u][0:d, :], X[0:d, 512:1024], ACT.Copy).then_inc(S[f"qk_sb{u}"], 1)

            def head_exp(u, B):
                a.wait_ge(S[f"nmax{u}"], B + 1)
                for i in range(TB):
                    x = p_sb[u][:, LOW[i]:LOW[i] + P * (i + 1)]
                    a.activation(x, x, ACT.Exp, bias=mx[:, u, i:i + 1], accum_out=row_sum[:, u, i:i + 1])\
                        .then_inc(S[f"p_exp{u}"], 1)

            def head_pT(u, B):
                X = (pa, pm)[u]
                a.wait_ge(S[f"p_turned{u}"], B + 1)
                a.activation(pT[u][:, :], X[:, 0:TRI_COLS], ACT.Copy).then_inc(S[f"pT_sb{u}"], 1)

            def head_out(u, B):
                X = (pa, pm)[u]
                a.wait_ge(S[f"pv{u}"], B + 1)
                if u == 0:
                    a.wait_ge(S["o_stored"], 16 * B + 16)
                a.activation(o_st[D_D * u:D_D * (u + 1), :], X[D_D * u:D_D * (u + 1), 0:512], ACT.Copy).then_inc(S[f"o_sb{u}"], 1)

            def gate(c, s, i):
                n = T_L + 6 * c + 3 * s + i
                q = (s + i) % 2
                a.wait_ge(S["tile_made"], n + 1)
                a.wait_ge(S[f"gates_stored{q}"], 16 * (3 * c + (3 * s + i) // 2) + 16)
                a.activation(gate_st[:, q], proj[:, q], ACT.Copy).then_inc(S["tile_free"], 1)
                a.wait_ge(S["tile_free"], n + 1)
                a.dma_start(gates_d[bass.ds(n - T_L, 1)].rearrange("a p n -> p (a n)"), gate_st[:, q])\
                    .then_inc(S[f"gates_stored{q}"], 16)

            for kind, d in enumerate((QK_M, D_D)):
                with a.Fori(0, 2) as b:
                    for s in range(2):
                        c = 2 * kind + b
                        B = 2 * c + s
                        split_hi(G_L + B + 1, s, 0, used=T_L + 3 * B)
                        head_turns(0, B, d)
                        head_turns(1, B, d)
                        gate(c, s, 0)
                        head_exp(0, B)
                        head_exp(1, B)
                        split_hi(G_L + B + 1, s, 1, used=T_L + 3 * B)
                        gate(c, s, 1)
                        head_pT(0, B)
                        head_pT(1, B)
                        gate(c, s, 2)
                        head_out(0, B)
                        head_out(1, B)
                        a.wait_ge(S["o_sb0"], B + 2)
                        a.wait_ge(S["o_sb1"], B + 2)
                        a.dma_start(o_d[bass.ds(B, 1)].rearrange("a p n -> p (a n)"), o_st[:, :]).then_inc(S["o_stored"], 16)
            a.wait_ge(S["tile_free"], T_BR)

            def gated(kind, steps):
                for i in steps:
                    if i < 4:
                        a.wait_ge(S["o_times_g"], 4 * kind + i + 1)
                        a.activation(g_all[:, 4 * kind + i], g_all[:, 4 * kind + i], ACT.Sigmoid).then_inc(S["g_sig"], 1)
                    if i >= 1:
                        a.wait_ge(S["o_gated"], 4 * kind + i)
                        a.activation(h_hi[:, 4 * kind + i - 1], o_all[:, 4 * kind + i - 1], ACT.Copy).then_inc(S["oh_hi"], 1)

            def merge_gates(js):
                for j in js:
                    a.wait_ge(S["m_landed0" if j < 6 else "m_landed1"], 16)
                    a.activation(m_all[:, j], m_all[:, j], ACT.Sigmoid, bias=merge_bias[:, j:j + 1]).then_inc(S["m_sig"], 1)

            gated(0, range(5))
            merge_gates(range(4))
            for hf in (0, 1):
                split_hi(G_BR + 1, 0, hf, used=T_BR)
            merge_gates((4, 5))
            gated(1, range(5))
            merge_gates(range(6, 2 * KT))
            split_hi(G_FIN, 1, 0, used=T_BR + 8)
            for j in range(KT):
                if j == 1:
                    split_hi(G_FIN, 1, 1, used=T_BR + 8)
                a.wait_ge(S["merged"], j + 1)
                a.activation(mg_hi[:, j], m_all[:, KT + j], ACT.Copy).then_inc(S["mg_hi"], 1)
            for hf in (0, 1):
                split_hi(G_FIN + 1, 0, hf, used=T_BR + 16)

        @block.vector
        def _(dve):
            v = nc.vector
            v.memset(tick[:, 0:1], 0.0).then_inc(S["head_done"], 1)
            v.memset(tick[:, 1:2], 0.0).then_inc(S["top_out"], 1)
            v.memset(tick[:, 2:3], 0.0).then_inc(S["pad_zero"], 1)
            for t in range(TB):
                v.wait_ge(S[f"x_first{t}"], 16)
                norm_scale(0, t)
            split_lo(0, 0, 0)
            split_lo(0, 0, 1)
            v.wait_ge(S["par_landed"], 128)
            for k in range(KT):
                norm_lo(0, k)
            for hf in (0, 1):
                split_lo(1, 1, hf)
            for i, (dst, op) in enumerate(ANGLES):
                if i:
                    v.wait_ge(S["angles"], i)
                op(v).then_inc(S["angles"], 1)
            v.wait_ge(S["rows_act"], 3)
            v.scalar_tensor_tensor(g_ls[:, :], g_f[:, :], 0.0, g_abs[:, :], ALU.min, ALU.subtract).then_inc(S["rows_dve"], 1)
            v.wait_ge(S["rows_dve"], 1)
            v.tensor_tensor_scan(g_F[:, :], one_row[:, :], g_ls[:, :], 0.0, ALU.mult, ALU.add).then_inc(S["rows_dve"], 1)
            v.wait_ge(S["rows_dve"], 2)
            v.tensor_tensor(g_a[:, :], g_i[:, :], g_F[:, :], ALU.subtract).then_inc(S["rows_a"], 1)
            v.wait_ge(S["rows_a"], 1)
            v.tensor_tensor_scan(g_G[:, :], g_a[:, :], g_a[:, :], 0.0, ALU.max, ALU.max).then_inc(S["rows_dve"], 1)
            v.wait_ge(S["rows_dve"], 3)
            v.tensor_tensor(g_m[:, :], g_F[:, :], g_G[:, :], ALU.add).then_inc(S["rows_m"], 1)
            v.wait_ge(S["rows_act"], 4)
            v.tensor_scalar(g_out[:, 0, :], g_G[:, :], -1.0, None, ALU.mult).then_inc(S["rows_ready"], 1)
            v.wait_ge(S["a_turned"], 1)
            for i, dst in enumerate((a_col, e_col)):
                v.tensor_copy(dst[:, :, :], pm[:, TB * HEADS * i:TB * HEADS * (i + 1)].rearrange("p (t h) -> p t h", h=HEADS))\
                    .then_inc(S["a_col"], 1)
            v.wait_ge(S["a_col"], 2)
            with v.Fori(0, HEADS) as h:
                ga = G_HEADS + 2 * h
                v.wait_ge(S["head_done"], h + 1)
                v.tensor_copy(par[:, :], hp[:, bass.ds(h, 1), :].rearrange("p a n -> p (a n)")).then_inc(S["par_head"], 1)
                v.tensor_copy(col[:, :], a_col[:, :, bass.ds(h, 1)].rearrange("p t a -> p (t a)")).then_inc(S["par_head"], 1)
                v.tensor_copy(floor[:, :], e_col[:, :, bass.ds(h, 1)].rearrange("p t a -> p (t a)")).then_inc(S["par_head"], 1)
                v.memset(qk_pad[:, 0:3], 0.0).then_inc(S["pad_zero"], 1)
                split_lo(ga + 1, 0, 0)
                split_lo(ga + 1, 0, 1)
                for j, (raw, r) in enumerate(((q_b, sq_q), (k_b, sq_k))):
                    v.wait_ge(S["rms_b"], 2 * h + j + 1)
                    v.scalar_tensor_tensor(raw[:, :], raw[:, :], sbg[:, j:j + 1], r[:, :], ALU.mult, ALU.mult)\
                        .then_inc(S["qk_normed"], 1)
                v.wait_ge(S["par_head"], 3 * h + 3)
                v.wait_ge(S["pad_zero"], h + 2)
                v.wait_ge(S["tile_free"], T_HEADS + 8 * h + 3)
                v.tensor_scalar(conv[:, :], qk_pad[:, 0:SEQ], par[:, 0:1], None, ALU.mult).then_inc(S["conv"], 1)
                for j in range(1, 4):
                    v.wait_ge(S["conv"], 4 * h + j)
                    v.scalar_tensor_tensor(conv[:, :], qk_pad[:, j:j + SEQ], par[:, j:j + 1], conv[:, :],
                                           ALU.mult, ALU.add).then_inc(S["conv"], 1)
                split_lo(ga + 2, 1, 0)
                v.wait_ge(S["bc_landed"], 16 * h + 16)
                for i in range(TB):
                    v.tensor_scalar(decay[:, TRI[i]:TRI[i] + SEQ - P * i], bc[:, P * i:], col[:, i:i + 1], 0.0,
                                    ALU.add, ALU.min).then_inc(S["arg_a"], 1)
                v.wait_ge(S["sp_act"], 3 * h + 3)
                v.scalar_tensor_tensor(sp[:, :], z[:, :], 0.0, sp[:, :], ALU.max, ALU.add).then_inc(S["sp_done"], 1)
                v.wait_ge(S["silu_sig"], h + 1)
                v.tensor_tensor(silu[:, :], silu[:, :], conv[:, :], ALU.mult).then_inc(S["silu_done"], 1)
                v.wait_ge(S["sp_masked"], 4 * h + 4)
                v.tensor_copy(sp_hi[:, :], sp[:, :]).then_inc(S["sp_hi"], 1)
                v.wait_ge(S["sp_hi"], h + 1)
                v.tensor_tensor(sp_lo[:, :], sp[:, :], sp_hi[:, :], ALU.subtract).then_inc(S["sp_lo"], 1)
                split_lo(ga + 2, 1, 1)
                v.wait_ge(S["s_made"], h + 1)
                v.wait_ge(S["decay_exp"], h + 1)
                v.scalar_tensor_tensor(decay[:, :], pm[:, 0:TRI_COLS], DQK_A ** -0.5, decay[:, :], ALU.mult, ALU.mult)\
                    .then_inc(S["p_done"], 1)
                v.wait_ge(S["c_made"], h + 1)
                v.tensor_tensor(z[:, :], z[:, :], pa[:, 0:TRI_COLS], ALU.subtract).then_inc(S["arg_b_done"], 1)
                v.wait_ge(S["num_sq"], 4 * h + 4)
                for i, (sign, least) in enumerate(((-1.0, floor[:, :]), (1.0, tok[:, 0]))):
                    if i:
                        v.wait_ge(S["den_dve"], 3 * h + 1)
                    v.scalar_tensor_tensor(tok[:, 0].rearrange("p (b q) -> p b q", b=2), by_tok[:, :, :, P], sign,
                                           least.rearrange("p (b q) -> p b q", b=2), ALU.mult, ALU.max)\
                        .then_inc(S["den_dve"], 1)
                v.wait_ge(S["den_dve"], 3 * h + 2)
                v.scalar_tensor_tensor(tok[:, 1], tok[:, 0], EPS * P, tok[:, 0], ALU.mult, ALU.mult).then_inc(S["den_dve"], 1)
                v.wait_ge(S["den_dve"], 3 * h + 3)
                v.tensor_tensor(tok[:, 3], tok[:, 1], tok[:, 2], ALU.add).then_inc(S["var_a"], 1)
                v.wait_ge(S["rms_a"], h + 1)
                v.tensor_tensor(y_tok[:, :].rearrange("p (b q n) -> p b q n", b=2, q=2), by_tok[:, :, :, 0:P],
                                tok[:, 3].rearrange("p (b q) -> p b q", b=2)[:, :, :, None].broadcast_to([P, 2, 2, P]),
                                ALU.mult).then_inc(S["y_tok"], 1)
                v.wait_ge(S["y_turned"], h + 1)
                v.wait_ge(S["gate_sig"], 2 * h + 1)
                v.scalar_tensor_tensor(scl[:, :], pm[:, 1024:1536], par[:, 4:5], gate_o[:, :], ALU.mult, ALU.mult)\
                    .then_inc(S["y"], 1)
                v.wait_ge(S["gate_sig"], 2 * h + 2)
                v.wait_ge(S["y"], 4 * h + 1)
                v.tensor_tensor(scl[:, :], scl[:, :], gate_a[:, :], ALU.mult).then_inc(S["y"], 1)
                v.wait_ge(S["pv_b_made"], h + 1)
                v.wait_ge(S["tile_free"], T_HEADS + 8 * h + 8)
                v.tensor_tensor(gate_b[:, :], pa[:, 0:512], gate_b[:, :], ALU.mult).then_inc(S["y"], 1)
                v.wait_ge(S["y"], 4 * h + 3)
                v.tensor_tensor(scl[:, :], scl[:, :], gate_b[:, :], ALU.add).then_inc(S["y"], 1)
                v.wait_ge(S["y"], 4 * h + 4)
                yh = y_hi[:, bass.ds(h, 1), :].rearrange("p a n -> p (a n)")
                v.tensor_copy(yh, scl[:, :]).then_inc(S["y_hi"], 1)
                v.wait_ge(S["y_hi"], h + 1)
                v.tensor_tensor(y_lo[:, bass.ds(h, 1), :].rearrange("p a n -> p (a n)"), scl[:, :], yh, ALU.subtract)\
                    .then_inc(S["head_done"], 1)
            v.wait_ge(S["head_done"], HEADS + 1)
            v.memset(eps[:, :], EPS).then_inc(S["x_area_free"], 1)
            for g in range(G_OUT, G_MLP):
                for hf in (0, 1):
                    split_lo(g + 1, (g + 1) % 2, hf)
                for t in range(TB):
                    n = T_OUT + 4 * (g - G_OUT) + t
                    v.wait_ge(S["x_landed"], 16)
                    v.wait_ge(S["tile_free"], n)
                    v.wait_ge(S["tile_made"], n + 1)
                    xx = x_res[:, t, 512 * (g - G_OUT):512 * (g - G_OUT + 1)]
                    v.tensor_tensor(xx, xx, proj[:, t % 2], ALU.add).then_inc(S["tile_free"], 1)
                    if g == G_MLP - 1:
                        norm_scale(1, t)
            for k in range(KT):
                norm_lo(1, k)
            with v.Fori(0, CHUNKS) as c:
                g = G_MLP + 4 * c
                n = T_MLP + 16 * c
                for gg in range(2):
                    split_lo(g + gg + 1, gg % 2, 0)
                    for j in range(4):
                        i = 4 * gg + j
                        v.wait_ge(S["tile_free"], n + i + 1)
                        v.tensor_tensor(relu_sq[:, i % 2], relu[:, i % 2], relu[:, i % 2], ALU.mult).then_inc(S["a_sq"], 1)
                        v.wait_ge(S["a_hi_done"], 8 * c + i + 1)
                        v.wait_ge(S["a_sq"], 8 * c + i + 1)
                        v.tensor_tensor(act_lo[:, i], relu_sq[:, i % 2], act_hi[:, i], ALU.subtract).then_inc(S["a_lo_done"], 1)
                        if j == 1:
                            split_lo(g + gg + 1, gg % 2, 1)
                for gg in range(2, 4):
                    for hf in (0, 1):
                        split_lo(g + gg + 1, gg % 2, hf)
                    for t in range(TB):
                        i = 4 * gg + t
                        v.wait_ge(S["tile_free"], n + i)
                        v.wait_ge(S["tile_made"], n + i + 1)
                        xx = x_res[:, t, 512 * (gg - 2):512 * (gg - 1)]
                        v.tensor_tensor(xx, xx, proj[:, t % 2], ALU.add).then_inc(S["tile_free"], 1)
            for t in range(TB):
                norm_scale(2, t)
            for k in range(KT):
                norm_lo(2, k)

            def norm_sum(p):
                x, T, h, d = PIECES[p]
                v.wait_ge(S["c_squared"], p + 1)
                v.tensor_reduce(c_ss[:, p, 0:T * h], squares[p % 2][:, 0:T * h * d].rearrange("p (r d) -> p r d", d=d),
                                AX.X, ALU.add).then_inc(S["c_summed"], 1)

            def norm_mult(p):
                x, T, h, d = PIECES[p]
                v.wait_ge(S["c_root"], p + 1)
                r = c_ss[:, p, 0:T * h].rearrange("p (t h) -> p t h", t=T)[:, :, :, None].broadcast_to([P, T, h, d])
                v.tensor_tensor(x, x, r, ALU.mult).then_inc(S["c_scaled"], 1)

            def norm_gain(p, row):
                x, T, h, d = PIECES[p]
                v.wait_ge(S["c_scaled"], p + 1)
                v.tensor_tensor(x, x, row[:, None, None, :].broadcast_to([P, T, h, d]), ALU.mult).then_inc(S["c_gained"], 1)

            rope_n = [0]

            def rope(x, h, o, half, f0, tiles=slice(0, TB)):
                x1, x2 = x[:, :, :, o:o + half], x[:, :, :, o + half:o + 2 * half]
                T = tiles.stop - tiles.start
                c, s_ = [b[:, tiles, None, f0:f0 + half].broadcast_to([P, T, h, half]) for b in (cosine, sine)]
                A_, B_, C_, D_ = [b[:, 0:T * h * half].rearrange("p (t h d) -> p t h d", t=T, h=h) for b in (ra, rb, rc, rd)]
                if rope_n[0]:
                    v.wait_ge(S["rope"], 6 * rope_n[0])
                for dst, xx, w in ((A_, x1, c), (B_, x2, s_), (C_, x2, c), (D_, x1, s_)):
                    v.tensor_tensor(dst, xx, w, ALU.mult).then_inc(S["rope"], 1)
                v.wait_ge(S["rope"], 6 * rope_n[0] + 4)
                v.tensor_tensor(x1, A_, B_, ALU.subtract).then_inc(S["rope"], 1)
                v.tensor_tensor(x2, C_, D_, ALU.add).then_inc(S["rope"], 1)
                rope_n[0] += 1

            def split(g):
                for hf in (0, 1):
                    split_lo(g, g % 2, hf)

            split(G_K)
            for t in range(TB):
                for p in (2 * t, 2 * t + 1):
                    norm_sum(p)
                for p in (2 * t, 2 * t + 1):
                    norm_mult(p)
            v.tensor_copy(k_a3[:, :, :, NOPE:QK_M], t_c[:, :, None, 384:416].broadcast_to([P, TB, HEADS, 32]))\
                .then_inc(S["k_pe_spread"], 1)
            split(G_U)
            for m in range(3):
                v.wait_ge(S["c_hi"], m + 1)
                dst, hi = (cq_lo[:, m], cq_hi[:, m]) if m < 2 else (ckv_lo[:, 0], ckv_hi[:, 0])
                v.scalar_tensor_tensor(dst, pa[:, 512 * m:512 * (m + 1)], c_gain[:, m:m + 1], hi, ALU.mult, ALU.subtract)\
                    .then_inc(S["c_lo"], 1)
            ki = t_c[:, :, 416:448].rearrange("p t (h d) -> p t h d", h=1)
            rope(ki, 1, 0, 4, 24)
            v.tensor_scalar(w_idx[:, :, :], t_c[:, :, 448:456], (HEADS ** -0.5) * (IDX_D ** -0.5), None, ALU.mult)\
                .then_inc(S["w_idx"], 1)
            v.wait_ge(S["wide_landed"], 64)
            norm_sum(P_KB)
            v.wait_ge(S["rope"], 6)
            v.wait_ge(S["kv_b"], 2)
            v.tensor_copy(t_k[:, :, 0:P].rearrange("p t (r d) -> p t r d", d=IDX_D),
                          t_c[:, :, None, 416:448].broadcast_to([P, TB, P // IDX_D, IDX_D])).then_inc(S["ki_spread"], 1)
            qi = t_k[:, :, 256:512].rearrange("p t (h d) -> p t h d", h=HEADS)
            rope(qi, HEADS, 0, 4, 24)
            norm_mult(P_KB)
            norm_gain(P_KB, gain_kb)
            v.wait_ge(S["c_gained"], 1)
            rope(k_b3, KV_D, 0, 8, 16)
            for p in range(P_A, P_QB):
                norm_sum(p)
                if p in (P_A + 3, P_A + 5):
                    split_lo(G_Q, G_Q % 2, (p - P_A - 3) // 2)
            for p in range(P_A, P_QB):
                norm_mult(p)
            for p in range(P_A, P_QB, 2):
                norm_gain(p, gain_qa)
            split(G_L)
            for t in range(TB):
                v.wait_ge(S["c_gained"], 2 + t)
                rope(q_a3[:, t:t + 1], HEADS, NOPE, 16, 0, slice(t, t + 1))
                v.wait_ge(S["ka_gained"], t + 1)
                rope(k_a3[:, t:t + 1], HEADS, NOPE, 16, 0, slice(t, t + 1))
            v.wait_ge(S["w_idx"], 1)
            for h in range(HEADS):
                v.wait_ge(S["idx_relu"], h + 1)
                if h:
                    v.wait_ge(S["idx_sum"], 4 * h)
                for i in range(TB):
                    c = slice(LOW[i], LOW[i] + P * (i + 1))
                    if h == 0:
                        ins = v.tensor_scalar(idx[:, c], rel[0][:, c], w_idx[:, i, 0:1], None, ALU.mult)
                    else:
                        ins = v.scalar_tensor_tensor(idx[:, c], rel[h % 2][:, c], w_idx[:, i, h:h + 1], idx[:, c],
                                                     ALU.mult, ALU.add)
                    ins.then_inc(S["idx_sum"], 1)
                if h >= 4:
                    norm_sum(P_QB + h - 4)
            v.wait_ge(S["idx_sum"], 4 * HEADS)
            v.memset(mx[:, 0, 0:1], 0.0).then_inc(S["idx_done"], 1)
            for t in range(TB):
                norm_mult(P_QB + t)
            for t in range(TB):
                norm_gain(P_QB + t, gain_qb)
            for t in range(TB):
                v.wait_ge(S["c_gained"], 6 + t)
                rope(q_b3[:, t:t + 1], HEADS, 0, 8, 16, slice(t, t + 1))
            v.wait_ge(S["idx_causal"], 4)
            v.wait_ge(S["causal_made"], 1)

            holds = [0]

            def held(value, name):
                v.wait_ge(S[name], value)
                v.memset(tick[:, holds[0]:holds[0] + 1], 0.0)
                holds[0] = holds[0] + 1

            def head_max(u, B, mask, scale):
                X = (pa, pm)[u]
                held(B + 1, f"scores{u}")
                for i in range(TB):
                    c = slice(LOW[i], LOW[i] + P * (i + 1))
                    v.tensor_tensor_reduce(p_sb[u][:, c], X[:, c], mask(i), scale, -3.0e38, ALU.add, ALU.max,
                                           mx[:, u, i:i + 1]).then_inc(S[f"smax{u}"], 1)
                v.wait_ge(S[f"smax{u}"], 4 * B + 4)
                v.tensor_scalar(mx[:, u, :], mx[:, u, :], -1.0, None, ALU.mult).then_inc(S[f"nmax{u}"], 1)

            def head_norm(u, B):
                v.wait_ge(S[f"p_exp{u}"], 4 * B + 4)
                v.reciprocal(row_sum[:, u, :], row_sum[:, u, :]).then_inc(S[f"rden{u}"], 1)
                v.wait_ge(S[f"rden{u}"], B + 1)
                for i in range(TB):
                    x = p_sb[u][:, LOW[i]:LOW[i] + P * (i + 1)]
                    v.tensor_scalar(x, x, row_sum[:, u, i:i + 1], None, ALU.mult).then_inc(S[f"p_norm{u}"], 1)

            def top(b, r):
                held(12 * b + 3 * r + 1, "top_out")
                for i in range(1, TB):
                    v.max(top8[:, i - 1, :], idx[:, LOW[i]:LOW[i] + P * (i + 1)]).then_inc(S["top_max"], 1)
                held(12 * b + 3 * r + 3, "top_max")
                for i in range(1, TB):
                    x = idx[:, LOW[i]:LOW[i] + P * (i + 1)]
                    v.match_replace(x, top8[:, i - 1, :], x, TAKEN).then_inc(S["top_out"], 1)

            for kind in range(2):
                scale = (QK_M if kind == 0 else D_D) ** -0.5
                mask = (lambda i: causal[:, 384 - P * i:512]) if kind == 0 else (lambda i: idx[:, LOW[i]:LOW[i] + P * (i + 1)])
                with v.Fori(0, 2) as b:
                    for s in range(2):
                        c = 2 * b + s
                        B = 4 * kind + c
                        split_lo(G_L + B + 1, s, 0)
                        head_max(0, B, mask, scale)
                        head_max(1, B, mask, scale)
                        head_norm(0, B)
                        head_norm(1, B)
                        split_lo(G_L + B + 1, s, 1)
                        if kind == 0:
                            for rnd in range(4):
                                top(c, rnd)
                if kind == 0:
                    v.wait_ge(S["top_out"], 49)
                    v.tensor_copy(idx[:, LOW[0]:LOW[0] + P], causal[:, 384:512]).then_inc(S["mask"], 1)
                    for i in range(1, TB):
                        x = idx[:, LOW[i]:LOW[i] + P * (i + 1)]
                        v.tensor_scalar(x, x, TAKEN / 2, NEG, ALU.is_gt, ALU.mult).then_inc(S["mask"], 1)
                    v.wait_ge(S["mask"], 4)
            def gated(kind, steps):
                for step in steps:
                    i = 4 * kind + step
                    if step < 4:
                        v.wait_ge(S["g_sig"], i + 1)
                        v.wait_ge(S["o_times_g"], i + 1)
                        v.tensor_tensor(o_all[:, i], o_all[:, i], g_all[:, i], ALU.mult).then_inc(S["o_gated"], 1)
                    if step:
                        low(i - 1)

            def low(i):
                v.wait_ge(S["oh_hi"], i + 1)
                v.tensor_tensor(h_lo[:, i], o_all[:, i], h_hi[:, i], ALU.subtract).then_inc(S["oh_lo"], 1)

            def merged_low(i):
                v.wait_ge(S["mg_hi"], i + 1)
                v.tensor_tensor(mg_lo[:, i], m_all[:, KT + i], mg_hi[:, i], ALU.subtract).then_inc(S["mg_lo"], 1)

            gated(0, range(5))
            for j in range(2 * KT):
                n = T_BR + j
                if 3 <= j <= 7:
                    gated(1, (j - 3,))
                if j in (1, 2):
                    split_lo(G_BR + 1, 0, j - 1)
                if j in (10, 12):
                    split_lo(G_FIN, 1, (j - 10) // 2)
                v.wait_ge(S["tile_free"], n)
                v.wait_ge(S["tile_made"], n + 1)
                v.wait_ge(S["m_sig"], j + 1)
                v.tensor_tensor(m_all[:, j], proj[:, j % 2], m_all[:, j], ALU.mult).then_inc(S["tile_free"], 1)
                if j > KT:
                    merged_low(j - KT - 1)
            merged_low(KT - 1)
            for hf in (0, 1):
                split_lo(G_FIN + 1, 0, hf)
            v.wait_ge(S["x2_landed"], 16)
            for j in range(KT):
                n = T_FIN + j
                v.wait_ge(S["tile_free"], n)
                v.wait_ge(S["tile_made"], n + 1)
                xx = x_fin[:, j % 4, 512 * (j // 4):512 * (j // 4 + 1)]
                v.tensor_tensor(xx, xx, proj[:, j % 2], ALU.add).then_inc(S["tile_free"], 1)

        @block.tensor
        def _(pe):
            t_ = nc.tensor
            t_.wait_ge(S["consts"], 8)
            norm_pe(0, 0)
            for j in (0, 1):
                made(project(G_GATES, 0, j, j, j, first=True, ready=("norm_lo", 0) if j == 0 else None))
            t_.wait_ge(S["rows_a"], 1)
            for t in range(TB):
                t_.transpose(pm[:, HEADS * t:HEADS * (t + 1)], g_a[:, t * P:(t + 1) * P], ident[0:HEADS, 0:HEADS])
            t_.wait_ge(S["rows_act"], 4)
            for t in range(TB):
                mm = t_.transpose(pm[:, HEADS * (TB + t):HEADS * (TB + t + 1)], g_out[:, 1, t * P:(t + 1) * P],
                                  ident[0:HEADS, 0:HEADS])
            mm.then_inc(S["a_turned"], 1)
            with t_.Fori(0, HEADS) as h:
                n = T_HEADS + 8 * h
                ga = G_HEADS + 2 * h

                def tile(j):
                    made(project(ga + j // 4, (1 + j // 4) % 2, n + j, j % 2, j % 4))

                def triangle(out_, lhsT, rhs, rows=P):
                    for i in range(TB):
                        mm = t_.matmul(out_[:, TRI[i]:TRI[i] + SEQ - P * i], lhsT[0:rows, P * i:P * (i + 1)],
                                       rhs[0:rows, P * i:], start=True, stop=True)
                    return mm

                def weighted(out_, keys, weights):
                    for i in range(TB):
                        mm = t_.matmul(out_[:, P * i:SEQ], keys(i), weights[:, TRI[i]:TRI[i] + SEQ - P * i],
                                       start=(i == 0), stop=(i == TB - 1))
                    return mm

                tile(0)
                tile(1)
                tile(2)
                t_.wait_ge(S["head_done"], h + 1)
                for j, sq in enumerate((sq_q, sq_k)):
                    t_.wait_ge(S["tile_free"], n + j + 1)
                    t_.matmul(pa[:, 512 * j:512 * (j + 1)], mean[:, :], sq[:, :], start=True, stop=True).then_inc(S["ssq_made"], 1)
                tile(3)
                t_.wait_ge(S["qk_normed"], 2 * h + 2)
                triangle(pa, k_b, q_b).then_inc(S["z_made"], 1)
                tile(4)
                t_.wait_ge(S["tile_free"], n + 5)
                t_.wait_ge(S["a_col"], 2)
                for m, vT in enumerate((v_bT, v_aT)):
                    for i in range(TB):
                        mm = t_.transpose(pm[:, 512 * m + P * i:512 * m + P * (i + 1)], vT[:, P * i:P * (i + 1)], ident[:, :])
                mm.then_inc(S["v_turned"], 1)
                tile(5)
                t_.wait_ge(S["v_sb"], 2 * h + 2)
                t_.wait_ge(S["ka_landed"], 16 * h + 16)
                triangle(pm, k_a, silu, DQK_A).then_inc(S["s_made"], 1)
                tile(6)
                t_.wait_ge(S["sp_lo"], h + 1)
                for i in range(TB):
                    mms = [(tri_r if i2 == i else ones_r, i2, s_) for i2 in range(i, TB - 1) for s_ in (sp_hi, sp_lo)]
                    mms.append((tri if i == TB - 1 else ones, TB - 1, sp))
                    for q, (w, i2, s_) in enumerate(mms):
                        mm = t_.matmul(pa[:, TRI[i] + P * (i2 - i):TRI[i] + SEQ - P * i], w[:, :],
                                       s_[:, TRI[i2]:TRI[i2] + SEQ - P * i2], start=(q == 0), stop=(q == len(mms) - 1))
                mm.then_inc(S["c_made"], 1)
                t_.wait_ge(S["p_masked"], 4 * h + 4)
                for t in range(TB):
                    for i in range(t + 1):
                        o = TRI[i] + P * (t - i)
                        mm = t_.matmul(by_tok[:, t // 2, t % 2, :], decay[:, o:o + P], v_a[:, i, :],
                                       start=(i == 0), stop=(i == t))
                mm.then_inc(S["num_made"], 1)
                tile(7)
                t_.wait_ge(S["y_tok"], h + 1)
                for t in range(TB):
                    mm = t_.transpose(pm[:, 1024 + P * t:1024 + P * (t + 1)], y_tok[:, P * t:P * (t + 1)], ident[:, :])
                mm.then_inc(S["y_turned"], 1)
                t_.wait_ge(S["a_b"], h + 1)
                weighted(pa[:, 0:512], lambda i: v_b[:, P * i:P * (i + 1)], z).then_inc(S["pv_b_made"], 1)
            t_.wait_ge(S["head_done"], HEADS)
            for g in range(G_OUT, G_MLP):
                for t in range(TB):
                    i = 4 * (g - G_OUT) + t
                    made(project(g, g % 2, T_OUT + i, i % 2, t, tokens=True, act=(y_hi, y_lo),
                                 last=("head_done", HEADS + 1) if i == 0 else None))
            norm_pe(1, T_MLP)
            with t_.Fori(0, CHUNKS) as c:
                g = G_MLP + 4 * c
                n = T_MLP + 16 * c
                for i in range(8):
                    made(project(g + i // 4, (1 + i // 4) % 2, n + i, i % 2, i % 4, ready=("norm_lo", KT) if i == 0 else None))
                for i in range(8, 16):
                    made(project(g + i // 4, (1 + i // 4) % 2, n + i, i % 2, i % 4,
                                 tokens=True, act=(act_hi, act_lo), ready=("a_lo_done", 8 * c) if i == 8 else None))
            norm_pe(2, T_END1)

            def tokens(g, n0, tiles):
                for t in tiles:
                    made(project(g, g % 2, n0 + t, (n0 + t) % 2, t, tokens=True,
                                 ready=("norm_lo", 2 * KT) if g == G_C and t == 0 else None))

            tokens(G_C, T_C, range(TB))
            tokens(G_K, T_K, (0, 1))
            t_.wait_ge(S["c_scaled"], 2 * TB)
            for m in range(3):
                for t in range(TB):
                    mm = t_.transpose(pa[:, 512 * m + P * t:512 * m + P * (t + 1)], t_c[:, t, P * m:P * (m + 1)], ident[:, :])
                mm.then_inc(S["c_turned"], 1)
            tokens(G_K, T_K, (2, 3))
            t_.wait_ge(S["c_lo"], 3)
            for t in range(TB):
                for q, (act_, kts, k0) in enumerate((((cq_hi, cq_lo), 2, 0), ((cq_hi, cq_lo), 2, 2),
                                                     ((ckv_hi, ckv_lo), 1, 4), ((ckv_hi, ckv_lo), 1, 5))):
                    n = T_U + 4 * t + q
                    made(project(G_U, G_U % 2, n, q % 2, t, tokens=True, act=act_, kts=kts, k0=k0))
            tokens(G_Q, T_Q, (0,))
            t_.wait_ge(S["ki_spread"], 1)
            t_.wait_ge(S["rope"], 12)
            for t in range(TB):
                mm = t_.transpose(pa[:, P * t:P * (t + 1)], t_k[:, t, 0:P], ident[:, :])
            mm.then_inc(S["ki_turned"], 1)
            for g in range(2):
                for t in range(TB):
                    mm = t_.transpose(pm[:, 512 * g + P * t:512 * g + P * (t + 1)], t_k[:, t, P * (g + 2):P * (g + 3)], ident[:, :])
            mm.then_inc(S["qi_turned"], 1)
            tokens(G_Q, T_Q, (1,))
            for h in range(HEADS):
                X = pm if h % 2 else pa
                if h in (2, 4):
                    tokens(G_Q, T_Q, (1 + h // 2,))
                if h == 0:
                    t_.wait_ge(S["qi_sb"], 3)
                if h >= 2:
                    t_.wait_ge(S["idx_relu"], h - 1)
                g, rows = h // 4, slice(IDX_D * (h % 4), IDX_D * (h % 4 + 1))
                for i in range(TB):
                    mm = t_.matmul(X[:, LOW[i]:LOW[i] + P * (i + 1)], t_c[rows, i, P * g:P * (g + 1)],
                                   t_c[rows, 0:i + 1, 256:384], start=True, stop=True)
                mm.then_inc(S["idx_made"], 1)
            t_.wait_ge(S["idx_relu"], HEADS)

            def gate(B, s, i):
                made(project(G_L + B, 1 - s, T_L + 3 * B + i, (s + i) % 2, i))

            def head_turn(u, B, d):
                X = (pa, pm)[u]
                t_.wait_ge(S[f"staged{u}"], 2 * B + 2)
                t_.wait_ge(S[f"o_sb{u}"], B + 1)
                d = QK_M
                for w, st in enumerate((q_st[u], k_st[u])):
                    for t in range(TB):
                        mm = t_.transpose(X[0:d, 512 * w + P * t:512 * w + P * (t + 1)], st[:, t, 0:d], ident[:, :])
                mm.then_inc(S[f"qk_turned{u}"], 1)

            def head_scores(u, B, d):
                X = (pa, pm)[u]
                t_.wait_ge(S[f"qk_sb{u}"], 2 * B + 2)
                for i in range(TB):
                    mm = t_.matmul(X[:, LOW[i]:LOW[i] + P * (i + 1)], qT[u][0:d, P * i:P * (i + 1)],
                                   kT[u][0:d, 0:P * (i + 1)], start=True, stop=True)
                mm.then_inc(S[f"scores{u}"], 1)

            def head_pT(u, B):
                X = (pa, pm)[u]
                t_.wait_ge(S[f"p_norm{u}"], 4 * B + 4)
                for j in range(TB):
                    for i in range(j, TB):
                        o = TRI[j] + P * (i - j)
                        mm = t_.transpose(X[:, o:o + P], p_sb[u][:, LOW[i] + P * j:LOW[i] + P * (j + 1)], ident[:, :])
                mm.then_inc(S[f"p_turned{u}"], 1)

            def head_pv(u, B):
                X = (pa, pm)[u]
                t_.wait_ge(S[f"pT_sb{u}"], B + 1)
                t_.wait_ge(S[f"v_staged{u}"], 2 * B + 2)
                for i in range(TB):
                    mm = t_.matmul(X[:, P * i:SEQ], v_st[u][:, i, :], pT[u][:, TRI[i]:TRI[i] + SEQ - P * i],
                                   start=(i == 0), stop=(i == TB - 1))
                mm.then_inc(S[f"pv{u}"], 1)

            for kind, d in enumerate((QK_M, D_D)):
                with t_.Fori(0, 2) as b:
                    for s in range(2):
                        B = 4 * kind + 2 * b + s
                        head_turn(0, B, d)
                        head_turn(1, B, d)
                        gate(B, s, 0)
                        head_scores(0, B, d)
                        head_scores(1, B, d)
                        gate(B, s, 1)
                        head_pT(0, B)
                        head_pT(1, B)
                        gate(B, s, 2)
                        head_pv(0, B)
                        head_pv(1, B)
            for kind in range(2):
                for j in range(KT):
                    n = T_BR + KT * kind + j
                    made(project(G_BR + kind, (1 + kind) % 2, n, j % 2, j % 4, kts=4, k0=4 * (j // 4),
                                 act=(h_hi[:, 4 * kind:4 * kind + 4], h_lo[:, 4 * kind:4 * kind + 4]),
                                 ready=("oh_lo", 4 * kind) if j == 0 else None))
            for g in range(2):
                for t in range(TB):
                    n = T_FIN + 4 * g + t
                    made(project(G_FIN + g, (1 + g) % 2, n, t % 2, t, tokens=True, act=(mg_hi, mg_lo),
                                 ready=("mg_lo", 0) if g == 0 and t == 0 else None))


def k_tiles(a):
    return a.reshape(-1, P, a.shape[1]).transpose(1, 0, 2)


def lay_out(v):
    v = {name: np.asarray(a) for name, a in v.items()}
    one = {name: a[0] for name, a in v.items()}
    wall = np.zeros((N_GROUPS, P, KT, 512), np.float32)

    sizes = (512, 512, 1024, 1024, HEADS, HEADS, 1024, 1024, 1024, 1024, 1024)
    q_a, k_a, v_a, o_a, i_a, f_a, q_b, k_b, v_b, g_a, g_b = np.split(k_tiles(one["w_in"]), np.cumsum(sizes)[:-1], axis=2)
    wall[G_GATES, :, :, 0:HEADS] = i_a
    wall[G_GATES, :, :, P:P + HEADS] = f_a
    for h in range(HEADS):
        wide, narrow = slice(P * h, P * (h + 1)), slice(DQK_A * h, DQK_A * (h + 1))
        wall[G_HEADS + 2 * h] = np.concatenate(
            [q_b[:, :, wide], k_b[:, :, wide], q_a[:, :, narrow], k_a[:, :, narrow], v_b[:, :, wide]], axis=2)
        wall[G_HEADS + 2 * h + 1] = np.concatenate([w[:, :, wide] for w in (v_a, o_a, g_a, g_b)], axis=2)
    for j in range(2):
        half = slice(512 * j, 512 * (j + 1))
        wall[G_OUT + j] = k_tiles(one["w_out"])[:, :, half]
        wall[G_FIN + j] = k_tiles(one["w_out_2"])[:, :, half]
        for c in range(CHUNKS):
            wall[G_MLP + 4 * c + j] = k_tiles(one["w_up"])[:, :, DM * c + 512 * j:DM * c + 512 * (j + 1)]
            wall[G_MLP + 4 * c + 2 + j] = k_tiles(one["w_down"][DM * c:DM * (c + 1)])[:, :, half]
    head_par = np.zeros((P, HEADS, 7), np.float32)
    taps = one["conv_w"].reshape(4, 2, HEADS, DQK_A)
    head_par[0:DQK_A, :, 0:4] = taps[:, 0].transpose(2, 1, 0)
    head_par[DQK_A:P, :, 0:4] = taps[:, 1].transpose(2, 1, 0)
    head_par[:, :, 4] = one["mlstm_norm_g"].reshape(HEADS, P).T
    head_par[:, :, 5:7] = one["b_gate"].reshape(2, HEADS, P).transpose(2, 1, 0)

    sizes = (256, 128, 32, 512, 512, 128, 128, 512, 256, 32, 8, 1024, 1024)
    (c_q, c_kv, k_pe, gate_a, q_b, k_b, v_b, gate_b, q_i, k_i, w_i, m_a, m_b) = np.split(
        k_tiles(one["w_in_2"]), np.cumsum(sizes)[:-1], axis=2)
    wall[G_C, :, :, 0:456] = np.concatenate([c_q, c_kv, k_pe, k_i, w_i], axis=2)
    wall[G_Q] = q_b
    wall[G_K] = np.concatenate([k_b, v_b, q_i], axis=2)
    uq = k_tiles(one["mla_w_uq_2"])
    ukv = one["mla_w_ukv_2"].reshape(P, HEADS, 2, NOPE)
    for k in range(2):
        wall[G_U, :, k] = uq[:, k, 0:512]
        wall[G_U, :, 2 + k, 0:256] = uq[:, k, 512:768]
        wall[G_U, :, 4 + k] = ukv[:, :, k].reshape(P, 512)
    gates = np.concatenate([gate_a, gate_b, m_a, m_b], axis=2)
    for j in range(8):
        wall[G_L + j, :, :, 0:384] = gates[:, :, 384 * j:384 * (j + 1)]
    for j, name in enumerate(("w_branch_mla_2", "w_branch_dsa_2")):
        wall[G_BR + j] = one[name].reshape(4, P, 2, 512).transpose(1, 2, 0, 3).reshape(P, 8, 512)
    wide_gains = np.zeros((4, QK_M), np.float32)
    for j, name in enumerate(("mla_q_gain_2", "mla_k_gain_2", "dsa_q_gain_2", "dsa_k_gain_2")):
        wide_gains[j, 0:one[name].size] = one[name]
    inv_freq = np.concatenate([np.float32(500000.0) ** (-np.arange(0, r, 2, dtype=np.float32) / np.float32(r))
                               for r in (32, 16, 8)])

    gains = np.concatenate([one[n].reshape(KT, P).T for n in ("norm_mix_g", "norm_mlp_g", "norm_gain_2")], axis=1)
    c_gains = np.concatenate([one["mla_q_norm_2"].reshape(2, P), one["mla_kv_norm_2"].reshape(1, P)]).T
    return {
        "x": one["x"], "wall": wall, "gains": gains, "head_par": head_par,
        "sb_gains": np.stack([one["sb_q_norm_g"], one["sb_k_norm_g"]], axis=1),
        "b_if": one["b_if"].reshape(2, HEADS).T,
        "positions": one["positions_2"].astype(np.int32).reshape(TB, P).T,
        "inv_freq": inv_freq.astype(np.float32).reshape(1, N_FREQ), "wide_gains": wide_gains, "c_gains": c_gains,
        "b_merge": one["b_merge_2"].reshape(2 * KT, P).T,
    }


def kernel(**inputs):
    import concourse.bacc as bacc
    from concourse.bass_utils import run_bass_kernel_spmd

    nc = bacc.Bacc("TRN2", target_bir_lowering=False, num_devices=1)
    arrays, args = {}, []
    for name, a in lay_out(inputs).items():
        a = np.ascontiguousarray(a)
        arrays[f"in_{name}"] = a
        args.append(nc.dram_tensor(f"in_{name}", a.shape, mybir.dt.from_np(a.dtype), kind="ExternalInput").ap())
    args.append(nc.dram_tensor("result", (SEQ, DM), F32, kind="ExternalOutput").ap())
    program(nc, *args)
    r = run_bass_kernel_spmd(nc, [arrays], core_ids=[0])
    return r.results[0]["result"].reshape(1, SEQ, DM)
```
